# Optimizing a Trainium2 kernel written in Bass

```python
import jax, jax.numpy as jnp
from jax import lax
import numpy as np

D_MODEL = 1024
BATCH = 1
SEQ = 256
DEPTH = 2

CHUNK = 64
N_MIXERS = 2
N_LAYERS_A = (DEPTH + N_MIXERS - 1) // N_MIXERS
N_LAYERS_B = DEPTH // N_MIXERS
CONV_A_WIDTH = 31
CONV_B_WIDTH = 3
N_GROUPS = 4
EXPERTS_PER_GROUP = 8
N_EXPERTS = N_GROUPS * EXPERTS_PER_GROUP
TOP_K = 2
D_EXPERT = D_MODEL // 2
ROUTE_BLOCK = 128
ALPHA = (2.0 * DEPTH) ** 0.25
BETA = (8.0 * DEPTH) ** -0.25
LN_EPS = 1e-5


def layer_norm(x, g, b):
    xf = x.astype(jnp.float32)
    mu = jnp.mean(xf, axis=-1, keepdims=True)
    var = jnp.mean(jnp.square(xf - mu), axis=-1, keepdims=True)
    y = (xf - mu) * lax.rsqrt(var + LN_EPS)
    return (y * g.astype(jnp.float32) + b.astype(jnp.float32)).astype(x.dtype)

def causal_depthwise_conv(u, w):
    k = w.shape[0]
    return lax.conv_general_dilated(
        u, w[:, None, :].astype(u.dtype), window_strides=(1,), padding=[(k - 1, 0)],
        dimension_numbers=("NWC", "WIO", "NWC"), feature_group_count=u.shape[-1])

def conformer_conv(h, w_in, b_in, w_dw, b_dw, ln_g, ln_b, w_out, b_out):
    a, g = jnp.split(h @ w_in + b_in, 2, axis=-1)
    u = a * jax.nn.sigmoid(g)
    u = causal_depthwise_conv(u, w_dw) + b_dw
    u = jax.nn.silu(layer_norm(u, ln_g, ln_b))
    return u @ w_out + b_out

def short_gated_conv(h, w_in, w_dw, w_out):
    gb, gc, v = jnp.split(h @ w_in, 3, axis=-1)
    u = causal_depthwise_conv(gc * v, w_dw)
    return (gb * u) @ w_out

def hierarchical_moe(h, w_group, b_group, w_router, b_router, w_gate, w_up, w_down):
    bsz, seq, d = h.shape
    t = bsz * seq
    xf = h.reshape(t, d)
    g_logits = (xf @ w_group + b_group).astype(jnp.float32)
    g_probs = jax.nn.softmax(g_logits, axis=-1)
    g_idx = jnp.argmax(g_logits, axis=-1).astype(jnp.int32)
    g_w = jnp.take_along_axis(g_probs, g_idx[:, None], axis=-1)
    e_logits = (xf @ w_router + b_router).astype(jnp.float32).reshape(t, N_GROUPS, EXPERTS_PER_GROUP)
    e_logits = jnp.take_along_axis(e_logits, g_idx[:, None, None], axis=1)[:, 0]
    e_probs = jax.nn.softmax(e_logits, axis=-1)
    top_p, top_e = lax.top_k(e_probs, TOP_K)
    top_p = top_p / jnp.sum(top_p, axis=-1, keepdims=True)
    weights = (g_w * top_p).reshape(-1)
    flat_e = (g_idx[:, None] * EXPERTS_PER_GROUP + top_e.astype(jnp.int32)).reshape(-1)
    n_assign = t * TOP_K
    order = jnp.argsort(flat_e)
    sorted_e = flat_e[order]
    sorted_tok = (order // TOP_K).astype(jnp.int32)
    counts = jnp.zeros((N_EXPERTS,), jnp.int32).at[flat_e].add(1)
    starts = jnp.cumsum(counts) - counts
    padded = (counts + ROUTE_BLOCK - 1) // ROUTE_BLOCK * ROUTE_BLOCK
    pad_ends = jnp.cumsum(padded)
    pad_starts = pad_ends - padded
    dest = pad_starts[sorted_e] + (jnp.arange(n_assign, dtype=jnp.int32) - starts[sorted_e])
    n_slots = n_assign + N_EXPERTS * ROUTE_BLOCK
    n_blocks = n_slots // ROUTE_BLOCK
    slot_tok = jnp.full((n_slots,), t, jnp.int32).at[dest].set(sorted_tok)
    block_start = jnp.arange(n_blocks, dtype=jnp.int32) * ROUTE_BLOCK
    block_e = jnp.minimum(jnp.sum(pad_ends[None, :] <= block_start[:, None], axis=-1), N_EXPERTS - 1)
    x_pad = jnp.concatenate([xf, jnp.zeros((1, d), xf.dtype)], axis=0)
    xb = x_pad[slot_tok].reshape(n_blocks, ROUTE_BLOCK, d)

    def expert_block(args):
        xblk, e = args
        hid = jax.nn.silu(xblk @ w_gate[e]) * (xblk @ w_up[e])
        return hid @ w_down[e]

    yb = lax.map(expert_block, (xb, block_e)).reshape(n_slots, d)
    contrib = weights[order][:, None].astype(xf.dtype) * yb[dest]
    y = jnp.zeros((t, d), xf.dtype).at[sorted_tok].add(contrib)
    return y.reshape(bsz, seq, d)

def first_inputs(seed: int = 0) -> dict:
    key = jax.random.key(seed)
    ks = jax.random.split(key, 26)
    D, F = D_MODEL, D_EXPERT
    nrm = lambda k, shape, s: jax.random.normal(k, shape, jnp.float32) * s
    return {
        "x": nrm(ks[0], (BATCH, SEQ, D), 1.0),
        "c": nrm(ks[1], (BATCH, D), 1.0),
        "ada_w": nrm(ks[2], (DEPTH, D, 6 * D), 0.5 * D ** -0.5),
        "ada_b": nrm(ks[3], (DEPTH, 6 * D), 0.01),
        "a_w_in": nrm(ks[4], (N_LAYERS_A, D, 2 * D), D ** -0.5),
        "a_b_in": nrm(ks[5], (N_LAYERS_A, 2 * D), 0.01),
        "a_w_dw": nrm(ks[6], (N_LAYERS_A, CONV_A_WIDTH, D), CONV_A_WIDTH ** -0.5),
        "a_b_dw": nrm(ks[7], (N_LAYERS_A, D), 0.01),
        "a_ln_g": 1.0 + nrm(ks[8], (N_LAYERS_A, D), 0.01),
        "a_ln_b": nrm(ks[9], (N_LAYERS_A, D), 0.01),
        "a_w_out": nrm(ks[10], (N_LAYERS_A, D, D), BETA * D ** -0.5),
        "a_b_out": nrm(ks[11], (N_LAYERS_A, D), 0.01),
        "b_w_in": nrm(ks[12], (N_LAYERS_B, D, 3 * D), D ** -0.5),
        "b_w_dw": nrm(ks[13], (N_LAYERS_B, CONV_B_WIDTH, D), CONV_B_WIDTH ** -0.5),
        "b_w_out": nrm(ks[14], (N_LAYERS_B, D, D), BETA * D ** -0.5),
        "mix_ln_g": 1.0 + nrm(ks[15], (DEPTH, D), 0.01),
        "mix_ln_b": nrm(ks[16], (DEPTH, D), 0.01),
        "ffn_ln_g": 1.0 + nrm(ks[17], (DEPTH, D), 0.01),
        "ffn_ln_b": nrm(ks[18], (DEPTH, D), 0.01),
        "r_w_group": nrm(ks[19], (DEPTH, D, N_GROUPS), D ** -0.5),
        "r_b_group": nrm(ks[20], (DEPTH, N_GROUPS), 0.01),
        "r_w_expert": nrm(ks[21], (DEPTH, D, N_EXPERTS), D ** -0.5),
        "r_b_expert": nrm(ks[22], (DEPTH, N_EXPERTS), 0.01),
        "e_w_gate": nrm(ks[23], (DEPTH, N_EXPERTS, D, F), D ** -0.5),
        "e_w_up": nrm(ks[24], (DEPTH, N_EXPERTS, D, F), D ** -0.5),
        "e_w_down": nrm(ks[25], (DEPTH, N_EXPERTS, F, D), BETA * F ** -0.5),
    }

def first_block(x, c, ada_w, ada_b, a_w_in, a_b_in, a_w_dw, a_b_dw, a_ln_g, a_ln_b, a_w_out, a_b_out,
              b_w_in, b_w_dw, b_w_out, mix_ln_g, mix_ln_b, ffn_ln_g, ffn_ln_b,
              r_w_group, r_b_group, r_w_expert, r_b_expert, e_w_gate, e_w_up, e_w_down):
    c_act = jax.nn.silu(c)
    for i in range(DEPTH):
        mods = (c_act @ ada_w[i] + ada_b[i])[:, None, :]
        sh_m, sc_m, g_m, sh_f, sc_f, g_f = jnp.split(mods, 6, axis=-1)
        h = x * (1.0 + sc_m) + sh_m
        j = i // N_MIXERS
        if i % N_MIXERS == 0:
            y = conformer_conv(h, a_w_in[j], a_b_in[j], a_w_dw[j], a_b_dw[j],
                               a_ln_g[j], a_ln_b[j], a_w_out[j], a_b_out[j])
        else:
            y = short_gated_conv(h, b_w_in[j], b_w_dw[j], b_w_out[j])
        x = layer_norm(ALPHA * x + (1.0 + g_m) * y, mix_ln_g[i], mix_ln_b[i])
        h = x * (1.0 + sc_f) + sh_f
        y = hierarchical_moe(h, r_w_group[i], r_b_group[i], r_w_expert[i], r_b_expert[i],
                             e_w_gate[i], e_w_up[i], e_w_down[i])
        x = layer_norm(ALPHA * x + (1.0 + g_f) * y, ffn_ln_g[i], ffn_ln_b[i])
    return x


HEAD_DIM = 64
ROPE_THETA = 10000.0
A_HEADS = 8
A_CONFIGS = ((128, 1), (512, 4), (2048, 16))
B_HEADS = 8
B_KV_HEADS = 2
B_WINDOW = 128
C_HEADS = 8
IDX_HEADS = 8
IDX_DIM = 64
TOPK_MAX = 256
QUERY_BLOCK = 128
BAND_BLOCK = 128
D_FF = 2816
DN_ALPHA = (2 * DEPTH) ** 0.25
DN_BETA = (8 * DEPTH) ** -0.25

A_W = A_HEADS * HEAD_DIM
B_QW = B_HEADS * HEAD_DIM
B_KW = B_KV_HEADS * HEAD_DIM
C_W = C_HEADS * HEAD_DIM
IN_SIZES = (A_W, A_W, A_W,
            B_QW, B_KW, B_KW,
            C_W, HEAD_DIM, HEAD_DIM,
            IDX_HEADS * IDX_DIM, IDX_DIM, IDX_HEADS,
            D_MODEL, D_MODEL, D_MODEL)
D_IN = sum(IN_SIZES)


def layer_norm_2(x, g, b):
    xf = x.astype(jnp.float32)
    mu = xf.mean(-1, keepdims=True)
    var = jnp.square(xf - mu).mean(-1, keepdims=True)
    y = (xf - mu) * lax.rsqrt(var + LN_EPS)
    return (y * g.astype(jnp.float32) + b.astype(jnp.float32)).astype(x.dtype)

def rope_tables(positions, dim):
    inv = ROPE_THETA ** (-jnp.arange(0, dim, 2, dtype=jnp.float32) / dim)
    ang = positions.astype(jnp.float32)[..., None] * inv
    return jnp.cos(ang), jnp.sin(ang)

def apply_rope(t, cos, sin):
    tf = t.astype(jnp.float32)
    t1, t2 = jnp.split(tf, 2, axis=-1)
    c = cos[:, :, None, :]
    s = sin[:, :, None, :]
    return jnp.concatenate([t1 * c - t2 * s, t2 * c + t1 * s], axis=-1).astype(t.dtype)

def swiglu(x, w_in, w_out):
    gate, up = jnp.split(x @ w_in, 2, axis=-1)
    return (jax.nn.silu(gate) * up) @ w_out

def banded_attention(q, k, v, max_dist, sink=None):
    n, l, h, dh = q.shape
    g = k.shape[2]
    r = h // g
    blk = BAND_BLOCK
    nb = -(-l // blk)
    pad = nb * blk - l
    qp = jnp.pad(q, ((0, 0), (0, pad), (0, 0), (0, 0))).reshape(n, nb, blk, g, r, dh)

    def kv_blocks(t):
        tp = jnp.pad(t, ((0, 0), (blk, pad), (0, 0), (0, 0))).reshape(n, nb + 1, blk, g, dh)
        return jnp.concatenate([tp[:, :-1], tp[:, 1:]], axis=2)

    kb, vb = kv_blocks(k), kv_blocks(v)
    s = jnp.einsum('nbqgrd,nbkgd->nbgrqk', qp, kb, preferred_element_type=jnp.float32) * (dh ** -0.5)
    qi = jnp.arange(blk)[:, None]
    kj = jnp.arange(2 * blk)[None, :]
    dist = qi + blk - kj
    kpos = jnp.arange(nb)[:, None, None] * blk - blk + kj[None]
    valid = (dist >= 0) & (dist <= max_dist) & (kpos >= 0)
    s = jnp.where(valid[:, None, None], s, -jnp.inf)
    m = s.max(-1)
    if sink is not None:
        sk = sink.astype(jnp.float32).reshape(g, r)[:, :, None]
        m = jnp.maximum(m, sk)
    p = jnp.exp(s - m[..., None])
    den = p.sum(-1)
    if sink is not None:
        den = den + jnp.exp(sk - m)
    o = jnp.einsum('nbgrqk,nbkgd->nbqgrd', p.astype(v.dtype), vb, preferred_element_type=jnp.float32)
    o = o / den.transpose(0, 1, 4, 2, 3)[..., None]
    o = o.reshape(n, nb * blk, h, dh)[:, :l].astype(q.dtype)
    lse = (m + jnp.log(den)).transpose(0, 1, 4, 2, 3).reshape(n, nb * blk, h)[:, :l]
    return o, lse

def dilated_attention(q, k, v):
    b, s, h, dh = q.shape
    outs, lses = [], []
    for window, dil in A_CONFIGS:
        def fold(t):
            return t.reshape(b, s // dil, dil, h, dh).transpose(0, 2, 1, 3, 4).reshape(b * dil, s // dil, h, dh)
        o, lse = banded_attention(fold(q), fold(k), fold(v), window // dil)
        outs.append(o.reshape(b, dil, s // dil, h, dh).transpose(0, 2, 1, 3, 4).reshape(b, s, h, dh))
        lses.append(lse.reshape(b, dil, s // dil, h).transpose(0, 2, 1, 3).reshape(b, s, h))
    wts = jax.nn.softmax(jnp.stack(lses, 0), axis=0)
    o = jnp.einsum('cbsh,cbshd->bshd', wts, jnp.stack(outs, 0).astype(jnp.float32))
    return o.astype(q.dtype)

def dsa_attention(q, k, v, q_idx, k_idx, w_idx):
    b, s, h, dh = q.shape
    k_sel = min(TOPK_MAX, s // 4)
    nq = s // QUERY_BLOCK
    key_pos = jnp.arange(s)
    gather = jax.vmap(lambda t, ix: t[ix])

    def block(i):
        start = i * QUERY_BLOCK
        qb = lax.dynamic_slice_in_dim(q, start, QUERY_BLOCK, axis=1)
        qib = lax.dynamic_slice_in_dim(q_idx, start, QUERY_BLOCK, axis=1)
        wb = lax.dynamic_slice_in_dim(w_idx, start, QUERY_BLOCK, axis=1)
        qpos = start + jnp.arange(QUERY_BLOCK)
        causal = key_pos[None, :] <= qpos[:, None]
        dots = jnp.einsum('bqhd,bsd->bqhs', qib, k_idx, preferred_element_type=jnp.float32)
        score = jnp.einsum('bqhs,bqh->bqs', jax.nn.relu(dots), wb.astype(jnp.float32))
        score = jnp.where(causal[None], score, -jnp.inf)
        _, idx = lax.top_k(score, k_sel)
        sel_valid = idx <= qpos[None, :, None]
        kg = gather(k, idx)
        vg = gather(v, idx)
        att = jnp.einsum('bqhd,bqkd->bhqk', qb, kg, preferred_element_type=jnp.float32) * (dh ** -0.5)
        att = jnp.where(sel_valid[:, None], att, -jnp.inf)
        p = jax.nn.softmax(att, axis=-1)
        return jnp.einsum('bhqk,bqkd->bqhd', p.astype(v.dtype), vg,
                          preferred_element_type=jnp.float32).astype(q.dtype)

    out = lax.map(block, jnp.arange(nq))
    return out.transpose(1, 0, 2, 3, 4).reshape(b, s, h, dh)

def hybrid_mixer(x, cos, sin, w_in, sink_b, w_br_a, w_br_b, w_br_c, w_out):
    b, s, _ = x.shape
    proj = x @ w_in
    splits = [int(c) for c in np.cumsum(IN_SIZES)[:-1]]
    (qa, ka, va, qb, kb, vb, qc, kc, vc, qi, ki, wi, ga, gb, gc) = jnp.split(proj, splits, axis=-1)

    def heads(t, nh):
        return t.reshape(b, s, nh, -1)

    o_a = dilated_attention(apply_rope(heads(qa, A_HEADS), cos, sin),
                            apply_rope(heads(ka, A_HEADS), cos, sin),
                            heads(va, A_HEADS)).reshape(b, s, A_W)
    o_b, _ = banded_attention(apply_rope(heads(qb, B_HEADS), cos, sin),
                              apply_rope(heads(kb, B_KV_HEADS), cos, sin),
                              heads(vb, B_KV_HEADS), B_WINDOW - 1, sink_b)
    o_b = o_b.reshape(b, s, B_QW)
    o_c = dsa_attention(apply_rope(heads(qc, C_HEADS), cos, sin),
                        apply_rope(heads(kc, 1), cos, sin)[:, :, 0],
                        vc,
                        apply_rope(heads(qi, IDX_HEADS), cos, sin),
                        apply_rope(heads(ki, 1), cos, sin)[:, :, 0],
                        wi).reshape(b, s, C_W)
    merged = (jax.nn.sigmoid(ga) * (o_a @ w_br_a)
              + jax.nn.sigmoid(gb) * (o_b @ w_br_b)
              + jax.nn.sigmoid(gc) * (o_c @ w_br_c))
    return merged @ w_out

def second_inputs(seed: int = 0) -> dict:
    key = jax.random.key(seed)
    ks = jax.random.split(key, 16)
    f32 = jnp.float32

    def nrm(k, shape, scale):
        return jax.random.normal(k, shape, f32) * scale

    x = jax.random.normal(ks[0], (BATCH, SEQ, D_MODEL), f32)
    offs = jax.random.randint(ks[1], (BATCH, 1), 0, 4096, dtype=jnp.int32)
    positions = jnp.arange(SEQ, dtype=jnp.int32)[None, :] + offs
    return {
        "x": x,
        "positions": positions,
        "w_in": nrm(ks[2], (DEPTH, D_MODEL, D_IN), D_MODEL ** -0.5),
        "sink_b": nrm(ks[3], (DEPTH, B_HEADS), 0.5),
        "w_br_a": nrm(ks[4], (DEPTH, A_W, D_MODEL), A_W ** -0.5),
        "w_br_b": nrm(ks[5], (DEPTH, B_QW, D_MODEL), B_QW ** -0.5),
        "w_br_c": nrm(ks[6], (DEPTH, C_W, D_MODEL), C_W ** -0.5),
        "w_out": nrm(ks[7], (DEPTH, D_MODEL, D_MODEL), D_MODEL ** -0.5 * DN_BETA),
        "ffn1_in": nrm(ks[8], (DEPTH, D_MODEL, 2 * D_FF), D_MODEL ** -0.5),
        "ffn1_out": nrm(ks[9], (DEPTH, D_FF, D_MODEL), D_FF ** -0.5 * DN_BETA),
        "ffn2_in": nrm(ks[10], (DEPTH, D_MODEL, 2 * D_FF), D_MODEL ** -0.5),
        "ffn2_out": nrm(ks[11], (DEPTH, D_FF, D_MODEL), D_FF ** -0.5 * DN_BETA),
        "ln_g": 1.0 + nrm(ks[12], (DEPTH, 3, D_MODEL), 0.02),
        "ln_b": nrm(ks[13], (DEPTH, 3, D_MODEL), 0.02),
    }

def second_block(x, positions, w_in, sink_b, w_br_a, w_br_b, w_br_c, w_out,
              ffn1_in, ffn1_out, ffn2_in, ffn2_out, ln_g, ln_b):
    cos, sin = rope_tables(positions, HEAD_DIM)
    for l in range(DEPTH):
        x = layer_norm_2(DN_ALPHA * x + 0.5 * swiglu(x, ffn1_in[l], ffn1_out[l]), ln_g[l, 0], ln_b[l, 0])
        x = layer_norm_2(DN_ALPHA * x + hybrid_mixer(x, cos, sin, w_in[l], sink_b[l], w_br_a[l],
                                                   w_br_b[l], w_br_c[l], w_out[l]),
                       ln_g[l, 1], ln_b[l, 1])
        x = layer_norm_2(DN_ALPHA * x + 0.5 * swiglu(x, ffn2_in[l], ffn2_out[l]), ln_g[l, 2], ln_b[l, 2])
    return x


def setup_inputs(seed=0):
    out = dict(first_inputs(seed))
    for name, value in second_inputs(seed + 1).items():
        if name != "x":
            out[name + "_2"] = value
    return out


def reference(
    x, c, ada_w, ada_b, a_w_in, a_b_in, a_w_dw, a_b_dw, a_ln_g, a_ln_b, a_w_out, a_b_out,
    b_w_in, b_w_dw, b_w_out, mix_ln_g, mix_ln_b, ffn_ln_g, ffn_ln_b, r_w_group, r_b_group,
    r_w_expert, r_b_expert, e_w_gate, e_w_up, e_w_down, positions_2, w_in_2, sink_b_2, w_br_a_2,
    w_br_b_2, w_br_c_2, w_out_2, ffn1_in_2, ffn1_out_2, ffn2_in_2, ffn2_out_2, ln_g_2, ln_b_2,
):
    x = first_block(
        x, c, ada_w, ada_b, a_w_in, a_b_in, a_w_dw, a_b_dw, a_ln_g, a_ln_b, a_w_out, a_b_out,
        b_w_in, b_w_dw, b_w_out, mix_ln_g, mix_ln_b, ffn_ln_g, ffn_ln_b, r_w_group, r_b_group,
        r_w_expert, r_b_expert, e_w_gate, e_w_up, e_w_down,
    )
    return second_block(
        x, positions_2, w_in_2, sink_b_2, w_br_a_2, w_br_b_2, w_br_c_2, w_out_2, ffn1_in_2,
        ffn1_out_2, ffn2_in_2, ffn2_out_2, ln_g_2, ln_b_2,
    )


_drawn_inputs = setup_inputs


def setup_inputs(seed=0):
    import zlib

    import numpy as np

    out = dict(_drawn_inputs(seed))
    spreads = {}
    factors = {'a_b_in': 6.142,
     'a_b_dw': 4.054,
     'a_ln_g': 15.743,
     'a_ln_b': 15.8,
     'a_b_out': 8.837,
     'r_b_group': 11.284,
     'r_b_expert': 7.376,
     'sink_b_2': 23.839,
     'mix_ln_b': 2.694,
     'ffn_ln_g': 2.783,
     'ffn_ln_b': 2.968}
    for name, (base, spread) in spreads.items():
        noise = np.random.default_rng([zlib.crc32(name.encode()), seed]).standard_normal(out[name].shape)
        drawn = base * np.exp(spread * noise) if base else spread * noise
        out[name] = __import__('jax').numpy.asarray(drawn.astype(out[name].dtype))
    for name, factor in factors.items():
        out[name] = (out[name] * factor).astype(out[name].dtype)
    return out
```

```python
from contextlib import ExitStack

import numpy as np
import concourse.bass as bass
from concourse import mybir

F32 = mybir.dt.float32
U32 = mybir.dt.uint32
I32 = mybir.dt.int32
ALU = mybir.AluOpType
ACT = mybir.ActivationFunctionType
AX = mybir.AxisListType.X

P = 128
T = 256
D = 1024
KC = 8
E = 32
F = 512
DFF = 2816
DEPTH = 2
ALPHA = (2.0 * DEPTH) ** 0.25
EPS = 1e-5
NEG = -1e30
GONE = -3e38
CW = 31
SLOT = 2048
NSLOT = 7

C_ID, C_PERM, C_MA, C_MB, C_MC, C_IO, C_IG, C_INV = 0, 128, 256, 640, 1024, 1408, 1440, 1472
NCONST = 1473

TWO_PI = 2.0 * np.pi


def split_const(value, parts, bits):
    out, rest = [], float(value)
    for _ in range(parts - 1):
        e = np.floor(np.log2(abs(rest))) + 1
        q = 2.0 ** (e - bits)
        c = np.floor(rest / q) * q
        out.append(float(c))
        rest -= c
    return out + [float(np.float32(rest))]


def constants():
    c = np.zeros((P, NCONST), np.float32)
    c[:, C_ID:C_ID + P] = np.eye(P)
    for i in range(P):
        if i % 64 < 32:
            c[i + 32, C_PERM + i] = -1.0
        else:
            c[i - 32, C_PERM + i] = 1.0
    t = np.arange(T)[:, None]
    s = np.arange(T)[None, :]
    d = t - s
    causal = d >= 0
    many = (causal & (d <= 128)).astype(np.float64) + (causal & (d % 4 == 0)) + (causal & (d % 16 == 0))
    ma = np.where(many > 0, np.log(np.maximum(many, 1)), NEG)
    mb = np.where(causal & (d <= 127), 0.0, NEG)
    mc = np.where(causal, 0.0, NEG)
    for off, m in ((C_MA, ma), (C_MB, mb), (C_MC, mc)):
        c[:, off:off + 128] = m[:128, :128]
        c[:, off + 128:off + 384] = m[128:, :]
    c[:, C_IO:C_IO + 32] = np.arange(32)[None, :]
    c[:, C_IG:C_IG + 32] = (np.arange(32) // 8)[None, :]
    inv = np.float32(10000.0) ** (-np.arange(0, 64, 2).astype(np.float32) / np.float32(64))
    c[:, C_INV] = np.tile(inv.astype(np.float32), 4)
    return c


class Queue:

    def __init__(self, sem):
        self.sem, self.n, self.ops, self.seen = sem, 0, [], {}

    def wait(self, *tokens):
        for tok in tokens:
            if tok is None:
                continue
            if isinstance(tok, list):
                self.wait(*tok)
                continue
            sem, v = tok
            if self.seen.get(id(sem), 0) < v:
                self.seen[id(sem)] = v
                self.ops.append(lambda e, sem=sem, v=v: e.wait_ge(sem, v))

    def do(self, fn, *waits, mark=True):
        self.wait(*waits)
        if not mark:
            self.ops.append(fn)
            return None
        self.n += 1
        self.ops.append(lambda e, fn=fn: fn(e).then_inc(self.sem, 1))
        return (self.sem, self.n)

    def dma(self, out, in_, sem, *waits):
        self.wait(*waits)
        self.ops.append(lambda e: e.dma_start(out, in_).then_inc(sem[0], 16))
        sem[1] += 16
        return (sem[0], sem[1])

    def emit(self, e):
        for op in self.ops:
            op(e)


def program(nc, I, out):
    with ExitStack() as ctx:
        sb = lambda name, shape, dt=F32: ctx.enter_context(nc.sbuf_tensor(name, shape, dt))
        sem = lambda name: ctx.enter_context(nc.semaphore(name))
        dsem = lambda name: [sem(name), 0]

        PE, V, S, G, SP = (Queue(sem(n)) for n in ("pe", "ve", "ac", "po", "sy"))

        const = sb("const", [P, NCONST])
        ident = const[:, C_ID:C_ID + P]
        perm = const[:, C_PERM:C_PERM + P]
        ones = sb("ones", [P, P])
        ring = sb("ring", [P, NSLOT, SLOT])
        ring_sem = [dsem(f"r{i}") for i in range(NSLOT)]
        xa = sb("xa", [P, 2, D])
        vv = sb("vv", [P, 2, D])
        hT = sb("hT", [P, KC, T])
        cols = sb("cols", [P, 5, P])
        mcol = sb("mcol", [P, 2, 48])
        ab = sb("ab", [P, 4, KC])
        mrow = sb("mrow", [P, 2, 3, 512])
        gb = sb("gb", [P, D])
        lnp = sb("lnp", [P, 2, D])
        cos = sb("cos", [P, T])
        sin = sb("sin", [P, T])
        cact = sb("cact", [P, KC, 32])
        small = sb("small", [P, 512])
        arena = sb("arena", [P, 14400])

        YB = [ctx.enter_context(nc.psum_tensor(f"y{i}", [P, 512], F32)) for i in range(4)]
        WB = [ctx.enter_context(nc.psum_tensor(f"w{i}", [P, 512], F32)) for i in range(4)]
        y_read = [None] * 4
        w_read = [None] * 4
        w_next = [0]

        def bank():
            i = w_next[0] % 4
            w_next[0] += 1
            PE.wait(w_read[i])
            return i, WB[i]

        def area(off, *shape):
            n = int(np.prod(shape))
            assert off + n <= 14400, (off, shape)
            a = arena[:, off:off + n]
            if len(shape) == 1:
                return a
            names = "abcd"[:len(shape)]
            return a.rearrange(f"p ({' '.join(names)}) -> p {' '.join(names)}",
                               **{k: s for k, s in zip(names, shape)})

        released = []

        def piece(*parts):
            n = len(released)
            s = n % NSLOT
            released.append(None)
            if n >= NSLOT:
                assert released[n - NSLOT] is not None, n
                SP.wait(released[n - NSLOT])
            for view, src in parts:
                tok = SP.dma(view(ring[:, s, :]), src, ring_sem[s])
            return n, ring[:, s, :], tok

        def block(src, k, n):
            view = lambda r: r[:, 0:k * n].rearrange("p (k n) -> p k n", k=k)
            i, r, tok = piece((view, src.rearrange("(k p) n -> p k n", p=P)))
            return i, view(r), tok

        def mm(o, l, r, start, stop, mark=False, **kw):
            return PE.do(lambda e: e.matmul(o, l, r, start=start, stop=stop, **kw), mark=mark)

        def tr(o, i, idn, mark=False):
            return PE.do(lambda e: e.transpose(o, i, idn), mark=mark)

        vrows = area(9216, 5, P)
        s_c = dsem("s_c")
        t_const = SP.dma(const[:, :], I["consts"], s_c)
        s_v = [dsem(f"s_v{i}") for i in range(5)]
        rows = {}

        def put(tile, at, name, ap, n):
            rows[name] = tile * P + at
            return SP.dma(vrows[at:at + n, tile, :], ap, s_v[tile])

        vec = lambda a: a.rearrange("r (c k) -> (r c) k", k=P)
        t0 = put(0, 0, "c", vec(I["c"]), 8)
        t0 = put(0, 8, "a_b_in", vec(I["a_b_in"]), 16)
        t0 = put(0, 24, "a_b_dw", vec(I["a_b_dw"]), 8)
        t0 = put(0, 32, "a_ln_g", vec(I["a_ln_g"]), 8)
        t0 = put(0, 40, "a_ln_b", vec(I["a_ln_b"]), 8)
        t0 = put(0, 48, "b_w_dw", vec(I["b_w_dw"][0]), 24)
        nv = [72, 64, 96, 124, 124]
        for j, nm in enumerate(("mix_ln_g", "mix_ln_b", "ffn_ln_g", "ffn_ln_b")):
            t1 = put(1, 16 * j, nm, vec(I[nm]), 16)
        for j, nm in enumerate(("ln_g_2", "ln_b_2")):
            t2 = put(2, 48 * j, nm, vec(I[nm].rearrange("l j d -> (l j) d")), 48)
        wdw = I["a_w_dw"][0].rearrange("r (c k) -> (r c) k", k=P)
        t3 = SP.dma(vrows[0:124, 3, :], wdw[0:124, :], s_v[3])
        t4 = SP.dma(vrows[0:124, 4, :], wdw[124:248, :], s_v[4])
        s_x = dsem("s_x")
        x_ap = I["x"][0].rearrange("(t p) d -> p t d", p=P)
        t_x = SP.dma(xa[:, :, :], x_ap, s_x)
        brow = vv[:, 0, :]
        bias = area(0, 2, 3, 512)
        s_ab = dsem("s_ab")
        for l in range(2):
            for g in range(4):
                src = I["ada_b"][l:l + 1, :].rearrange("o (c g n) -> o g c n", c=3, g=4)[:, g, :, :]
                t_ab = SP.dma(bias[32 * g:32 * g + 32, l, :, :], src.to_broadcast([32, 3, 512]), s_ab)
        bout = sb("bout", [1, D])
        rb = sb("rb", [1, 2, 36])
        wr = sb("wr", [P, 2, KC, 36])
        sink = sb("sink", [P, 2, 8, 2])
        sinkr = sb("sinkr", [P, 16])
        s_m = dsem("s_m")
        SP.dma(bout[:, :], I["a_b_out"], s_m)
        for l in range(2):
            SP.dma(rb[:, l, 0:4], I["r_b_group"][l:l + 1, :], s_m)
            SP.dma(rb[:, l, 4:36], I["r_b_expert"][l:l + 1, :], s_m)
            SP.dma(wr[:, l, :, 0:4], I["r_w_group"][l].rearrange("(k p) n -> p k n", p=P), s_m)
            SP.dma(wr[:, l, :, 4:36], I["r_w_expert"][l].rearrange("(k p) n -> p k n", p=P), s_m)
        t_m = SP.dma(sinkr[:, :], I["sink_b_2"].rearrange("l h -> (l h)").unsqueeze(0).to_broadcast([P, 16]), s_m)
        posi = sb("posi", [P, T], I32)
        s_p = dsem("s_p")
        t_p = SP.dma(posi[:, :], I["positions_2"].to_broadcast([P, T]), s_p)

        t_ones = G.do(lambda e: e.memset(ones[:, :], 1.0))
        nhalf = small[:, 0:1]
        t_nh = G.do(lambda e: e.memset(nhalf, -0.5))

        PE.wait(t_const, t_ones, t0, t1, t2, t3, t4)
        _, b0 = bank()
        for j in range(4):
            tk = tr(b0[:, j * P:j * P + nv[j]], vrows[0:nv[j], j, :], const[0:nv[j], 0:nv[j]], mark=(j == 3))
        for j in range(4):
            tv = V.do(lambda e, j=j: e.tensor_copy(cols[:, j, 0:nv[j]], b0[:, j * P:j * P + nv[j]]), tk)
        w_read[0] = tv
        _, b1 = bank()
        tk = tr(b1[:, 0:124], vrows[0:124, 4, :], const[0:124, 0:124], mark=True)
        t_cols = V.do(lambda e: e.tensor_copy(cols[:, 4, 0:124], b1[:, 0:124]), tk)
        w_read[1] = t_cols
        flat = cols[:, :, :].rearrange("p a b -> p (a b)")
        col = lambda name, i: flat[:, rows[name] + i:rows[name] + i + 1]
        colr = lambda name, i, n: flat[:, rows[name] + i:rows[name] + i + n]

        def dw(j, f):
            r = j * 8 + f
            return cols[:, 3 + r // 124, r % 124:r % 124 + 1]

        ang = area(8192, T)
        kq = area(8448, T)
        red = area(8704, T)
        V.do(lambda e: e.tensor_copy(ang, posi[:, :]), t_p)
        tk = V.do(lambda e: e.tensor_scalar(red, ang, const[:, C_INV:C_INV + 1], None, ALU.mult), (V.sem, V.n), t_const)
        magic = 1.5 * 2.0 ** 23
        tk = V.do(lambda e: e.tensor_scalar(kq, red, float(np.float32(1 / TWO_PI)), magic, ALU.mult, ALU.add), tk)
        tk = V.do(lambda e: e.tensor_scalar(kq, kq, -magic, None, ALU.add), tk)
        for cst in split_const(TWO_PI, 4, 10):
            tk = V.do(lambda e, c=cst: e.scalar_tensor_tensor(red, kq, -c, red, ALU.mult, ALU.add), tk)
        tk = V.do(lambda e: e.tensor_scalar(red, red, float(np.float32(3.1415925)), float(np.float32(-3.1415925)), ALU.min, ALU.max), tk)
        ta = S.do(lambda e: e.activation(sin[:, :], red, ACT.Sin), tk)
        ta = S.do(lambda e: e.activation(cos[:, :], red, ACT.Sin, scale=0.5), tk)
        tk = V.do(lambda e: e.tensor_tensor(cos[:, :], cos[:, :], cos[:, :], ALU.mult), ta)
        t_rope = V.do(lambda e: e.tensor_scalar(cos[:, :], cos[:, :], -2.0, 1.0, ALU.mult, ALU.add), tk)
        tk = V.do(lambda e: e.tensor_copy(sink[:, :, :, 0], sinkr[:, :].rearrange("p (l h) -> p l h", l=2)), t_m)
        t_sink = V.do(lambda e: e.tensor_copy(sink[:, :, :, 1], sinkr[:, :].rearrange("p (l h) -> p l h", l=2)), t_m)

        ca = small[:, 8:16]
        ta = S.do(lambda e: e.activation(ca, colr("c", 0, 8), ACT.Silu), t_cols)
        t_ca = V.do(lambda e: e.tensor_copy(cact[:, :, :], ca.unsqueeze(2).to_broadcast([P, KC, 32])), ta)

        def ada(l):
            for cb in range(3):
                wi, b = bank()
                for kc in range(KC):
                    n, w, tok = piece((lambda r: r, I["ada_w"][l, kc * P:(kc + 1) * P, cb * 2048:(cb + 1) * 2048]))
                    PE.wait(tok, t_ca)
                    for g in range(4):
                        tk = mm(b[32 * g:32 * g + 32, :], cact[:, kc, :], w[:, g * 512:(g + 1) * 512],
                                kc == 0, kc == KC - 1, mark=(g == 3))
                    released[n] = tk
                tv = V.do(lambda e, b=b, cb=cb: e.tensor_tensor(mrow[:, l, cb, :], b[:, :], bias[:, l, cb, :], ALU.add), tk, t_ab)
                w_read[wi] = tv
                wi, b = bank()
                PE.wait(tv)
                for j in range(4):
                    tk = tr(b[:, j * P:(j + 1) * P], mrow[:, l, cb, j * P:(j + 1) * P], ident, mark=(j == 3))
                src = b[:, :].rearrange("p (j g r) -> p j g r", j=4, g=4)[:, :, :, 0]
                dst = mcol[:, l, cb * 16:(cb + 1) * 16].rearrange("p (g j) -> p j g", g=4)
                tv = V.do(lambda e, s=src, d=dst: e.tensor_copy(d, s), tk)
                w_read[wi] = tv
            return tv

        def spread(l, cb, g):
            for h in range(2):
                wi, b = bank()
                p = 32 * (g + h)
                tk = mm(b[:, :], ones[p:p + 1, :], mrow[p:p + 1, l, cb, :], True, True, mark=True)
                tv = V.do(lambda e, b=b, h=h: e.tensor_scalar(gb[:, h * 512:(h + 1) * 512], b[:, :], 1.0, None, ALU.add), tk)
                w_read[wi] = tv
            return tv

        t_mod = [ada(0), ada(1)]
        SHM, SCM, GM, SHF, SCF, GF = range(6)
        mvec = lambda l, w: mcol[:, l, 8 * w:8 * w + 8]

        def fold(gcol, bcol, l, sc, sh, *waits):
            if sc is None:
                V.do(lambda e: e.tensor_copy(ab[:, 0, :], gcol), *waits)
                return V.do(lambda e: e.tensor_copy(ab[:, 1, :], bcol))
            t = V.do(lambda e: e.tensor_scalar(ab[:, 2, :], mvec(l, sc), 1.0, None, ALU.add), *waits)
            if gcol is None:
                V.do(lambda e: e.tensor_copy(ab[:, 0, :], ab[:, 2, :]), t)
                return V.do(lambda e: e.tensor_copy(ab[:, 1, :], mvec(l, sh)))
            V.do(lambda e: e.tensor_tensor(ab[:, 0, :], ab[:, 2, :], gcol, ALU.mult), t)
            t = V.do(lambda e: e.tensor_tensor(ab[:, 3, :], ab[:, 2, :], bcol, ALU.mult))
            return V.do(lambda e: e.tensor_tensor(ab[:, 1, :], ab[:, 3, :], mvec(l, sh), ALU.add), t)

        def to_feature(src, t_src, t_ab, t_free):
            toks = []
            for f in range(0, KC, 2):
                wi, b = bank()
                for q in range(2):
                    for t in range(2):
                        PE.wait(t_src[t])
                        tk = tr(b[:, q * T + t * P:q * T + (t + 1) * P], src[:, t, (f + q) * P:(f + q + 1) * P],
                                ident, mark=(q == 1 and t == 1))
                for q in range(2):
                    if f % 4 == 0:
                        tv = V.do(lambda e, b=b, f=f + q, q=q: e.tensor_scalar(
                            hT[:, f, :], b[:, q * T:(q + 1) * T], ab[:, 0, f:f + 1], ab[:, 1, f:f + 1],
                            ALU.mult, ALU.add), tk, t_ab, t_free)
                    else:
                        tv = S.do(lambda e, b=b, f=f + q, q=q: e.activation(
                            hT[:, f, :], b[:, q * T:(q + 1) * T], ACT.Identity, bias=ab[:, 1, f:f + 1],
                            scale=ab[:, 0, f:f + 1]), tk, t_ab, t_free)
                w_read[wi] = tv
                toks.append(tv)
            return toks[-2:]

        st = small[:, 32:80].rearrange("p (t h s) -> p t h s", t=2, h=2)[:, :, :, 0:6]
        st = small[:, 32:56].rearrange("p (t h s) -> p t h s", t=2, h=2)
        mv = small[:, 64:68].rearrange("p (t s) -> p t s", t=2)
        ve = small[:, 72:74]
        rs = small[:, 76:78]
        s_ln = dsem("s_ln")
        s_o = dsem("s_o")
        lnp_free = [None]
        xa_tok = [t_x]

        def load_ln(gsrc, bsrc):
            SP.dma(lnp[:, 0, :], gsrc.to_broadcast([P, D]), s_ln, lnp_free[0])
            return SP.dma(lnp[:, 1, :], bsrc.to_broadcast([P, D]), s_ln)

        def layer_norm(t_y, gate, t_ln, last=False):
            tx = []
            for t in range(2):
                for h in range(2):
                    y = YB[2 * t + h]
                    v = vv[:, t, h * 512:(h + 1) * 512]
                    xs = xa[:, t, h * 512:(h + 1) * 512]
                    if isinstance(gate, float):
                        tk = V.do(lambda e, y=y, v=v, xs=xs: e.scalar_tensor_tensor(v, y[:, :], gate, xs, ALU.mult, ALU.add),
                                  t_y, xa_tok[0])
                        y_read[2 * t + h] = tk
                    else:
                        g = gb[:, h * 512:(h + 1) * 512]
                        tk = V.do(lambda e, y=y, v=v, g=g: e.tensor_tensor(v, y[:, :], g, ALU.mult), t_y, gate)
                        y_read[2 * t + h] = tk
                        tk = V.do(lambda e, v=v, xs=xs: e.tensor_tensor(v, v, xs, ALU.add), tk, xa_tok[0])
                    tk = V.do(lambda e, t=t, h=h, v=v: e.bn_stats(st[:, t, h, :], v), tk)
                tk = V.do(lambda e, t=t: e.bn_aggr(mv[:, t, :], st[:, t, :, :].rearrange("p a b -> p (a b)")), tk)
                tg = G.do(lambda e, t=t: e.tensor_scalar(ve[:, t:t + 1], mv[:, t, 1:2], EPS, None, ALU.add), tk)
                tg = G.do(lambda e, t=t: e.tensor_tensor(rs[:, t:t + 1], ve[:, t:t + 1], nhalf, ALU.pow), tg, t_nh)
                tx.append(V.do(lambda e, t=t: e.tensor_scalar(vv[:, t, :], vv[:, t, :], mv[:, t, 0:1], rs[:, t:t + 1],
                                                              ALU.subtract, ALU.mult), tg, tk))
            if not last:
                tl = S.do(lambda e: e.activation(lnp[:, :, :], lnp[:, :, :], ACT.Copy, scale=ALPHA), t_ln)
            else:
                tl = t_ln
            for t in range(2):
                tg = G.do(lambda e, t=t: e.tensor_tensor(xa[:, t, :], vv[:, t, :], lnp[:, 0, :], ALU.mult), tx[t], tl)
                tg = G.do(lambda e, t=t: e.tensor_tensor(xa[:, t, :], xa[:, t, :], lnp[:, 1, :], ALU.add), tg)
            lnp_free[0] = tg
            xa_tok[0] = tg
            return tx

        def proj(w, c0, dst, half=None):
            m = 64 if half is not None else P
            for kc in range(KC):
                tk = mm(dst, w[:, kc, c0:c0 + m], hT[:, kc, :], kc == 0, kc == KC - 1, mark=(kc == KC - 1))
            return tk

        def out_rows(pieces, zT, t_z, first_bias=None, n_total=KC):
            k = 0
            for src in pieces:
                n, w, tok = block(src, 2, D)
                PE.wait(tok)
                for q in range(2):
                    PE.wait(t_z[k] if isinstance(t_z, list) else t_z)
                    for t in range(2):
                        for h in range(2):
                            if k == 0 and first_bias is None:
                                PE.wait(y_read[2 * t + h])
                            tk = mm(YB[2 * t + h][:, :], zT(k)[:, t * P:(t + 1) * P], w[:, q, h * 512:(h + 1) * 512],
                                    k == 0 and first_bias is None, k == n_total - 1, mark=(t == 1 and h == 1))
                    k += 1
                released[n] = tk
            return tk

        def mixer_a(t_h):
            uT = area(0, KC, 30 + T)
            acc = area(2304, KC, T)
            zT = area(4352, KC, T)
            tmp = area(6400, 4, T)
            sq = area(7424, KC, T)
            tz = G.do(lambda e: e.memset(uT[:, :, 0:30], 0.0), t_mod[1])
            tu = []
            tmp_rd = [None] * 4
            for j in range(4):
                na, wa, ta_ = block(I["a_w_in"][0, :, 256 * j:256 * j + 256], KC, 256)
                ng, wg, tg_ = block(I["a_w_in"][0, :, D + 256 * j:D + 256 * j + 256], KC, 256)
                PE.wait(ta_, tg_, *t_h)
                for q in range(2):
                    f = 2 * j + q
                    wi, b = bank()
                    proj(wa, q * P, b[:, 0:T])
                    tk = proj(wg, q * P, b[:, T:2 * T])
                    r = f % 4
                    ts = S.do(lambda e, b=b, f=f, r=r: e.activation(tmp[:, r, :], b[:, T:2 * T], ACT.Sigmoid,
                                                                    bias=col("a_b_in", 8 + f)), tk, tmp_rd[r])
                    tv = V.do(lambda e, b=b, f=f, r=r: e.scalar_tensor_tensor(
                        uT[:, f, 30:30 + T], b[:, 0:T], col("a_b_in", f), tmp[:, r, :], ALU.add, ALU.mult), ts, tk)
                    w_read[wi] = tv
                    tmp_rd[r] = tv
                    tu.append(tv)
                released[na] = released[ng] = tk
            for f0 in range(0, KC, 2):
                last = [tu[f0], tu[f0 + 1]]
                for j in range(CW):
                    for q in range(2):
                        f = f0 + q
                        if j == 0:
                            last[q] = V.do(lambda e, f=f: e.tensor_scalar(acc[:, f, :], uT[:, f, 0:T], dw(0, f),
                                                                          col("a_b_dw", f), ALU.mult, ALU.add), last[q], tz)
                        else:
                            last[q] = V.do(lambda e, f=f, j=j: e.scalar_tensor_tensor(
                                acc[:, f, :], uT[:, f, j:j + T], dw(j, f), acc[:, f, :], ALU.mult, ALU.add), last[q])
            wi, b = bank()
            PE.wait(last[1], t_ones)
            for f in range(KC):
                tk = mm(b[:, 0:T], ones[:, :], acc[:, f, :], f == 0, f == KC - 1, mark=(f == KC - 1))
            td, tq = [], []
            for f in range(KC):
                td.append(V.do(lambda e, f=f, b=b: e.scalar_tensor_tensor(acc[:, f, :], b[:, 0:T], -1.0 / D, acc[:, f, :],
                                                                     ALU.mult, ALU.add), tk))
                tq.append(S.do(lambda e, f=f: e.activation(sq[:, f, :], acc[:, f, :], ACT.Square), td[-1]))
            w_read[wi] = td[-1]
            wi, b = bank()
            for f in range(KC):
                PE.wait(tq[f])
                tk = mm(b[:, 0:T], ones[:, :], sq[:, f, :], f == 0, f == KC - 1, mark=(f == KC - 1))
            tv = V.do(lambda e, b=b: e.tensor_scalar(tmp[:, 0, :], b[:, 0:T], 1.0 / D, EPS, ALU.mult, ALU.add), tk)
            w_read[wi] = tv
            tg = G.do(lambda e: e.tensor_tensor(tmp[:, 1, :], tmp[:, 0, :], nhalf.to_broadcast([P, T]), ALU.pow), tv, t_nh)
            tzs = []
            for f in range(KC):
                tv = V.do(lambda e, f=f: e.tensor_tensor(acc[:, f, :], acc[:, f, :], tmp[:, 1, :], ALU.mult), tg)
                tzs.append(S.do(lambda e, f=f: e.activation(zT[:, f, :], acc[:, f, :], ACT.Silu, bias=col("a_ln_b", f),
                                                            scale=col("a_ln_g", f)), tv))
            for t in range(2):
                for h in range(2):
                    PE.wait(y_read[2 * t + h], t_m)
                    mm(YB[2 * t + h][:, :], ones[0:1, :], bout[:, h * 512:(h + 1) * 512], True, False)
            return out_rows([I["a_w_out"][0, 256 * j:256 * j + 256, :] for j in range(4)], lambda k: zT[:, k, :], tzs,
                            first_bias=True)

        def mixer_b(t_h):
            uT = area(0, KC, 2 + T)
            gbT = area(2304, KC, T)
            zT = area(4352, KC, T)
            tmp = area(6400, 4, T)
            tz = G.do(lambda e: e.memset(uT[:, :, 0:2], 0.0), *t_h)
            tzs = []
            tmp_rd = [None] * 4
            for j in range(4):
                ps = [block(I["b_w_in"][0, :, D * k + 256 * j:D * k + 256 * j + 256], KC, 256) for k in range(3)]
                PE.wait(*[p[2] for p in ps], *t_h)
                for q in range(2):
                    f = 2 * j + q
                    wi, b = bank()
                    proj(ps[1][1], q * P, b[:, 0:T])
                    tk = proj(ps[2][1], q * P, b[:, T:2 * T])
                    r = f % 4
                    ta = S.do(lambda e, b=b, r=r: e.copy(tmp[:, r, :], b[:, 0:T]), tk, tmp_rd[r])
                    tv = V.do(lambda e, b=b, f=f, r=r: e.tensor_tensor(uT[:, f, 2:2 + T], b[:, T:2 * T], tmp[:, r, :], ALU.mult), ta)
                    w_read[wi] = tv
                    tmp_rd[r] = tv
                    wi, b = bank()
                    tk = proj(ps[0][1], q * P, b[:, 0:T])
                    ta = S.do(lambda e, b=b, f=f: e.copy(gbT[:, f, :], b[:, 0:T]), tk)
                    w_read[wi] = ta
                    w = lambda i, f=f: col("b_w_dw", i * 8 + f)
                    tv = V.do(lambda e, f=f, w=w: e.tensor_scalar(zT[:, f, :], uT[:, f, 0:T], w(0), None, ALU.mult), tv, tz)
                    for i in (1, 2):
                        tv = V.do(lambda e, f=f, w=w, i=i: e.scalar_tensor_tensor(
                            zT[:, f, :], uT[:, f, i:i + T], w(i), zT[:, f, :], ALU.mult, ALU.add), tv)
                    tzs.append(V.do(lambda e, f=f: e.tensor_tensor(zT[:, f, :], zT[:, f, :], gbT[:, f, :], ALU.mult), tv, ta))
                for p in ps:
                    released[p[0]] = tk
            return out_rows([I["b_w_out"][0, 256 * j:256 * j + 256, :] for j in range(4)], lambda k: zT[:, k, :], tzs)

        def moe(l, t_h):
            lg = area(0, 2, 40)
            m8 = area(80, 2, 2, 8)
            ix = area(112, 2, 2, 8).bitcast(U32)
            sc = area(144, 2, 8)
            ef = area(160, 2, 32)
            wt = area(224, 2, 32)
            pen = area(288, 2, 32)
            wT = area(352, T)
            hid = area(1024, 4, 4, T)
            sg = area(5120, 4, T)
            wi, b = bank()
            PE.wait(t_m, t_ones, *t_h)
            for t in range(2):
                o = b[:, 64 * t:64 * t + 36]
                for kc in range(KC):
                    mm(o, hT[:, kc, t * P:(t + 1) * P], wr[:, l, kc, :], kc == 0, False)
                tk = mm(o, ones[0:1, :], rb[:, l, :], False, True, mark=True)
            V.do(lambda e: e.memset(lg[:, :, 4:8], NEG))
            v = lambda f, *w: V.do(f, (V.sem, V.n), *w)
            v(lambda e, b=b: e.tensor_copy(lg[:, :, 0:4], b[:, 0:128].rearrange("p (t n) -> p t n", t=2)[:, :, 0:4]), tk)
            tv = v(lambda e, b=b: e.tensor_copy(lg[:, :, 8:40], b[:, 0:128].rearrange("p (t n) -> p t n", t=2)[:, :, 4:36]))
            w_read[wi] = tv
            for t in range(2):
                v(lambda e, t=t: e.max(m8[:, t, 0, :], lg[:, t, 0:8]))
                v(lambda e, t=t: e.max_index(ix[:, t, 0, :], m8[:, t, 0, :], lg[:, t, 0:8]))
                tv = v(lambda e, t=t: e.tensor_scalar(sc[:, t, 0:1], m8[:, t, 0, 0:1], -1.0, None, ALU.mult))
                ts = S.do(lambda e, t=t: e.activation(ef[:, t, 0:4], lg[:, t, 0:4], ACT.Exp, bias=sc[:, t, 0:1],
                                                      accum_out=sc[:, t, 1:2]), tv)
                v(lambda e, t=t: e.tensor_copy(sc[:, t, 2:3], ix[:, t, 0, 0:1]))
                v(lambda e, t=t: e.tensor_scalar(pen[:, t, :], const[:, C_IG:C_IG + 32], sc[:, t, 2:3], NEG,
                                                 ALU.not_equal, ALU.mult))
                v(lambda e, t=t: e.tensor_tensor(lg[:, t, 8:40], lg[:, t, 8:40], pen[:, t, :], ALU.add))
                v(lambda e, t=t: e.max(m8[:, t, 1, :], lg[:, t, 8:40]))
                v(lambda e, t=t: e.max_index(ix[:, t, 1, :], m8[:, t, 1, :], lg[:, t, 8:40]))
                tv = v(lambda e, t=t: e.tensor_scalar(sc[:, t, 0:1], m8[:, t, 1, 0:1], -1.0, None, ALU.mult), ts)
                ts = S.do(lambda e, t=t: e.activation(sc[:, t, 3:4], m8[:, t, 1, 1:2], ACT.Exp, bias=sc[:, t, 0:1]), tv)
                v(lambda e, t=t: e.tensor_scalar(sc[:, t, 4:5], sc[:, t, 3:4], 1.0, None, ALU.add), ts)
                v(lambda e, t=t: e.tensor_tensor(sc[:, t, 4:5], sc[:, t, 4:5], sc[:, t, 1:2], ALU.mult))
                v(lambda e, t=t: e.reciprocal(sc[:, t, 5:6], sc[:, t, 4:5]))
                v(lambda e, t=t: e.tensor_tensor(sc[:, t, 6:7], sc[:, t, 5:6], sc[:, t, 3:4], ALU.mult))
                v(lambda e, t=t: e.tensor_copy(sc[:, t, 0:1], ix[:, t, 1, 0:1]))
                v(lambda e, t=t: e.tensor_copy(sc[:, t, 1:2], ix[:, t, 1, 1:2]))
                v(lambda e, t=t: e.tensor_scalar(wt[:, t, :], const[:, C_IO:C_IO + 32], sc[:, t, 0:1], sc[:, t, 5:6],
                                                 ALU.is_equal, ALU.mult))
                v(lambda e, t=t: e.tensor_scalar(pen[:, t, :], const[:, C_IO:C_IO + 32], sc[:, t, 1:2], sc[:, t, 6:7],
                                                 ALU.is_equal, ALU.mult))
                tw = v(lambda e, t=t: e.tensor_tensor(wt[:, t, :], wt[:, t, :], pen[:, t, :], ALU.add))
            sg_rd = [None] * 4
            hid_rd = [None] * 4
            for e_ in range(E):
                gs, us = [], []
                for h in range(2):
                    gs.append(block(I["e_w_gate"][l, e_, 512 * h:512 * h + 512, :], 4, F))
                    us.append(block(I["e_w_up"][l, e_, 512 * h:512 * h + 512, :], 4, F))
                wi, wb = bank()
                PE.wait(tw)
                for t in range(2):
                    tk = mm(wb[:, t * P:(t + 1) * P], wt[:, t, e_:e_ + 1].to_broadcast([P, P]), ident, True, True, mark=True)
                k0 = e_ % 4
                twb = S.do(lambda e, wb=wb, k0=k0: e.copy(sg[:, k0, :], wb[:, 0:T]), tk, sg_rd[k0])
                w_read[wi] = twb
                PE.wait(*[x[2] for x in gs + us])
                th = []
                for f in range(4):
                    wi, b = bank()
                    for ws, o in ((gs, 0), (us, T)):
                        for kc in range(KC):
                            tk = mm(b[:, o:o + T], ws[kc // 4][1][:, kc % 4, f * P:(f + 1) * P], hT[:, kc, :],
                                    kc == 0, kc == KC - 1, mark=(kc == KC - 1))
                    hd = hid[:, k0, f, :]
                    ts = S.do(lambda e, b=b, hd=hd: e.activation(hd, b[:, 0:T], ACT.Silu), tk, hid_rd[k0])
                    tv = V.do(lambda e, b=b, hd=hd: e.tensor_tensor(hd, b[:, T:2 * T], hd, ALU.mult), ts)
                    w_read[wi] = tv
                    tv = V.do(lambda e, hd=hd, k0=k0: e.tensor_tensor(hd, hd, sg[:, k0, :], ALU.mult), tv, twb)
                    th.append(tv)
                sg_rd[k0] = tv
                for x in gs + us:
                    released[x[0]] = tk
                for h in range(2):
                    n, w, tok = block(I["e_w_down"][l, e_, 256 * h:256 * h + 256, :], 2, D)
                    PE.wait(tok)
                    for q in range(2):
                        k = 2 * h + q
                        PE.wait(th[k])
                        for t in range(2):
                            for n2 in range(2):
                                if e_ == 0 and k == 0:
                                    PE.wait(y_read[2 * t + n2])
                                tk = mm(YB[2 * t + n2][:, :], hid[:, k0, k, t * P:(t + 1) * P], w[:, q, n2 * 512:(n2 + 1) * 512],
                                        e_ == 0 and k == 0, e_ == E - 1 and k == 3, mark=(t == 1 and n2 == 1))
                    released[n] = tk
                hid_rd[k0] = tk
            return tk

        def ffn(win, wout, t_h):
            hid = area(0, 4, T)
            hrd = [None] * 4
            k = 0
            for j in range(11):
                ng, wg, tg_ = block(win[:, 256 * j:256 * j + 256], KC, 256)
                nu, wu, tu_ = block(win[:, DFF + 256 * j:DFF + 256 * j + 256], KC, 256)
                PE.wait(tg_, tu_, *t_h)
                th = []
                for q in range(2):
                    wi, b = bank()
                    proj(wg, q * P, b[:, 0:T])
                    tk = proj(wu, q * P, b[:, T:2 * T])
                    r = (2 * j + q) % 4
                    ts = S.do(lambda e, b=b, r=r: e.activation(hid[:, r, :], b[:, 0:T], ACT.Silu), tk, hrd[r])
                    tv = V.do(lambda e, b=b, r=r: e.tensor_tensor(hid[:, r, :], b[:, T:2 * T], hid[:, r, :], ALU.mult), ts)
                    w_read[wi] = tv
                    th.append(tv)
                released[ng] = released[nu] = tk
                n, w, tok = block(wout[256 * j:256 * j + 256, :], 2, D)
                PE.wait(tok)
                for q in range(2):
                    r = (2 * j + q) % 4
                    PE.wait(th[q])
                    for t in range(2):
                        for h in range(2):
                            if k == 0:
                                PE.wait(y_read[2 * t + h])
                            tk = mm(YB[2 * t + h][:, :], hid[:, r, t * P:(t + 1) * P], w[:, q, h * 512:(h + 1) * 512],
                                    k == 0, k == 21, mark=(t == 1 and h == 1))
                    hrd[r] = tk
                    k += 1
                released[n] = tk
            return tk

        def hybrid(l, t_h):
            W = I["w_in_2"][l]
            o = 0

            def take(*shape):
                nonlocal o
                a = area(o, *shape)
                o += int(np.prod(shape))
                return a

            qT = {"a": take(4, T), "b": take(4, T), "c": take(4, T), "i": take(4, T)}
            kT = {"a": take(4, T), "b": take(2, T), "c": take(1, T), "i": take(1, T)}
            va = take(2, 512)
            vb = take(2, 128)
            vc = take(2, 64)
            wi_ = take(2, 8)
            raw = take(2, T)
            rot = take(2, T)
            gates = hybrid_gates
            sm = take(4, 384)
            pt = take(2, 384)
            oT = {"a": take(4, T), "b": take(4, T), "c": take(4, T)}
            maskc = take(384)
            stt = take(2, 2, 4)
            raw_rd = [None] * 2
            rot_rd = [None] * 2
            cnt = [0]

            def rope(src, dst, scale, tk, wi, last):
                r = cnt[0] % 2
                cnt[0] += 1
                ta = S.do(lambda e, r=r: e.activation(raw[:, r, :], src, ACT.Copy, scale=scale), tk, raw_rd[r])
                if last:
                    w_read[wi] = ta
                wj, b = bank()
                PE.wait(ta)
                tp = mm(b[:, 0:T], perm, raw[:, r, :], True, True, mark=True)
                tg = G.do(lambda e, r=r: e.tensor_tensor(rot[:, r, :], raw[:, r, :], cos[:, :], ALU.mult), ta, t_rope, rot_rd[r])
                raw_rd[r] = [tg, tp]
                tv = V.do(lambda e, b=b: e.tensor_tensor(dst, b[:, 0:T], sin[:, :], ALU.mult), tp, t_rope)
                w_read[wj] = tv
                tv = V.do(lambda e, r=r: e.tensor_tensor(dst, dst, rot[:, r, :], ALU.add), tv, tg)
                rot_rd[r] = tv
                return tv

            pend = []

            def flush():
                for f in pend:
                    f()
                pend.clear()

            tok_of = {}

            def feat(c0, dst, key, scale):
                for j in range(2):
                    n, w, tok = block(W[:, c0 + 256 * j:c0 + 256 * j + 256], KC, 256)
                    PE.wait(tok, *t_h)
                    for q in range(2):
                        wi, b = bank()
                        tk = proj(w, q * P, b[:, 0:T])
                        f = 2 * j + q
                        flush()
                        pend.append(lambda b=b, f=f, tk=tk, wi=wi: tok_of.__setitem__(
                            key, rope(b[:, 0:T], dst[:, f, :], scale, tk, wi, True)))
                    released[n] = tk

            def dup(w, c0, dst, key):
                wi, b = bank()
                for hh in range(2):
                    tk = proj(w, c0, b[64 * hh:64 * hh + 64, 0:T], half=hh)
                flush()
                pend.append(lambda b=b, tk=tk, wi=wi: tok_of.__setitem__(key, rope(b[:, 0:T], dst, 1.0, tk, wi, True)))
                return tk

            def tokmajor(w, c0, n, dst):
                wi, b = bank()
                for t in range(2):
                    for kc in range(KC):
                        tk = mm(b[:, t * T:t * T + n], hT[:, kc, t * P:(t + 1) * P], w[:, kc, c0:c0 + n],
                                kc == 0, kc == KC - 1, mark=(kc == KC - 1))
                tv = V.do(lambda e, b=b: e.tensor_copy(dst, b[:, :].rearrange("p (t n) -> p t n", t=2)[:, :, 0:n]), tk)
                w_read[wi] = tv
                return tk, tv

            feat(2944, qT["i"], "qi", 1.0)
            n, w, tok = block(W[:, 3456:3528], KC, 72)
            PE.wait(tok)
            dup(w, 0, kT["i"][:, 0, :], "ki")
            tk, t_wi = tokmajor(w, 64, 8, wi_[:, :, :])
            released[n] = tk
            feat(2304, qT["c"], "qc", 0.125)
            n, w, tok = block(W[:, 2816:2944], KC, 128)
            PE.wait(tok)
            dup(w, 0, kT["c"][:, 0, :], "kc")
            tk, t_vc = tokmajor(w, 64, 64, vc[:, :, :])
            released[n] = tk

            srd = [None] * 4
            isc = sm[:, 3, :]
            flush()
            tacc = None
            for h in range(8):
                p = 64 * (h % 2)
                wi, b = bank()
                PE.wait(tok_of["qi"], tok_of["ki"])
                q = qT["i"][p:p + 64, h // 2, :]
                k = kT["i"][p:p + 64, 0, :]
                mm(b[:, 0:128], q[:, 0:128], k[:, 0:128], True, True)
                tk = mm(b[:, 128:384], q[:, 128:256], k[:, 0:256], True, True, mark=True)
                r = h % 2
                ts = S.do(lambda e, b=b, r=r: e.activation(sm[:, r, :], b[:, 0:384], ACT.Relu), tk, srd[r])
                w_read[wi] = ts
                for t, (a, z) in enumerate(((0, 128), (128, 384))):
                    if h == 0:
                        tv = V.do(lambda e, t=t, a=a, z=z, h=h, r=r: e.tensor_scalar(
                            isc[:, a:z], sm[:, r, a:z], wi_[:, t, h:h + 1], None, ALU.mult), ts, t_wi)
                    else:
                        tv = V.do(lambda e, t=t, a=a, z=z, h=h, r=r: e.scalar_tensor_tensor(
                            isc[:, a:z], sm[:, r, a:z], wi_[:, t, h:h + 1], isc[:, a:z], ALU.mult, ALU.add), ts, tacc)
                tacc = tv
                srd[r] = tv
            tv = V.do(lambda e: e.tensor_tensor(isc, isc, const[:, C_MC:C_MC + 384], ALU.add), tacc)
            top = small[:, 128:144].rearrange("p (t k) -> p t k", t=2)
            last = [tv, tv]
            for rnd in range(8):
                for t, (a, z) in enumerate(((0, 128), (128, 384))):
                    last[t] = V.do(lambda e, t=t, a=a, z=z: e.max(top[:, t, :], isc[:, a:z]), last[t])
                for t, (a, z) in enumerate(((0, 128), (128, 384))):
                    last[t] = V.do(lambda e, t=t, a=a, z=z: e.match_replace(isc[:, a:z], top[:, t, :], isc[:, a:z], GONE),
                                   last[t])
            tv = V.do(lambda e: e.tensor_scalar(maskc, isc, -2e38, NEG, ALU.is_gt, ALU.mult), last[1])
            t_mc = V.do(lambda e: e.tensor_tensor(maskc, maskc, const[:, C_MC:C_MC + 384], ALU.add), tv)

            hcount = [0]
            pt_rd = [None] * 2

            def heads(name, kidx, mask, t_mask, vsl, t_v, t_qk, sinks=None):
                t_o = []
                for j in range(4):
                    tkk, banks = [], []
                    for q in range(2):
                        h = 2 * j + q
                        p = 64 * q
                        wi, b = bank()
                        PE.wait(*t_qk)
                        qq = qT[name][p:p + 64, j, :]
                        kk = kT[name][p:p + 64, kidx(j), :]
                        mm(b[:, 0:128], qq[:, 0:128], kk[:, 0:128], True, True)
                        tkk.append(mm(b[:, 128:384], qq[:, 128:256], kk[:, 0:256], True, True, mark=True))
                        banks.append((wi, b))
                    u = hcount[0] % 2
                    hcount[0] += 1
                    mx, dn = stt[:, u, 0, :], stt[:, u, 1, :]
                    for q in range(2):
                        wi, b = banks[q]
                        r = 2 * u + q if False else q
                        for t, (a, z) in enumerate(((0, 128), (128, 384))):
                            tv = V.do(lambda e, a=a, z=z, q=q, t=t, b=b, mx=mx: e.tensor_tensor_reduce(
                                sm[:, q, a:z], b[:, a:z], mask[:, a:z], 1.0, GONE, ALU.add, ALU.max,
                                mx[:, 2 * q + t:2 * q + t + 1]), tkk[q], t_mask, srd[q])
                        w_read[wi] = tv
                    nmx = small[:, 160 + 4 * u:164 + 4 * u]
                    if sinks is None:
                        tv = V.do(lambda e, mx=mx, nmx=nmx: e.tensor_scalar(nmx, mx, -1.0, None, ALU.mult), tv)
                    else:
                        sk = sinks(j)
                        tv = V.do(lambda e, mx=mx, sk=sk: e.tensor_tensor(mx, mx, sk, ALU.max), tv, t_sink)
                        tv = V.do(lambda e, mx=mx, nmx=nmx: e.tensor_scalar(nmx, mx, -1.0, None, ALU.mult), tv)
                    for q in range(2):
                        for t, (a, z) in enumerate(((0, 128), (128, 384))):
                            i = 2 * q + t
                            ts = S.do(lambda e, a=a, z=z, q=q, i=i, nmx=nmx, dn=dn: e.activation(
                                sm[:, q, a:z], sm[:, q, a:z], ACT.Exp, bias=nmx[:, i:i + 1], accum_out=dn[:, i:i + 1]), tv)
                    if sinks is not None:
                        tmp4 = small[:, 176 + 4 * u:180 + 4 * u]
                        tv = V.do(lambda e, nmx=nmx, tmp4=tmp4, sk=sk: e.tensor_tensor(tmp4, nmx, sk, ALU.add), tv)
                        te = S.do(lambda e, tmp4=tmp4: e.activation(tmp4, tmp4, ACT.Exp), tv)
                        ts = V.do(lambda e, dn=dn, tmp4=tmp4: e.tensor_tensor(dn, dn, tmp4, ALU.add), te, ts)
                    rd = small[:, 192 + 4 * u:196 + 4 * u]
                    tv = V.do(lambda e, rd=rd, dn=dn: e.reciprocal(rd, dn), ts)
                    tn = []
                    for q in range(2):
                        for t, (a, z) in enumerate(((0, 128), (128, 384))):
                            i = 2 * q + t
                            tg = G.do(lambda e, a=a, z=z, q=q, i=i, rd=rd: e.tensor_scalar(
                                sm[:, q, a:z], sm[:, q, a:z], rd[:, i:i + 1], None, ALU.mult), tv, ts)
                        tn.append(tg)
                    wo, bo = bank()
                    for q in range(2):
                        wi, b = bank()
                        PE.wait(tn[q])
                        tr(b[:, 0:128], sm[:, q, 0:128], ident)
                        tr(b[:, 128:256], sm[:, q, 128:256], ident)
                        tk = tr(b[:, 256:384], sm[:, q, 256:384], ident, mark=True)
                        srd[q] = tk
                        tc = S.do(lambda e, q=q, b=b: e.copy(pt[:, q, :], b[:, 0:384]), tk, pt_rd[q])
                        w_read[wi] = tc
                        PE.wait(tc, t_v)
                        h = 2 * j + q
                        mm(bo[64 * q:64 * q + 64, 0:256], vsl(h, 0), pt[:, q, 0:256], True, False)
                        tk = mm(bo[64 * q:64 * q + 64, 128:256], vsl(h, 1), pt[:, q, 256:384], False, True, mark=True)
                        pt_rd[q] = tk
                    tv = V.do(lambda e, j=j, bo=bo: e.tensor_copy(oT[name][:, j, :], bo[:, 0:256]), tk)
                    w_read[wo] = tv
                return tv

            to = {}
            to["c"] = heads("c", lambda j: 0, maskc, t_mc, lambda h, s: vc[:, s, :], t_vc, (tok_of["qc"], tok_of["kc"]))
            feat(1536, qT["b"], "qb", 0.125)
            n, w, tok = block(W[:, 2048:2304], KC, 256)
            PE.wait(tok)
            dup(w, 0, kT["b"][:, 0, :], "kb0")
            dup(w, 64, kT["b"][:, 1, :], "kb1")
            tk, t_vb = tokmajor(w, 128, 128, vb[:, :, :])
            released[n] = tk
            flush()
            sk = lambda j: sink[:, l, 2 * j:2 * j + 2, :].rearrange("p h t -> p (h t)")
            to["b"] = heads("b", lambda j: j // 2, const[:, C_MB:C_MB + 384], t_const,
                            lambda h, s: vb[:, s, 64 * (h // 4):64 * (h // 4) + 64], t_vb,
                            (tok_of["qb"], tok_of["kb0"], tok_of["kb1"]), sk)
            feat(0, qT["a"], "qa", 0.125)
            feat(512, kT["a"], "ka", 1.0)
            for j in range(2):
                n, w, tok = block(W[:, 1024 + 256 * j:1280 + 256 * j], KC, 256)
                PE.wait(tok)
                tk, t_va = tokmajor(w, 0, 256, va[:, :, 256 * j:256 * j + 256])
                released[n] = tk
            flush()
            to["a"] = heads("a", lambda j: j, const[:, C_MA:C_MA + 384], t_const,
                            lambda h, s: va[:, s, 64 * h:64 * h + 64], t_va, (tok_of["qa"], tok_of["ka"]))

            tgt = {}
            for bi, nm in enumerate("abc"):
                for j in range(4):
                    c0 = 3528 + D * bi + 256 * j
                    n, w, tok = block(W[:, c0:c0 + 256], KC, 256)
                    PE.wait(tok)
                    for q in range(2):
                        f = 2 * j + q
                        wi, b = bank()
                        tk = proj(w, q * P, b[:, 0:T])
                        ts = S.do(lambda e, b=b, bi=bi, f=f: e.activation(gates[:, bi, f, :], b[:, 0:T], ACT.Sigmoid), tk)
                        w_read[wi] = ts
                        tgt[(nm, f)] = ts
                    released[n] = tk
            mT = area(0, KC, T)
            tz = []
            for nh in range(2):
                ws = [block(I[f"w_br_{nm}_2"][l, :, 512 * nh:512 * nh + 512], 4, 512) for nm in "abc"]
                PE.wait(*[w[2] for w in ws], *to.values())
                for fq in range(4):
                    f = 4 * nh + fq
                    wi, b = bank()
                    wj, b2 = bank()
                    dsts = {"a": b[:, 0:T], "b": b[:, T:2 * T], "c": b2[:, 0:T]}
                    for bi, nm in enumerate("abc"):
                        for k in range(4):
                            tk = mm(dsts[nm], ws[bi][1][:, k, fq * P:(fq + 1) * P], oT[nm][:, k, :], k == 0, k == 3,
                                    mark=(k == 3))
                    for bi, nm in enumerate("abc"):
                        tv = V.do(lambda e, bi=bi, f=f, s=dsts[nm]: e.tensor_tensor(gates[:, bi, f, :], s, gates[:, bi, f, :], ALU.mult),
                                  tk, tgt[(nm, f)])
                    w_read[wi] = w_read[wj] = tv
                    tv = G.do(lambda e, f=f: e.tensor_tensor(mT[:, f, :], gates[:, 0, f, :], gates[:, 1, f, :], ALU.add), tv)
                    tz.append(G.do(lambda e, f=f: e.tensor_tensor(mT[:, f, :], mT[:, f, :], gates[:, 2, f, :], ALU.add), tv))
                for w in ws:
                    released[w[0]] = tk
            return out_rows([I["w_out_2"][l, 256 * j:256 * j + 256, :] for j in range(4)], lambda k: mT[:, k, :], tz)

        hybrid_gates = sb("gates", [P, 3, KC, T])

        tf = fold(None, None, 0, SCM, SHM, t_mod[0])
        t_h = to_feature(xa, [t_x, t_x], tf, None)
        t_xa0 = S.do(lambda e: e.activation(xa[:, :, :], xa[:, :, :], ACT.Copy, scale=ALPHA), (PE.sem, PE.n))
        xa_tok[0] = t_xa0
        for l in range(DEPTH):
            tg = spread(l, 1, 0)
            t_ln = load_ln(I["mix_ln_g"][l:l + 1, :], I["mix_ln_b"][l:l + 1, :])
            ty = mixer_a(t_h) if l == 0 else mixer_b(t_h)
            tx = layer_norm(ty, tg, t_ln)
            tf = fold(colr("mix_ln_g", 8 * l, 8), colr("mix_ln_b", 8 * l, 8), l, SCF, SHF, t_mod[l], *t_h)
            t_h = to_feature(vv, tx, tf, ty)
            tg = spread(l, 2, 2)
            t_ln = load_ln(I["ffn_ln_g"][l:l + 1, :], I["ffn_ln_b"][l:l + 1, :])
            ty = moe(l, t_h)
            tx = layer_norm(ty, tg, t_ln)
            g_, b_ = colr("ffn_ln_g", 8 * l, 8), colr("ffn_ln_b", 8 * l, 8)
            if l == 0:
                tf = fold(g_, b_, 1, SCM, SHM, t_mod[1], *t_h)
            else:
                tf = fold(g_, b_, None, None, None, *t_h)
            t_h = to_feature(vv, tx, tf, ty)
        for l in range(DEPTH):
            for j in range(3):
                t_ln = load_ln(I["ln_g_2"][l, j:j + 1, :], I["ln_b_2"][l, j:j + 1, :])
                if j == 0:
                    ty = ffn(I["ffn1_in_2"][l], I["ffn1_out_2"][l], t_h)
                elif j == 1:
                    ty = hybrid(l, t_h)
                else:
                    ty = ffn(I["ffn2_in_2"][l], I["ffn2_out_2"][l], t_h)
                last = l == DEPTH - 1 and j == 2
                tx = layer_norm(ty, 1.0 if j == 1 else 0.5, t_ln, last)
                if not last:
                    i = 8 * (3 * l + j)
                    tf = fold(colr("ln_g_2", i, 8), colr("ln_b_2", i, 8), None, None, None, *t_h)
                    t_h = to_feature(vv, tx, tf, ty)
        t_out = SP.dma(out[0].rearrange("(t p) d -> p t d", p=P), xa[:, :, :], s_o, xa_tok[0])
        SP.wait(t_out)

        blk = ctx.enter_context(nc.Block())

        @blk.sync
        def _(e):
            SP.emit(e)

        @blk.tensor
        def _(e):
            PE.emit(e)

        @blk.vector
        def _(e):
            V.emit(e)

        @blk.scalar
        def _(e):
            S.emit(e)

        @blk.gpsimd
        def _(e):
            G.emit(e)


_INS = ["x", "c", "ada_w", "ada_b", "a_w_in", "a_b_in", "a_w_dw", "a_b_dw", "a_ln_g", "a_ln_b", "a_w_out", "a_b_out",
        "b_w_in", "b_w_dw", "b_w_out", "mix_ln_g", "mix_ln_b", "ffn_ln_g", "ffn_ln_b", "r_w_group", "r_b_group",
        "r_w_expert", "r_b_expert", "e_w_gate", "e_w_up", "e_w_down", "positions_2", "w_in_2", "sink_b_2", "w_br_a_2",
        "w_br_b_2", "w_br_c_2", "w_out_2", "ffn1_in_2", "ffn1_out_2", "ffn2_in_2", "ffn2_out_2", "ln_g_2", "ln_b_2"]


def kernel(**inputs):
    import numpy as _np
    import concourse.bacc as _bacc
    from concourse import mybir as _mybir
    from concourse.bass_utils import run_bass_kernel_spmd as _run

    nc = _bacc.Bacc("TRN2", target_bir_lowering=False, num_devices=1)
    arrays, aps = {}, {}
    for name in _INS:
        a = _np.ascontiguousarray(inputs[name])
        arrays[f"in_{name}_dram"] = a
        aps[name] = nc.dram_tensor(f"in_{name}_dram", a.shape, _mybir.dt.from_np(a.dtype), kind="ExternalInput").ap()
    c = constants()
    arrays["in_consts_dram"] = c
    aps["consts"] = nc.dram_tensor("in_consts_dram", c.shape, _mybir.dt.float32, kind="ExternalInput").ap()
    o = nc.dram_tensor("out_0_dram", (1, T, D), _mybir.dt.float32, kind="ExternalOutput").ap()
    program(nc, aps, o)
    r = _run(nc, [arrays], core_ids=[0])
    return r.results[0]["out_0_dram"]
```

```python
from contextlib import ExitStack

import numpy as np
import concourse.bass as bass
from concourse import mybir

F32 = mybir.dt.float32
U32 = mybir.dt.uint32
I32 = mybir.dt.int32
ALU = mybir.AluOpType
ACT = mybir.ActivationFunctionType
AX = mybir.AxisListType.X

P = 128
T = 256
D = 1024
KC = 8
E = 32
F = 512
DFF = 2816
DEPTH = 2
ALPHA = (2.0 * DEPTH) ** 0.25
EPS = 1e-5
NEG = -1e30
GONE = -3e38
CW = 31
SLOT = 2048
NSLOT = 7

C_ID, C_PERM, C_MA, C_MB, C_MC, C_IO, C_IG, C_INV, C_TRI, C_I5 = 0, 128, 256, 640, 1024, 1408, 1440, 1472, 1473, 1601
NCONST = 2113
CAP = 64

TWO_PI = 2.0 * np.pi


def split_const(value, parts, bits):
    out, rest = [], float(value)
    for _ in range(parts - 1):
        e = np.floor(np.log2(abs(rest))) + 1
        q = 2.0 ** (e - bits)
        c = np.floor(rest / q) * q
        out.append(float(c))
        rest -= c
    return out + [float(np.float32(rest))]


def constants():
    c = np.zeros((P, NCONST), np.float32)
    c[:, C_ID:C_ID + P] = np.eye(P)
    for i in range(P):
        if i % 64 < 32:
            c[i + 32, C_PERM + i] = -1.0
        else:
            c[i - 32, C_PERM + i] = 1.0
    t = np.arange(T)[:, None]
    s = np.arange(T)[None, :]
    d = t - s
    causal = d >= 0
    many = (causal & (d <= 128)).astype(np.float64) + (causal & (d % 4 == 0)) + (causal & (d % 16 == 0))
    ma = np.where(many > 0, np.log(np.maximum(many, 1)), NEG)
    mb = np.where(causal & (d <= 127), 0.0, NEG)
    mc = np.where(causal, 0.0, NEG)
    for off, m in ((C_MA, ma), (C_MB, mb), (C_MC, mc)):
        c[:, off:off + 128] = m[:128, :128]
        c[:, off + 128:off + 384] = m[128:, :]
    c[:, C_IO:C_IO + 32] = np.arange(32)[None, :]
    c[:, C_IG:C_IG + 32] = (np.arange(32) // 8)[None, :]
    inv = np.float32(10000.0) ** (-np.arange(0, 64, 2).astype(np.float32) / np.float32(64))
    c[:, C_INV] = np.tile(inv.astype(np.float32), 4)
    c[:, C_TRI:C_TRI + P] = np.triu(np.ones((P, P)), 1)
    c[:, C_I5:C_I5 + 512] = np.arange(512)[None, :]
    return c


class Queue:

    def __init__(self, sem):
        self.sem, self.n, self.ops, self.seen = sem, 0, [], {}

    def wait(self, *tokens):
        for tok in tokens:
            if tok is None:
                continue
            if isinstance(tok, list):
                self.wait(*tok)
                continue
            sem, v = tok
            if self.seen.get(id(sem), 0) < v:
                self.seen[id(sem)] = v
                self.ops.append(lambda e, sem=sem, v=v: e.wait_ge(sem, v))

    def do(self, fn, *waits, mark=True):
        self.wait(*waits)
        if not mark:
            self.ops.append(fn)
            return None
        self.n += 1
        self.ops.append(lambda e, fn=fn: fn(e).then_inc(self.sem, 1))
        return (self.sem, self.n)

    def dma(self, out, in_, sem, *waits):
        self.wait(*waits)
        self.ops.append(lambda e: e.dma_start(out, in_).then_inc(sem[0], 16))
        sem[1] += 16
        return (sem[0], sem[1])

    def emit(self, e):
        for op in self.ops:
            op(e)


def program(nc, I, out):
    with ExitStack() as ctx:
        sb = lambda name, shape, dt=F32: ctx.enter_context(nc.sbuf_tensor(name, shape, dt))
        sem = lambda name: ctx.enter_context(nc.semaphore(name))
        dsem = lambda name: [sem(name), 0]

        PE, V, S, G, SP = (Queue(sem(n)) for n in ("pe", "ve", "ac", "po", "sy"))

        const = sb("const", [P, NCONST])
        ident = const[:, C_ID:C_ID + P]
        perm = const[:, C_PERM:C_PERM + P]
        ones = sb("ones", [P, P])
        ring = sb("ring", [P, NSLOT, SLOT])
        ring_sem = [dsem(f"r{i}") for i in range(NSLOT)]
        xa = sb("xa", [P, 2, D])
        vv = sb("vv", [P, 2, D])
        hT = sb("hT", [P, KC, T])
        cols = sb("cols", [P, 5, P])
        mcol = sb("mcol", [P, 2, 48])
        ab = sb("ab", [P, 4, KC])
        mrow = sb("mrow", [P, 2, 3, 512])
        gb = sb("gb", [P, D])
        lnp = sb("lnp", [P, 2, D])
        cos = sb("cos", [P, T])
        sin = sb("sin", [P, T])
        cact = sb("cact", [P, KC, 32])
        small = sb("small", [P, 512])
        arena = sb("arena", [P, 20544])

        YB = [ctx.enter_context(nc.psum_tensor(f"y{i}", [P, 512], F32)) for i in range(4)]
        WB = [ctx.enter_context(nc.psum_tensor(f"w{i}", [P, 512], F32)) for i in range(4)]
        y_read = [None] * 4
        w_read = [None] * 4
        w_next = [0]

        def bank():
            i = w_next[0] % 4
            w_next[0] += 1
            PE.wait(w_read[i])
            return i, WB[i]

        def area(off, *shape):
            n = int(np.prod(shape))
            assert off + n <= 20544, (off, shape)
            a = arena[:, off:off + n]
            if len(shape) == 1:
                return a
            names = "abcd"[:len(shape)]
            return a.rearrange(f"p ({' '.join(names)}) -> p {' '.join(names)}",
                               **{k: s for k, s in zip(names, shape)})

        released = []

        def piece(*parts):
            n = len(released)
            s = n % NSLOT
            released.append(None)
            if n >= NSLOT:
                assert released[n - NSLOT] is not None, n
                SP.wait(released[n - NSLOT])
            for view, src in parts:
                tok = SP.dma(view(ring[:, s, :]), src, ring_sem[s])
            return n, ring[:, s, :], tok

        def block(src, k, n):
            view = lambda r: r[:, 0:k * n].rearrange("p (k n) -> p k n", k=k)
            i, r, tok = piece((view, src.rearrange("(k p) n -> p k n", p=P)))
            return i, view(r), tok

        def mm(o, l, r, start, stop, mark=False, **kw):
            return PE.do(lambda e: e.matmul(o, l, r, start=start, stop=stop, **kw), mark=mark)

        def tr(o, i, idn, mark=False):
            return PE.do(lambda e: e.transpose(o, i, idn), mark=mark)

        vrows = area(9216, 5, P)
        s_c = dsem("s_c")
        t_const = SP.dma(const[:, :], I["consts"], s_c)
        s_v = [dsem(f"s_v{i}") for i in range(5)]
        rows = {}

        def put(tile, at, name, ap, n):
            rows[name] = tile * P + at
            return SP.dma(vrows[at:at + n, tile, :], ap, s_v[tile])

        vec = lambda a: a.rearrange("r (c k) -> (r c) k", k=P)
        t0 = put(0, 0, "c", vec(I["c"]), 8)
        t0 = put(0, 8, "a_b_in", vec(I["a_b_in"]), 16)
        t0 = put(0, 24, "a_b_dw", vec(I["a_b_dw"]), 8)
        t0 = put(0, 32, "a_ln_g", vec(I["a_ln_g"]), 8)
        t0 = put(0, 40, "a_ln_b", vec(I["a_ln_b"]), 8)
        t0 = put(0, 48, "b_w_dw", vec(I["b_w_dw"][0]), 24)
        nv = [72, 64, 96, 124, 124]
        for j, nm in enumerate(("mix_ln_g", "mix_ln_b", "ffn_ln_g", "ffn_ln_b")):
            t1 = put(1, 16 * j, nm, vec(I[nm]), 16)
        for j, nm in enumerate(("ln_g_2", "ln_b_2")):
            t2 = put(2, 48 * j, nm, vec(I[nm].rearrange("l j d -> (l j) d")), 48)
        wdw = I["a_w_dw"][0].rearrange("r (c k) -> (r c) k", k=P)
        t3 = SP.dma(vrows[0:124, 3, :], wdw[0:124, :], s_v[3])
        t4 = SP.dma(vrows[0:124, 4, :], wdw[124:248, :], s_v[4])
        s_x = dsem("s_x")
        x_ap = I["x"][0].rearrange("(t p) d -> p t d", p=P)
        t_x = SP.dma(xa[:, :, :], x_ap, s_x)
        brow = vv[:, 0, :]
        bias = area(0, 2, 3, 512)
        s_ab = dsem("s_ab")
        for l in range(2):
            for g in range(4):
                src = I["ada_b"][l:l + 1, :].rearrange("o (c g n) -> o g c n", c=3, g=4)[:, g, :, :]
                t_ab = SP.dma(bias[32 * g:32 * g + 32, l, :, :], src.to_broadcast([32, 3, 512]), s_ab)
        bout = area(18432, D)[0:1, :]
        rb = sb("rb", [1, 2, 36])
        wr = sb("wr", [P, 2, KC, 36])
        cnt = sb("cnt", [P, E])
        blk_n = sb("blk_n", [P, 97], I32)
        slot_all = sb("slot_all", [P, 4])
        most = small[:, 208:209]
        late_sems = [sem(f"late{i}") for i in range(4)]
        late_dma, late_in, late_step = sem("late_dma"), sem("late_in"), sem("late_step")
        late_go = [sem(f"late_go{i}") for i in range(4)]
        sink = sb("sink", [P, 2, 8, 2])
        sinkr = sb("sinkr", [P, 16])
        s_m = dsem("s_m")
        SP.dma(bout, I["a_b_out"], s_m)
        for l in range(2):
            SP.dma(rb[:, l, 0:4], I["r_b_group"][l:l + 1, :], s_m)
            SP.dma(rb[:, l, 4:36], I["r_b_expert"][l:l + 1, :], s_m)
            SP.dma(wr[:, l, :, 0:4], I["r_w_group"][l].rearrange("(k p) n -> p k n", p=P), s_m)
            SP.dma(wr[:, l, :, 4:36], I["r_w_expert"][l].rearrange("(k p) n -> p k n", p=P), s_m)
        t_m = SP.dma(sinkr[:, :], I["sink_b_2"].rearrange("l h -> (l h)").unsqueeze(0).to_broadcast([P, 16]), s_m)
        posi = area(19456, T).bitcast(I32)
        s_p = dsem("s_p")
        t_p = SP.dma(posi, I["positions_2"].to_broadcast([P, T]), s_p)

        t_ones = G.do(lambda e: e.memset(ones[:, :], 1.0))
        nhalf = small[:, 0:1]
        t_nh = G.do(lambda e: e.memset(nhalf, -0.5))

        PE.wait(t_const, t_ones, t0, t1, t2, t3, t4)
        _, b0 = bank()
        for j in range(4):
            tk = tr(b0[:, j * P:j * P + nv[j]], vrows[0:nv[j], j, :], const[0:nv[j], 0:nv[j]], mark=(j == 3))
        for j in range(4):
            tv = V.do(lambda e, j=j: e.tensor_copy(cols[:, j, 0:nv[j]], b0[:, j * P:j * P + nv[j]]), tk)
        w_read[0] = tv
        _, b1 = bank()
        tk = tr(b1[:, 0:124], vrows[0:124, 4, :], const[0:124, 0:124], mark=True)
        t_cols = V.do(lambda e: e.tensor_copy(cols[:, 4, 0:124], b1[:, 0:124]), tk)
        w_read[1] = t_cols
        flat = cols[:, :, :].rearrange("p a b -> p (a b)")
        col = lambda name, i: flat[:, rows[name] + i:rows[name] + i + 1]
        colr = lambda name, i, n: flat[:, rows[name] + i:rows[name] + i + n]

        def dw(j, f):
            r = j * 8 + f
            return cols[:, 3 + r // 124, r % 124:r % 124 + 1]

        ang = area(8192, T)
        kq = area(8448, T)
        red = area(8704, T)
        V.do(lambda e: e.tensor_copy(ang, posi), t_p)
        tk = V.do(lambda e: e.tensor_scalar(red, ang, const[:, C_INV:C_INV + 1], None, ALU.mult), (V.sem, V.n), t_const)
        magic = 1.5 * 2.0 ** 23
        tk = V.do(lambda e: e.tensor_scalar(kq, red, float(np.float32(1 / TWO_PI)), magic, ALU.mult, ALU.add), tk)
        tk = V.do(lambda e: e.tensor_scalar(kq, kq, -magic, None, ALU.add), tk)
        for cst in split_const(TWO_PI, 4, 10):
            tk = V.do(lambda e, c=cst: e.scalar_tensor_tensor(red, kq, -c, red, ALU.mult, ALU.add), tk)
        tk = V.do(lambda e: e.tensor_scalar(red, red, float(np.float32(3.1415925)), float(np.float32(-3.1415925)), ALU.min, ALU.max), tk)
        ta = S.do(lambda e: e.activation(sin[:, :], red, ACT.Sin), tk)
        ta = S.do(lambda e: e.activation(cos[:, :], red, ACT.Sin, scale=0.5), tk)
        tk = V.do(lambda e: e.tensor_tensor(cos[:, :], cos[:, :], cos[:, :], ALU.mult), ta)
        t_rope = V.do(lambda e: e.tensor_scalar(cos[:, :], cos[:, :], -2.0, 1.0, ALU.mult, ALU.add), tk)
        tk = V.do(lambda e: e.tensor_copy(sink[:, :, :, 0], sinkr[:, :].rearrange("p (l h) -> p l h", l=2)), t_m)
        t_sink = V.do(lambda e: e.tensor_copy(sink[:, :, :, 1], sinkr[:, :].rearrange("p (l h) -> p l h", l=2)), t_m)

        ca = small[:, 8:16]
        ta = S.do(lambda e: e.activation(ca, colr("c", 0, 8), ACT.Silu), t_cols)
        t_ca = V.do(lambda e: e.tensor_copy(cact[:, :, :], ca.unsqueeze(2).to_broadcast([P, KC, 32])), ta)

        def ada(l):
            for cb in range(3):
                wi, b = bank()
                for kc in range(KC):
                    n, w, tok = piece((lambda r: r, I["ada_w"][l, kc * P:(kc + 1) * P, cb * 2048:(cb + 1) * 2048]))
                    PE.wait(tok, t_ca)
                    for g in range(4):
                        tk = mm(b[32 * g:32 * g + 32, :], cact[:, kc, :], w[:, g * 512:(g + 1) * 512],
                                kc == 0, kc == KC - 1, mark=(g == 3))
                    released[n] = tk
                tv = V.do(lambda e, b=b, cb=cb: e.tensor_tensor(mrow[:, l, cb, :], b[:, :], bias[:, l, cb, :], ALU.add), tk, t_ab)
                w_read[wi] = tv
                wi, b = bank()
                PE.wait(tv)
                for j in range(4):
                    tk = tr(b[:, j * P:(j + 1) * P], mrow[:, l, cb, j * P:(j + 1) * P], ident, mark=(j == 3))
                src = b[:, :].rearrange("p (j g r) -> p j g r", j=4, g=4)[:, :, :, 0]
                dst = mcol[:, l, cb * 16:(cb + 1) * 16].rearrange("p (g j) -> p j g", g=4)
                tv = V.do(lambda e, s=src, d=dst: e.tensor_copy(d, s), tk)
                w_read[wi] = tv
            return tv

        def spread(l, cb, g):
            for h in range(2):
                wi, b = bank()
                p = 32 * (g + h)
                tk = mm(b[:, :], ones[p:p + 1, :], mrow[p:p + 1, l, cb, :], True, True, mark=True)
                tv = V.do(lambda e, b=b, h=h: e.tensor_scalar(gb[:, h * 512:(h + 1) * 512], b[:, :], 1.0, None, ALU.add), tk)
                w_read[wi] = tv
            return tv

        t_mod = [ada(0), ada(1)]
        SHM, SCM, GM, SHF, SCF, GF = range(6)
        mvec = lambda l, w: mcol[:, l, 8 * w:8 * w + 8]

        def fold(gcol, bcol, l, sc, sh, *waits):
            if sc is None:
                V.do(lambda e: e.tensor_copy(ab[:, 0, :], gcol), *waits)
                return V.do(lambda e: e.tensor_copy(ab[:, 1, :], bcol))
            t = V.do(lambda e: e.tensor_scalar(ab[:, 2, :], mvec(l, sc), 1.0, None, ALU.add), *waits)
            if gcol is None:
                V.do(lambda e: e.tensor_copy(ab[:, 0, :], ab[:, 2, :]), t)
                return V.do(lambda e: e.tensor_copy(ab[:, 1, :], mvec(l, sh)))
            V.do(lambda e: e.tensor_tensor(ab[:, 0, :], ab[:, 2, :], gcol, ALU.mult), t)
            t = V.do(lambda e: e.tensor_tensor(ab[:, 3, :], ab[:, 2, :], bcol, ALU.mult))
            return V.do(lambda e: e.tensor_tensor(ab[:, 1, :], ab[:, 3, :], mvec(l, sh), ALU.add), t)

        def to_feature(src, t_src, t_ab, t_free):
            toks = []
            for f in range(0, KC, 2):
                wi, b = bank()
                for q in range(2):
                    for t in range(2):
                        PE.wait(t_src[t])
                        tk = tr(b[:, q * T + t * P:q * T + (t + 1) * P], src[:, t, (f + q) * P:(f + q + 1) * P],
                                ident, mark=(q == 1 and t == 1))
                for q in range(2):
                    if f % 4 == 0:
                        tv = V.do(lambda e, b=b, f=f + q, q=q: e.tensor_scalar(
                            hT[:, f, :], b[:, q * T:(q + 1) * T], ab[:, 0, f:f + 1], ab[:, 1, f:f + 1],
                            ALU.mult, ALU.add), tk, t_ab, t_free)
                    else:
                        tv = S.do(lambda e, b=b, f=f + q, q=q: e.activation(
                            hT[:, f, :], b[:, q * T:(q + 1) * T], ACT.Identity, bias=ab[:, 1, f:f + 1],
                            scale=ab[:, 0, f:f + 1]), tk, t_ab, t_free)
                w_read[wi] = tv
                toks.append(tv)
            return toks[-2:]

        st = small[:, 32:80].rearrange("p (t h s) -> p t h s", t=2, h=2)[:, :, :, 0:6]
        st = small[:, 32:56].rearrange("p (t h s) -> p t h s", t=2, h=2)
        mv = small[:, 64:68].rearrange("p (t s) -> p t s", t=2)
        ve = small[:, 72:74]
        rs = small[:, 76:78]
        s_ln = dsem("s_ln")
        s_o = dsem("s_o")
        lnp_free = [None]
        xa_tok = [t_x]

        def load_ln(gsrc, bsrc):
            SP.dma(lnp[:, 0, :], gsrc.to_broadcast([P, D]), s_ln, lnp_free[0])
            return SP.dma(lnp[:, 1, :], bsrc.to_broadcast([P, D]), s_ln)

        def layer_norm(t_y, gate, t_ln, last=False):
            tx = []
            for t in range(2):
                for h in range(2):
                    y = YB[2 * t + h]
                    v = vv[:, t, h * 512:(h + 1) * 512]
                    xs = xa[:, t, h * 512:(h + 1) * 512]
                    if isinstance(gate, float):
                        tk = V.do(lambda e, y=y, v=v, xs=xs: e.scalar_tensor_tensor(v, y[:, :], gate, xs, ALU.mult, ALU.add),
                                  t_y, xa_tok[0])
                        y_read[2 * t + h] = tk
                    else:
                        g = gb[:, h * 512:(h + 1) * 512]
                        tk = V.do(lambda e, y=y, v=v, g=g: e.tensor_tensor(v, y[:, :], g, ALU.mult), t_y, gate)
                        y_read[2 * t + h] = tk
                        tk = V.do(lambda e, v=v, xs=xs: e.tensor_tensor(v, v, xs, ALU.add), tk, xa_tok[0])
                    tk = V.do(lambda e, t=t, h=h, v=v: e.bn_stats(st[:, t, h, :], v), tk)
                tk = V.do(lambda e, t=t: e.bn_aggr(mv[:, t, :], st[:, t, :, :].rearrange("p a b -> p (a b)")), tk)
                tg = G.do(lambda e, t=t: e.tensor_scalar(ve[:, t:t + 1], mv[:, t, 1:2], EPS, None, ALU.add), tk)
                tg = G.do(lambda e, t=t: e.tensor_tensor(rs[:, t:t + 1], ve[:, t:t + 1], nhalf, ALU.pow), tg, t_nh)
                tx.append(V.do(lambda e, t=t: e.tensor_scalar(vv[:, t, :], vv[:, t, :], mv[:, t, 0:1], rs[:, t:t + 1],
                                                              ALU.subtract, ALU.mult), tg, tk))
            if not last:
                tl = S.do(lambda e: e.activation(lnp[:, :, :], lnp[:, :, :], ACT.Copy, scale=ALPHA), t_ln)
            else:
                tl = t_ln
            for t in range(2):
                tg = G.do(lambda e, t=t: e.tensor_tensor(xa[:, t, :], vv[:, t, :], lnp[:, 0, :], ALU.mult), tx[t], tl)
                tg = G.do(lambda e, t=t: e.tensor_tensor(xa[:, t, :], xa[:, t, :], lnp[:, 1, :], ALU.add), tg)
            lnp_free[0] = tg
            xa_tok[0] = tg
            return tx

        def proj(w, c0, dst, half=None):
            m = 64 if half is not None else P
            for kc in range(KC):
                tk = mm(dst, w[:, kc, c0:c0 + m], hT[:, kc, :], kc == 0, kc == KC - 1, mark=(kc == KC - 1))
            return tk

        def out_rows(pieces, zT, t_z, first_bias=None, n_total=KC):
            k = 0
            for src in pieces:
                n, w, tok = block(src, 2, D)
                PE.wait(tok)
                for q in range(2):
                    PE.wait(t_z[k] if isinstance(t_z, list) else t_z)
                    for t in range(2):
                        for h in range(2):
                            if k == 0 and first_bias is None:
                                PE.wait(y_read[2 * t + h])
                            tk = mm(YB[2 * t + h][:, :], zT(k)[:, t * P:(t + 1) * P], w[:, q, h * 512:(h + 1) * 512],
                                    k == 0 and first_bias is None, k == n_total - 1, mark=(t == 1 and h == 1))
                    k += 1
                released[n] = tk
            return tk

        def mixer_a(t_h):
            uT = area(0, KC, 30 + T)
            acc = area(2304, KC, T)
            zT = area(4352, KC, T)
            tmp = area(6400, 4, T)
            sq = area(7424, KC, T)
            tz = G.do(lambda e: e.memset(uT[:, :, 0:30], 0.0), t_mod[1])
            tu = []
            tmp_rd = [None] * 4
            for j in range(4):
                na, wa, ta_ = block(I["a_w_in"][0, :, 256 * j:256 * j + 256], KC, 256)
                ng, wg, tg_ = block(I["a_w_in"][0, :, D + 256 * j:D + 256 * j + 256], KC, 256)
                PE.wait(ta_, tg_, *t_h)
                for q in range(2):
                    f = 2 * j + q
                    wi, b = bank()
                    proj(wa, q * P, b[:, 0:T])
                    tk = proj(wg, q * P, b[:, T:2 * T])
                    r = f % 4
                    ts = S.do(lambda e, b=b, f=f, r=r: e.activation(tmp[:, r, :], b[:, T:2 * T], ACT.Sigmoid,
                                                                    bias=col("a_b_in", 8 + f)), tk, tmp_rd[r])
                    tv = V.do(lambda e, b=b, f=f, r=r: e.scalar_tensor_tensor(
                        uT[:, f, 30:30 + T], b[:, 0:T], col("a_b_in", f), tmp[:, r, :], ALU.add, ALU.mult), ts, tk)
                    w_read[wi] = tv
                    tmp_rd[r] = tv
                    tu.append(tv)
                released[na] = released[ng] = tk
            for f0 in range(0, KC, 2):
                last = [tu[f0], tu[f0 + 1]]
                for j in range(CW):
                    for q in range(2):
                        f = f0 + q
                        if j == 0:
                            last[q] = V.do(lambda e, f=f: e.tensor_scalar(acc[:, f, :], uT[:, f, 0:T], dw(0, f),
                                                                          col("a_b_dw", f), ALU.mult, ALU.add), last[q], tz)
                        else:
                            last[q] = V.do(lambda e, f=f, j=j: e.scalar_tensor_tensor(
                                acc[:, f, :], uT[:, f, j:j + T], dw(j, f), acc[:, f, :], ALU.mult, ALU.add), last[q])
            wi, b = bank()
            PE.wait(last[1], t_ones)
            for f in range(KC):
                tk = mm(b[:, 0:T], ones[:, :], acc[:, f, :], f == 0, f == KC - 1, mark=(f == KC - 1))
            td, tq = [], []
            for f in range(KC):
                td.append(V.do(lambda e, f=f, b=b: e.scalar_tensor_tensor(acc[:, f, :], b[:, 0:T], -1.0 / D, acc[:, f, :],
                                                                     ALU.mult, ALU.add), tk))
                tq.append(S.do(lambda e, f=f: e.activation(sq[:, f, :], acc[:, f, :], ACT.Square), td[-1]))
            w_read[wi] = td[-1]
            wi, b = bank()
            for f in range(KC):
                PE.wait(tq[f])
                tk = mm(b[:, 0:T], ones[:, :], sq[:, f, :], f == 0, f == KC - 1, mark=(f == KC - 1))
            tv = V.do(lambda e, b=b: e.tensor_scalar(tmp[:, 0, :], b[:, 0:T], 1.0 / D, EPS, ALU.mult, ALU.add), tk)
            w_read[wi] = tv
            tg = G.do(lambda e: e.tensor_tensor(tmp[:, 1, :], tmp[:, 0, :], nhalf.to_broadcast([P, T]), ALU.pow), tv, t_nh)
            tzs = []
            for f in range(KC):
                tv = V.do(lambda e, f=f: e.tensor_tensor(acc[:, f, :], acc[:, f, :], tmp[:, 1, :], ALU.mult), tg)
                tzs.append(S.do(lambda e, f=f: e.activation(zT[:, f, :], acc[:, f, :], ACT.Silu, bias=col("a_ln_b", f),
                                                            scale=col("a_ln_g", f)), tv))
            for t in range(2):
                for h in range(2):
                    PE.wait(y_read[2 * t + h], t_m)
                    mm(YB[2 * t + h][:, :], ones[0:1, :], bout[:, h * 512:(h + 1) * 512], True, False)
            return out_rows([I["a_w_out"][0, 256 * j:256 * j + 256, :] for j in range(4)], lambda k: zT[:, k, :], tzs,
                            first_bias=True)

        def mixer_b(t_h):
            uT = area(0, KC, 2 + T)
            gbT = area(2304, KC, T)
            zT = area(4352, KC, T)
            tmp = area(6400, 4, T)
            tz = G.do(lambda e: e.memset(uT[:, :, 0:2], 0.0), *t_h)
            tzs = []
            tmp_rd = [None] * 4
            for j in range(4):
                ps = [block(I["b_w_in"][0, :, D * k + 256 * j:D * k + 256 * j + 256], KC, 256) for k in range(3)]
                PE.wait(*[p[2] for p in ps], *t_h)
                for q in range(2):
                    f = 2 * j + q
                    wi, b = bank()
                    proj(ps[1][1], q * P, b[:, 0:T])
                    tk = proj(ps[2][1], q * P, b[:, T:2 * T])
                    r = f % 4
                    ta = S.do(lambda e, b=b, r=r: e.copy(tmp[:, r, :], b[:, 0:T]), tk, tmp_rd[r])
                    tv = V.do(lambda e, b=b, f=f, r=r: e.tensor_tensor(uT[:, f, 2:2 + T], b[:, T:2 * T], tmp[:, r, :], ALU.mult), ta)
                    w_read[wi] = tv
                    tmp_rd[r] = tv
                    wi, b = bank()
                    tk = proj(ps[0][1], q * P, b[:, 0:T])
                    ta = S.do(lambda e, b=b, f=f: e.copy(gbT[:, f, :], b[:, 0:T]), tk)
                    w_read[wi] = ta
                    w = lambda i, f=f: col("b_w_dw", i * 8 + f)
                    tv = V.do(lambda e, f=f, w=w: e.tensor_scalar(zT[:, f, :], uT[:, f, 0:T], w(0), None, ALU.mult), tv, tz)
                    for i in (1, 2):
                        tv = V.do(lambda e, f=f, w=w, i=i: e.scalar_tensor_tensor(
                            zT[:, f, :], uT[:, f, i:i + T], w(i), zT[:, f, :], ALU.mult, ALU.add), tv)
                    tzs.append(V.do(lambda e, f=f: e.tensor_tensor(zT[:, f, :], zT[:, f, :], gbT[:, f, :], ALU.mult), tv, ta))
                for p in ps:
                    released[p[0]] = tk
            return out_rows([I["b_w_out"][0, 256 * j:256 * j + 256, :] for j in range(4)], lambda k: zT[:, k, :], tzs)

        def moe(l, t_h):
            lg = area(0, 2, 40)
            m8 = area(80, 2, 2, 8)
            ix = area(112, 2, 2, 8).bitcast(U32)
            sc = area(144, 2, 8)
            ef = area(160, 2, 32)
            oh = area(224, 2, 2, 32)
            pen = area(352, 2, 32)
            cum = area(416, 2, 32)
            rk = area(480, 4)
            slot = area(484, 4)
            sg = area(488, 4, 4)
            jk = area(504, 4, 32)
            oo = area(632, 2, 32)
            xg = area(768, 2, KC, 512)
            Sg = area(8960, 2, 2, 512)
            Cg = area(11008, 2, 2, 512)
            hd = area(13056, 2, T)
            he = area(13568, 2, 2, 2, CAP)
            ye = area(14080, 2, 2, 512)
            ct = area(16128, 2, T)
            tmpc = area(16640, 512)
            wi, b = bank()
            PE.wait(t_m, t_ones, *t_h)
            for t in range(2):
                o = b[:, 64 * t:64 * t + 36]
                for kc in range(KC):
                    mm(o, hT[:, kc, t * P:(t + 1) * P], wr[:, l, kc, :], kc == 0, False)
                tk = mm(o, ones[0:1, :], rb[:, l, :], False, True, mark=True)
            V.do(lambda e: e.memset(lg[:, :, 4:8], NEG))
            v = lambda f, *w: V.do(f, (V.sem, V.n), *w)
            v(lambda e, b=b: e.tensor_copy(lg[:, :, 0:4], b[:, 0:128].rearrange("p (t n) -> p t n", t=2)[:, :, 0:4]), tk)
            tv = v(lambda e, b=b: e.tensor_copy(lg[:, :, 8:40], b[:, 0:128].rearrange("p (t n) -> p t n", t=2)[:, :, 4:36]))
            w_read[wi] = tv
            for t in range(2):
                v(lambda e, t=t: e.max(m8[:, t, 0, :], lg[:, t, 0:8]))
                v(lambda e, t=t: e.max_index(ix[:, t, 0, :], m8[:, t, 0, :], lg[:, t, 0:8]))
                tv = v(lambda e, t=t: e.tensor_scalar(sc[:, t, 0:1], m8[:, t, 0, 0:1], -1.0, None, ALU.mult))
                ts = S.do(lambda e, t=t: e.activation(ef[:, t, 0:4], lg[:, t, 0:4], ACT.Exp, bias=sc[:, t, 0:1],
                                                      accum_out=sc[:, t, 1:2]), tv)
                v(lambda e, t=t: e.tensor_copy(sc[:, t, 2:3], ix[:, t, 0, 0:1]))
                v(lambda e, t=t: e.tensor_scalar(pen[:, t, :], const[:, C_IG:C_IG + 32], sc[:, t, 2:3], NEG,
                                                 ALU.not_equal, ALU.mult))
                v(lambda e, t=t: e.tensor_tensor(lg[:, t, 8:40], lg[:, t, 8:40], pen[:, t, :], ALU.add))
                v(lambda e, t=t: e.max(m8[:, t, 1, :], lg[:, t, 8:40]))
                v(lambda e, t=t: e.max_index(ix[:, t, 1, :], m8[:, t, 1, :], lg[:, t, 8:40]))
                tv = v(lambda e, t=t: e.tensor_scalar(sc[:, t, 0:1], m8[:, t, 1, 0:1], -1.0, None, ALU.mult), ts)
                ts = S.do(lambda e, t=t: e.activation(sc[:, t, 3:4], m8[:, t, 1, 1:2], ACT.Exp, bias=sc[:, t, 0:1]), tv)
                v(lambda e, t=t: e.tensor_scalar(sc[:, t, 4:5], sc[:, t, 3:4], 1.0, None, ALU.add), ts)
                v(lambda e, t=t: e.tensor_tensor(sc[:, t, 4:5], sc[:, t, 4:5], sc[:, t, 1:2], ALU.mult))
                v(lambda e, t=t: e.reciprocal(sc[:, t, 5:6], sc[:, t, 4:5]))
                v(lambda e, t=t: e.tensor_tensor(sc[:, t, 6:7], sc[:, t, 5:6], sc[:, t, 3:4], ALU.mult))
                v(lambda e, t=t: e.tensor_copy(sc[:, t, 0:2], ix[:, t, 1, 0:2]))
                for j in range(2):
                    v(lambda e, t=t, j=j: e.tensor_scalar(oh[:, t, j, :], const[:, C_IO:C_IO + 32], sc[:, t, j:j + 1], None,
                                                          ALU.is_equal))
                to_ = v(lambda e, t=t: e.tensor_tensor(oo[:, t, :], oh[:, t, 0, :], oh[:, t, 1, :], ALU.add))
            wi, b = bank()
            PE.wait(to_)
            tri = const[:, C_TRI:C_TRI + P]
            mm(b[:, 0:32], tri, oo[:, 0, :], True, True)
            mm(b[:, 32:64], ones[:, :], oo[:, 0, :], True, False)
            mm(b[:, 32:64], tri, oo[:, 1, :], False, True)
            mm(b[:, 64:96], ones[:, :], oo[:, 0, :], True, False)
            tk = mm(b[:, 64:96], ones[:, :], oo[:, 1, :], False, True, mark=True)
            v(lambda e, b=b: e.tensor_copy(cum[:, :, :], b[:, 0:64].rearrange("p (t n) -> p t n", t=2)), tk)
            tv = v(lambda e, b=b: e.tensor_copy(cnt[:, :], b[:, 64:96]))
            w_read[wi] = tv
            for r in range(3):
                v(lambda e, r=r: e.tensor_scalar(blk_n[:, 1 + 32 * r:33 + 32 * r], cnt[:, :], float(CAP * (r + 1)), None,
                                                 ALU.is_gt))
            v(lambda e: e.tensor_reduce(most, cnt[:, :], AX, ALU.max))
            t_blk = v(lambda e: e.tensor_scalar(blk_n[:, 0:1], most, float(CAP), None, ALU.is_gt))
            for t in range(2):
                for j in range(2):
                    i = 2 * t + j
                    V.do(lambda e, t=t, j=j, i=i: e.tensor_tensor_reduce(
                        jk[:, i, :], oh[:, t, j, :], cum[:, t, :], 1.0, 0.0, ALU.mult, ALU.add, rk[:, i:i + 1]), tv)
            v(lambda e: e.scalar_tensor_tensor(slot, sc[:, :, 0:2], float(CAP), rk.rearrange("p (t j) -> p t j", t=2),
                                               ALU.mult, ALU.add) if False else
              e.scalar_tensor_tensor(slot.rearrange("p (t j) -> p t j", t=2), sc[:, :, 0:2], float(CAP),
                                     rk.rearrange("p (t j) -> p t j", t=2), ALU.mult, ALU.add))
            v(lambda e: e.tensor_copy(slot_all[:, :], slot))
            for r in range(1, 4):
                v(lambda e, r=r: e.tensor_scalar(jk[:, 0, 0:4], rk, float(CAP * r), float(CAP * (E - 1)), ALU.is_ge, ALU.mult))
                v(lambda e: e.tensor_tensor(slot_all[:, :], slot_all[:, :], jk[:, 0, 0:4], ALU.add))
            v(lambda e: e.tensor_scalar(slot_all[:, :], slot_all[:, :], -float(CAP * (E - 1)), None, ALU.add))
            v(lambda e: e.tensor_scalar(jk[:, 0, 0:4], rk, float(CAP), -1e6, ALU.is_ge, ALU.mult))
            v(lambda e: e.tensor_tensor(slot, slot, jk[:, 0, 0:4], ALU.add))
            for g in range(4):
                v(lambda e, g=g: e.tensor_scalar(sg[:, g, :], slot, -512.0 * g, None, ALU.add))

            xg_rd, c_rd = [None] * 2, [None] * 2
            t_S, t_C, t_xg = [None] * 4, [None] * 4, {}

            def choose(g):
                u = g % 2
                i5 = const[:, C_I5:C_I5 + 512]
                for t in range(2):
                    a = sg[:, g, 2 * t:2 * t + 1]
                    z = sg[:, g, 2 * t + 1:2 * t + 2]
                    tv = V.do(lambda e, t=t, a=a: e.tensor_scalar(Sg[:, u, t, :], i5, a, None, ALU.is_equal),
                              (V.sem, V.n), xg_rd[u])
                    t_S[g] = V.do(lambda e, t=t, z=z: e.scalar_tensor_tensor(Sg[:, u, t, :], i5, z, Sg[:, u, t, :],
                                                                             ALU.is_equal, ALU.add), tv)
                for t in range(2):
                    a = sg[:, g, 2 * t:2 * t + 1]
                    z = sg[:, g, 2 * t + 1:2 * t + 2]
                    V.do(lambda e, t=t, a=a: e.tensor_scalar(Cg[:, u, t, :], i5, a, sc[:, t, 5:6], ALU.is_equal, ALU.mult),
                         c_rd[u], t_S[g])
                    tv = V.do(lambda e, t=t, z=z: e.tensor_scalar(tmpc, i5, z, sc[:, t, 6:7], ALU.is_equal, ALU.mult),
                              (V.sem, V.n))
                    t_C[g] = V.do(lambda e, t=t: e.tensor_tensor(Cg[:, u, t, :], Cg[:, u, t, :], tmpc, ALU.add), tv)

            def gather(g, kc):
                u = g % 2
                wi, b = bank()
                PE.wait(t_S[g])
                for t in range(2):
                    tk = mm(b[:, :], vv[:, t, kc * P:(kc + 1) * P], Sg[:, u, t, :], t == 0, t == 1, mark=(t == 1))
                if kc == KC - 1:
                    xg_rd[u] = tk
                if kc % 2:
                    tv = V.do(lambda e, b=b: e.tensor_scalar(xg[:, u, kc, :], b[:, :], ab[:, 0, kc:kc + 1],
                                                             ab[:, 1, kc:kc + 1], ALU.mult, ALU.add), tk, x_done.get(g - 2))
                else:
                    tv = S.do(lambda e, b=b: e.activation(xg[:, u, kc, :], b[:, :], ACT.Identity, bias=ab[:, 1, kc:kc + 1],
                                                          scale=ab[:, 0, kc:kc + 1]), tk, x_done.get(g - 2))
                w_read[wi] = tv
                t_xg.setdefault(g, []).append(tv)

            x_done = {}
            hd_t, he_t, ye_t, ct_t = {}, {}, {}, {}
            hd_rd, he_rd, ye_rd, ct_rd = [None] * 2, [None] * 2, [None] * 2, [None] * 2

            def up(e_):
                g, u, x0 = e_ // 8, (e_ // 8) % 2, CAP * (e_ % 8)
                wi, b = bank()
                PE.wait(*t_xg[g])
                for h in range(4):
                    vw = lambda r, q: r.rearrange("p (k u n) -> p k u n", k=2, u=2)[:, :, q, :]
                    n, r, tok = piece(*[(lambda r, q=q: vw(r, q),
                                         I[nm][l, e_, 256 * h:256 * h + 256, :].rearrange("(k p) n -> p k n", p=P))
                                        for q, nm in enumerate(("e_w_gate", "e_w_up"))])
                    PE.wait(tok)
                    r4 = r.rearrange("p (k u n) -> p k u n", k=2, u=2)
                    for k in range(2):
                        kc = 2 * h + k
                        for c in range(2):
                            tk = mm(b[64 * c:64 * c + 64, :], xg[:, u, kc, x0:x0 + CAP], r4[:, k, :, 256 * c:256 * c + 256],
                                    kc == 0, kc == KC - 1, mark=(k == 1 and c == 1))
                    released[n] = tk
                if e_ % 8 == 7:
                    x_done[g] = tk
                i = e_ % 2
                ts = S.do(lambda e, b=b, i=i: e.activation(hd[:, i, :], b[:, 0:T], ACT.Silu), tk, hd_rd[i])
                hd_t[e_] = V.do(lambda e, b=b, i=i: e.tensor_tensor(hd[:, i, :], b[:, T:2 * T], hd[:, i, :], ALU.mult), ts)
                w_read[wi] = hd_t[e_]

            def turn(e_):
                i = e_ % 2
                wi, b = bank()
                PE.wait(hd_t[e_])
                for c in range(2):
                    tk = tr(b[:, c * P:(c + 1) * P], hd[:, i, c * P:(c + 1) * P], ident, mark=(c == 1))
                hd_rd[i] = tk
                he_t[e_] = V.do(lambda e, b=b, i=i: e.tensor_copy(he[:, i, :, :, :].rearrange("p c h s -> p (c h s)"), b[:, 0:T]), tk, he_rd[i])
                w_read[wi] = he_t[e_]
                if e_ % 2 == 0:
                    g, u, x0 = e_ // 8, (e_ // 8) % 2, CAP * (e_ % 8)
                    i = (e_ // 2) % 2
                    wi, b = bank()
                    PE.wait(t_C[g])
                    for t in range(2):
                        tk = tr(b[:, t * P:(t + 1) * P], Cg[:, u, t, x0:x0 + P], ident, mark=(t == 1))
                    if e_ % 8 == 6:
                        c_rd[u] = tk
                    ct_t[e_ // 2] = S.do(lambda e, b=b, i=i: e.copy(ct[:, i, :], b[:, 0:T]), tk, ct_rd[i])
                    w_read[wi] = ct_t[e_ // 2]

            def down(e_):
                i = e_ % 2
                wi, b = bank()
                PE.wait(he_t[e_])
                for h in range(2):
                    n, w, tok = block(I["e_w_down"][l, e_, 256 * h:256 * h + 256, :], 2, D)
                    PE.wait(tok)
                    for c in range(2):
                        for dh in range(2):
                            tk = mm(b[64 * dh:64 * dh + 64, :], he[:, i, c, h, :], w[:, c, 512 * dh:512 * dh + 512],
                                    h == 0 and c == 0, h == 1 and c == 1, mark=(c == 1 and dh == 1))
                    released[n] = tk
                he_rd[i] = tk
                pr = (e_ // 2) % 2
                p0 = 64 * i
                for dh in range(2):
                    Q, nm = (S, "copy") if e_ % 2 else (V, "tensor_copy")
                    o = ye[p0:p0 + 64, pr, dh, :]
                    src = b[64 * dh:64 * dh + 64, :]
                    if e_ % 2:
                        tv = S.do(lambda e, o=o, src=src: e.copy(o, src), tk, ye_rd[pr])
                    else:
                        tv = V.do(lambda e, o=o, src=src: e.tensor_copy(o, src), tk, ye_rd[pr])
                w_read[wi] = tv
                ye_t[e_] = tv

            def combine(p):
                i = p % 2
                PE.wait(ye_t[2 * p], ye_t[2 * p + 1], ct_t[p])
                for t in range(2):
                    for dh in range(2):
                        if p == 0:
                            PE.wait(y_read[2 * t + dh])
                        tk = mm(YB[2 * t + dh][:, :], ct[:, i, t * P:(t + 1) * P], ye[:, i, dh, :], p == 0, p == E // 2 - 1,
                                mark=(t == 1 and dh == 1))
                ye_rd[i] = ct_rd[i] = tk
                return tk

            choose(0)
            for kc in range(KC):
                gather(0, kc)
            choose(1)
            for e_ in range(E + 3):
                if e_ < E:
                    up(e_)
                if 1 <= e_ <= E:
                    down(e_ - 1)
                if e_ % 2 == 1 and e_ >= 3:
                    tk = combine((e_ - 3) // 2)
                if e_ < E:
                    turn(e_)
                    g = e_ // 8 + 1
                    if g < 4:
                        gather(g, e_ % 8)
                    if e_ % 8 == 7 and g + 1 < 4:
                        choose(g + 1)
            late(l, t_blk, Sg, Cg, xg, hd, he, ye, ct, sc)
            return tk

        def late(l, t_blk, Sg, Cg, xg, hd, he, ye, ct, sc):
            before = [(q.sem, q.n) for q in (PE, V, S, G)]
            pe, ve, ac = (Queue(x) for x in late_sems[:3])
            at = {}
            S1 = Sg[:, 0, :, 0:CAP]
            C1 = Cg[:, 0, :, 0:CAP]
            tmp1 = Cg[:, 1, 0, 0:CAP]
            x1 = xg[:, 0, :, 0:CAP]
            io = const[:, C_I5:C_I5 + CAP]
            sl = lambda t, j: slot_all[:, 2 * t + j:2 * t + j + 1]

            def loads(e):
                x = at[id(e)]
                n = 0
                for h in range(4):
                    dst = ring[:, h, :].rearrange("p (k u n) -> p k u n", k=2, u=2)
                    for q, nm in enumerate(("e_w_gate", "e_w_up")):
                        src = I[nm][l].rearrange("e (h k p) n -> p h e k n", h=4, p=P)[:, h, bass.ds(x, 1), :, :]
                        e.dma_start(dst[:, :, q, :], src[:, 0, :, :]).then_inc(late_dma, 16)
                for h in range(2):
                    dst = ring[:, 4 + h, :].rearrange("p (k n) -> p k n", k=2)
                    src = I["e_w_down"][l].rearrange("e (h k p) n -> p h e k n", h=2, p=P)[:, h, bass.ds(x, 1), :, :]
                    e.dma_start(dst, src[:, 0, :, :]).then_inc(late_dma, 16)
            t_w = (late_dma, 160)

            for t in range(2):
                tv = ve.do(lambda e, t=t: e.tensor_scalar(S1[:, t, :], io, sl(t, 0), None, ALU.is_equal))
                t_s = ve.do(lambda e, t=t: e.scalar_tensor_tensor(S1[:, t, :], io, sl(t, 1), S1[:, t, :], ALU.is_equal,
                                                                  ALU.add), tv)
            for t in range(2):
                ve.do(lambda e, t=t: e.tensor_scalar(C1[:, t, :], io, sl(t, 0), sc[:, t, 5:6], ALU.is_equal, ALU.mult))
                tv = ve.do(lambda e, t=t: e.tensor_scalar(tmp1, io, sl(t, 1), sc[:, t, 6:7], ALU.is_equal, ALU.mult),
                           (ve.sem, ve.n))
                t_c = ve.do(lambda e, t=t: e.tensor_tensor(C1[:, t, :], C1[:, t, :], tmp1, ALU.add), tv)
            b = WB[0]
            pe.wait(t_s)
            for kc in range(KC):
                for t in range(2):
                    tk = pe.do(lambda e, kc=kc, t=t: e.matmul(b[:, kc * CAP:(kc + 1) * CAP], vv[:, t, kc * P:(kc + 1) * P],
                                                              S1[:, t, :], start=(t == 0), stop=(t == 1)))
            for kc in range(KC):
                tv = ve.do(lambda e, kc=kc: e.tensor_scalar(x1[:, kc, :], b[:, kc * CAP:(kc + 1) * CAP], ab[:, 0, kc:kc + 1],
                                                            ab[:, 1, kc:kc + 1], ALU.mult, ALU.add), tk)
            b1 = WB[1]
            pe.wait(tv, t_w)
            for kc in range(KC):
                for c in range(2):
                    w = ring[:, kc // 2, :].rearrange("p (k u n) -> p k u n", k=2, u=2)[:, kc % 2, :, 256 * c:256 * c + 256]
                    tk = pe.do(lambda e, kc=kc, c=c, w=w: e.matmul(b1[64 * c:64 * c + 64, :], x1[:, kc, :], w,
                                                                   start=(kc == 0), stop=(kc == KC - 1)))
            ts = ac.do(lambda e: e.activation(hd[:, 0, :], b1[:, 0:T], ACT.Silu), tk)
            tv = ve.do(lambda e: e.tensor_tensor(hd[:, 0, :], b1[:, T:2 * T], hd[:, 0, :], ALU.mult), ts)
            b2 = WB[2]
            pe.wait(tv, t_c)
            for c in range(2):
                tk = pe.do(lambda e, c=c: e.transpose(b2[:, c * P:(c + 1) * P], hd[:, 0, c * P:(c + 1) * P], ident))
            for t in range(2):
                tk = pe.do(lambda e, t=t: e.transpose(b2[0:CAP, T + t * P:T + (t + 1) * P], C1[:, t, :], ident))
            ve.do(lambda e: e.tensor_copy(he[:, 0, :, :, :].rearrange("p c h s -> p (c h s)"), b2[:, 0:T]), tk)
            tv = ve.do(lambda e: e.tensor_copy(ct[0:CAP, 0, :], b2[0:CAP, T:2 * T]))
            b3 = WB[3]
            pe.wait(tv)
            for h in range(2):
                for c in range(2):
                    for dh in range(2):
                        w = ring[:, 4 + h, c * D + 512 * dh:c * D + 512 * dh + 512]
                        tk = pe.do(lambda e, h=h, c=c, dh=dh, w=w: e.matmul(
                            b3[64 * dh:64 * dh + 64, :], he[:, 0, c, h, :], w, start=(h == 0 and c == 0),
                            stop=(h == 1 and c == 1)))
            for dh in range(2):
                tv = ve.do(lambda e, dh=dh: e.tensor_copy(ye[0:64, 0, dh, :], b3[64 * dh:64 * dh + 64, :]), tk)
            pe.wait(tv)
            for t in range(2):
                for dh in range(2):
                    pe.do(lambda e, t=t, dh=dh: e.matmul(YB[2 * t + dh][:, :], ct[0:64, 0, t * P:(t + 1) * P],
                                                         ye[0:64, 0, dh, :], start=False, stop=True,
                                                         skip_group_check=True))

            def walk(q, who, body):
                def run(e):
                    e.wait_ge(*t_blk)
                    any_ = e.value_load(blk_n[0:1, 0:1], min_val=0, max_val=1)
                    with e.If(any_ != 0):
                        for tok in before:
                            e.wait_ge(*tok)
                        with e.Fori(0, 3) as r:
                            with e.Fori(0, E) as x:
                                if who == 1:
                                    e.tensor_scalar(slot_all[:, :], slot_all[:, :], -float(CAP), None,
                                                    ALU.add).then_inc(late_step, 1)
                                    e.wait_ge(late_step, 1)
                                    e.sem_clear(late_step)
                                here = e.value_load(blk_n[0:1, bass.ds(r * E + x + 1, 1)], min_val=0, max_val=1)
                                with e.If(here != 0):
                                    at[id(e)] = x
                                    body(e)
                                    if who is None:
                                        e.wait_ge(late_in, 4)
                                        for s_ in late_sems[:3] + [late_dma, late_in]:
                                            e.sem_clear(s_)
                                        for s_ in late_go:
                                            e.sem_inc(s_, 1)
                                    else:
                                        e.drain().then_inc(late_in, 1)
                                        e.wait_ge(late_go[who], 1)
                                        e.sem_clear(late_go[who])
                q.ops.append(run)

            walk(SP, None, loads)
            walk(PE, 0, pe.emit)
            walk(V, 1, ve.emit)
            walk(S, 2, ac.emit)
            walk(G, 3, lambda e: None)

        def ffn(win, wout, t_h):
            hid = area(0, 4, T)
            hrd = [None] * 4
            k = 0
            for j in range(11):
                ng, wg, tg_ = block(win[:, 256 * j:256 * j + 256], KC, 256)
                nu, wu, tu_ = block(win[:, DFF + 256 * j:DFF + 256 * j + 256], KC, 256)
                PE.wait(tg_, tu_, *t_h)
                th = []
                for q in range(2):
                    wi, b = bank()
                    proj(wg, q * P, b[:, 0:T])
                    tk = proj(wu, q * P, b[:, T:2 * T])
                    r = (2 * j + q) % 4
                    ts = S.do(lambda e, b=b, r=r: e.activation(hid[:, r, :], b[:, 0:T], ACT.Silu), tk, hrd[r])
                    tv = V.do(lambda e, b=b, r=r: e.tensor_tensor(hid[:, r, :], b[:, T:2 * T], hid[:, r, :], ALU.mult), ts)
                    w_read[wi] = tv
                    th.append(tv)
                released[ng] = released[nu] = tk
                n, w, tok = block(wout[256 * j:256 * j + 256, :], 2, D)
                PE.wait(tok)
                for q in range(2):
                    r = (2 * j + q) % 4
                    PE.wait(th[q])
                    for t in range(2):
                        for h in range(2):
                            if k == 0:
                                PE.wait(y_read[2 * t + h])
                            tk = mm(YB[2 * t + h][:, :], hid[:, r, t * P:(t + 1) * P], w[:, q, h * 512:(h + 1) * 512],
                                    k == 0, k == 21, mark=(t == 1 and h == 1))
                    hrd[r] = tk
                    k += 1
                released[n] = tk
            return tk

        def hybrid(l, t_h):
            W = I["w_in_2"][l]
            o = 0

            def take(*shape):
                nonlocal o
                a = area(o, *shape)
                o += int(np.prod(shape))
                return a

            qT = {"a": take(4, T), "b": take(4, T), "c": take(4, T), "i": take(4, T)}
            kT = {"a": take(4, T), "b": take(2, T), "c": take(1, T), "i": take(1, T)}
            va = take(2, 512)
            vb = take(2, 128)
            vc = take(2, 64)
            wi_ = take(2, 8)
            raw = take(2, T)
            rot = take(2, T)
            gates = hybrid_gates
            sm = take(4, 384)
            pt = take(2, 384)
            oT = {"a": take(4, T), "b": take(4, T), "c": take(4, T)}
            maskc = take(384)
            stt = take(2, 2, 4)
            raw_rd = [None] * 2
            rot_rd = [None] * 2
            cnt = [0]

            def rope(src, dst, scale, tk, wi, last):
                r = cnt[0] % 2
                cnt[0] += 1
                ta = S.do(lambda e, r=r: e.activation(raw[:, r, :], src, ACT.Copy, scale=scale), tk, raw_rd[r])
                if last:
                    w_read[wi] = ta
                wj, b = bank()
                PE.wait(ta)
                tp = mm(b[:, 0:T], perm, raw[:, r, :], True, True, mark=True)
                tg = G.do(lambda e, r=r: e.tensor_tensor(rot[:, r, :], raw[:, r, :], cos[:, :], ALU.mult), ta, t_rope, rot_rd[r])
                raw_rd[r] = [tg, tp]
                tv = V.do(lambda e, b=b: e.tensor_tensor(dst, b[:, 0:T], sin[:, :], ALU.mult), tp, t_rope)
                w_read[wj] = tv
                tv = V.do(lambda e, r=r: e.tensor_tensor(dst, dst, rot[:, r, :], ALU.add), tv, tg)
                rot_rd[r] = tv
                return tv

            pend = []

            def flush():
                for f in pend:
                    f()
                pend.clear()

            tok_of = {}

            def feat(c0, dst, key, scale):
                for j in range(2):
                    n, w, tok = block(W[:, c0 + 256 * j:c0 + 256 * j + 256], KC, 256)
                    PE.wait(tok, *t_h)
                    for q in range(2):
                        wi, b = bank()
                        tk = proj(w, q * P, b[:, 0:T])
                        f = 2 * j + q
                        flush()
                        pend.append(lambda b=b, f=f, tk=tk, wi=wi: tok_of.__setitem__(
                            key, rope(b[:, 0:T], dst[:, f, :], scale, tk, wi, True)))
                    released[n] = tk

            def dup(w, c0, dst, key):
                wi, b = bank()
                for hh in range(2):
                    tk = proj(w, c0, b[64 * hh:64 * hh + 64, 0:T], half=hh)
                flush()
                pend.append(lambda b=b, tk=tk, wi=wi: tok_of.__setitem__(key, rope(b[:, 0:T], dst, 1.0, tk, wi, True)))
                return tk

            def tokmajor(w, c0, n, dst):
                wi, b = bank()
                for t in range(2):
                    for kc in range(KC):
                        tk = mm(b[:, t * T:t * T + n], hT[:, kc, t * P:(t + 1) * P], w[:, kc, c0:c0 + n],
                                kc == 0, kc == KC - 1, mark=(kc == KC - 1))
                tv = V.do(lambda e, b=b: e.tensor_copy(dst, b[:, :].rearrange("p (t n) -> p t n", t=2)[:, :, 0:n]), tk)
                w_read[wi] = tv
                return tk, tv

            feat(2944, qT["i"], "qi", 1.0)
            n, w, tok = block(W[:, 3456:3528], KC, 72)
            PE.wait(tok)
            dup(w, 0, kT["i"][:, 0, :], "ki")
            tk, t_wi = tokmajor(w, 64, 8, wi_[:, :, :])
            released[n] = tk
            feat(2304, qT["c"], "qc", 0.125)
            n, w, tok = block(W[:, 2816:2944], KC, 128)
            PE.wait(tok)
            dup(w, 0, kT["c"][:, 0, :], "kc")
            tk, t_vc = tokmajor(w, 64, 64, vc[:, :, :])
            released[n] = tk

            srd = [None] * 4
            isc = sm[:, 3, :]
            flush()
            tacc = None
            for h in range(8):
                p = 64 * (h % 2)
                wi, b = bank()
                PE.wait(tok_of["qi"], tok_of["ki"])
                q = qT["i"][p:p + 64, h // 2, :]
                k = kT["i"][p:p + 64, 0, :]
                mm(b[:, 0:128], q[:, 0:128], k[:, 0:128], True, True)
                tk = mm(b[:, 128:384], q[:, 128:256], k[:, 0:256], True, True, mark=True)
                r = h % 2
                ts = S.do(lambda e, b=b, r=r: e.activation(sm[:, r, :], b[:, 0:384], ACT.Relu), tk, srd[r])
                w_read[wi] = ts
                for t, (a, z) in enumerate(((0, 128), (128, 384))):
                    if h == 0:
                        tv = V.do(lambda e, t=t, a=a, z=z, h=h, r=r: e.tensor_scalar(
                            isc[:, a:z], sm[:, r, a:z], wi_[:, t, h:h + 1], None, ALU.mult), ts, t_wi)
                    else:
                        tv = V.do(lambda e, t=t, a=a, z=z, h=h, r=r: e.scalar_tensor_tensor(
                            isc[:, a:z], sm[:, r, a:z], wi_[:, t, h:h + 1], isc[:, a:z], ALU.mult, ALU.add), ts, tacc)
                tacc = tv
                srd[r] = tv
            tv = V.do(lambda e: e.tensor_tensor(isc, isc, const[:, C_MC:C_MC + 384], ALU.add), tacc)
            top = small[:, 128:144].rearrange("p (t k) -> p t k", t=2)
            last = [tv, tv]
            for rnd in range(8):
                for t, (a, z) in enumerate(((0, 128), (128, 384))):
                    last[t] = V.do(lambda e, t=t, a=a, z=z: e.max(top[:, t, :], isc[:, a:z]), last[t])
                for t, (a, z) in enumerate(((0, 128), (128, 384))):
                    last[t] = V.do(lambda e, t=t, a=a, z=z: e.match_replace(isc[:, a:z], top[:, t, :], isc[:, a:z], GONE),
                                   last[t])
            tv = V.do(lambda e: e.tensor_scalar(maskc, isc, -2e38, NEG, ALU.is_gt, ALU.mult), last[1])
            t_mc = V.do(lambda e: e.tensor_tensor(maskc, maskc, const[:, C_MC:C_MC + 384], ALU.add), tv)

            hcount = [0]
            pt_rd = [None] * 2

            def heads(name, kidx, mask, t_mask, vsl, t_v, t_qk, sinks=None):
                t_o = []
                for j in range(4):
                    tkk, banks = [], []
                    for q in range(2):
                        h = 2 * j + q
                        p = 64 * q
                        wi, b = bank()
                        PE.wait(*t_qk)
                        qq = qT[name][p:p + 64, j, :]
                        kk = kT[name][p:p + 64, kidx(j), :]
                        mm(b[:, 0:128], qq[:, 0:128], kk[:, 0:128], True, True)
                        tkk.append(mm(b[:, 128:384], qq[:, 128:256], kk[:, 0:256], True, True, mark=True))
                        banks.append((wi, b))
                    u = hcount[0] % 2
                    hcount[0] += 1
                    mx, dn = stt[:, u, 0, :], stt[:, u, 1, :]
                    for q in range(2):
                        wi, b = banks[q]
                        r = 2 * u + q if False else q
                        for t, (a, z) in enumerate(((0, 128), (128, 384))):
                            tv = V.do(lambda e, a=a, z=z, q=q, t=t, b=b, mx=mx: e.tensor_tensor_reduce(
                                sm[:, q, a:z], b[:, a:z], mask[:, a:z], 1.0, GONE, ALU.add, ALU.max,
                                mx[:, 2 * q + t:2 * q + t + 1]), tkk[q], t_mask, srd[q])
                        w_read[wi] = tv
                    nmx = small[:, 160 + 4 * u:164 + 4 * u]
                    if sinks is None:
                        tv = V.do(lambda e, mx=mx, nmx=nmx: e.tensor_scalar(nmx, mx, -1.0, None, ALU.mult), tv)
                    else:
                        sk = sinks(j)
                        tv = V.do(lambda e, mx=mx, sk=sk: e.tensor_tensor(mx, mx, sk, ALU.max), tv, t_sink)
                        tv = V.do(lambda e, mx=mx, nmx=nmx: e.tensor_scalar(nmx, mx, -1.0, None, ALU.mult), tv)
                    for q in range(2):
                        for t, (a, z) in enumerate(((0, 128), (128, 384))):
                            i = 2 * q + t
                            ts = S.do(lambda e, a=a, z=z, q=q, i=i, nmx=nmx, dn=dn: e.activation(
                                sm[:, q, a:z], sm[:, q, a:z], ACT.Exp, bias=nmx[:, i:i + 1], accum_out=dn[:, i:i + 1]), tv)
                    if sinks is not None:
                        tmp4 = small[:, 176 + 4 * u:180 + 4 * u]
                        tv = V.do(lambda e, nmx=nmx, tmp4=tmp4, sk=sk: e.tensor_tensor(tmp4, nmx, sk, ALU.add), tv)
                        te = S.do(lambda e, tmp4=tmp4: e.activation(tmp4, tmp4, ACT.Exp), tv)
                        ts = V.do(lambda e, dn=dn, tmp4=tmp4: e.tensor_tensor(dn, dn, tmp4, ALU.add), te, ts)
                    rd = small[:, 192 + 4 * u:196 + 4 * u]
                    tv = V.do(lambda e, rd=rd, dn=dn: e.reciprocal(rd, dn), ts)
                    tn = []
                    for q in range(2):
                        for t, (a, z) in enumerate(((0, 128), (128, 384))):
                            i = 2 * q + t
                            tg = G.do(lambda e, a=a, z=z, q=q, i=i, rd=rd: e.tensor_scalar(
                                sm[:, q, a:z], sm[:, q, a:z], rd[:, i:i + 1], None, ALU.mult), tv, ts)
                        tn.append(tg)
                    wo, bo = bank()
                    for q in range(2):
                        wi, b = bank()
                        PE.wait(tn[q])
                        tr(b[:, 0:128], sm[:, q, 0:128], ident)
                        tr(b[:, 128:256], sm[:, q, 128:256], ident)
                        tk = tr(b[:, 256:384], sm[:, q, 256:384], ident, mark=True)
                        srd[q] = tk
                        tc = S.do(lambda e, q=q, b=b: e.copy(pt[:, q, :], b[:, 0:384]), tk, pt_rd[q])
                        w_read[wi] = tc
                        PE.wait(tc, t_v)
                        h = 2 * j + q
                        mm(bo[64 * q:64 * q + 64, 0:256], vsl(h, 0), pt[:, q, 0:256], True, False)
                        tk = mm(bo[64 * q:64 * q + 64, 128:256], vsl(h, 1), pt[:, q, 256:384], False, True, mark=True)
                        pt_rd[q] = tk
                    tv = V.do(lambda e, j=j, bo=bo: e.tensor_copy(oT[name][:, j, :], bo[:, 0:256]), tk)
                    w_read[wo] = tv
                return tv

            to = {}
            to["c"] = heads("c", lambda j: 0, maskc, t_mc, lambda h, s: vc[:, s, :], t_vc, (tok_of["qc"], tok_of["kc"]))
            feat(1536, qT["b"], "qb", 0.125)
            n, w, tok = block(W[:, 2048:2304], KC, 256)
            PE.wait(tok)
            dup(w, 0, kT["b"][:, 0, :], "kb0")
            dup(w, 64, kT["b"][:, 1, :], "kb1")
            tk, t_vb = tokmajor(w, 128, 128, vb[:, :, :])
            released[n] = tk
            flush()
            sk = lambda j: sink[:, l, 2 * j:2 * j + 2, :].rearrange("p h t -> p (h t)")
            to["b"] = heads("b", lambda j: j // 2, const[:, C_MB:C_MB + 384], t_const,
                            lambda h, s: vb[:, s, 64 * (h // 4):64 * (h // 4) + 64], t_vb,
                            (tok_of["qb"], tok_of["kb0"], tok_of["kb1"]), sk)
            feat(0, qT["a"], "qa", 0.125)
            feat(512, kT["a"], "ka", 1.0)
            for j in range(2):
                n, w, tok = block(W[:, 1024 + 256 * j:1280 + 256 * j], KC, 256)
                PE.wait(tok)
                tk, t_va = tokmajor(w, 0, 256, va[:, :, 256 * j:256 * j + 256])
                released[n] = tk
            flush()
            to["a"] = heads("a", lambda j: j, const[:, C_MA:C_MA + 384], t_const,
                            lambda h, s: va[:, s, 64 * h:64 * h + 64], t_va, (tok_of["qa"], tok_of["ka"]))

            tgt = {}
            for bi, nm in enumerate("abc"):
                for j in range(4):
                    c0 = 3528 + D * bi + 256 * j
                    n, w, tok = block(W[:, c0:c0 + 256], KC, 256)
                    PE.wait(tok)
                    for q in range(2):
                        f = 2 * j + q
                        wi, b = bank()
                        tk = proj(w, q * P, b[:, 0:T])
                        ts = S.do(lambda e, b=b, bi=bi, f=f: e.activation(gates[:, bi, f, :], b[:, 0:T], ACT.Sigmoid), tk)
                        w_read[wi] = ts
                        tgt[(nm, f)] = ts
                    released[n] = tk
            mT = area(0, KC, T)
            tz = []
            for nh in range(2):
                ws = [block(I[f"w_br_{nm}_2"][l, :, 512 * nh:512 * nh + 512], 4, 512) for nm in "abc"]
                PE.wait(*[w[2] for w in ws], *to.values())
                for fq in range(4):
                    f = 4 * nh + fq
                    wi, b = bank()
                    wj, b2 = bank()
                    dsts = {"a": b[:, 0:T], "b": b[:, T:2 * T], "c": b2[:, 0:T]}
                    for bi, nm in enumerate("abc"):
                        for k in range(4):
                            tk = mm(dsts[nm], ws[bi][1][:, k, fq * P:(fq + 1) * P], oT[nm][:, k, :], k == 0, k == 3,
                                    mark=(k == 3))
                    for bi, nm in enumerate("abc"):
                        tv = V.do(lambda e, bi=bi, f=f, s=dsts[nm]: e.tensor_tensor(gates[:, bi, f, :], s, gates[:, bi, f, :], ALU.mult),
                                  tk, tgt[(nm, f)])
                    w_read[wi] = w_read[wj] = tv
                    tv = G.do(lambda e, f=f: e.tensor_tensor(mT[:, f, :], gates[:, 0, f, :], gates[:, 1, f, :], ALU.add), tv)
                    tz.append(G.do(lambda e, f=f: e.tensor_tensor(mT[:, f, :], mT[:, f, :], gates[:, 2, f, :], ALU.add), tv))
                for w in ws:
                    released[w[0]] = tk
            return out_rows([I["w_out_2"][l, 256 * j:256 * j + 256, :] for j in range(4)], lambda k: mT[:, k, :], tz)

        hybrid_gates = area(14400, 3, KC, T)

        tf = fold(None, None, 0, SCM, SHM, t_mod[0])
        t_h = to_feature(xa, [t_x, t_x], tf, None)
        t_xa0 = S.do(lambda e: e.activation(xa[:, :, :], xa[:, :, :], ACT.Copy, scale=ALPHA), (PE.sem, PE.n))
        xa_tok[0] = t_xa0
        for l in range(DEPTH):
            tg = spread(l, 1, 0)
            t_ln = load_ln(I["mix_ln_g"][l:l + 1, :], I["mix_ln_b"][l:l + 1, :])
            ty = mixer_a(t_h) if l == 0 else mixer_b(t_h)
            tx = layer_norm(ty, tg, t_ln)
            tf = fold(colr("mix_ln_g", 8 * l, 8), colr("mix_ln_b", 8 * l, 8), l, SCF, SHF, t_mod[l], *t_h)
            t_h = to_feature(vv, tx, tf, ty)
            tg = spread(l, 2, 2)
            t_ln = load_ln(I["ffn_ln_g"][l:l + 1, :], I["ffn_ln_b"][l:l + 1, :])
            ty = moe(l, t_h)
            tx = layer_norm(ty, tg, t_ln)
            g_, b_ = colr("ffn_ln_g", 8 * l, 8), colr("ffn_ln_b", 8 * l, 8)
            if l == 0:
                tf = fold(g_, b_, 1, SCM, SHM, t_mod[1], *t_h)
            else:
                tf = fold(g_, b_, None, None, None, *t_h)
            t_h = to_feature(vv, tx, tf, ty)
        for l in range(DEPTH):
            for j in range(3):
                t_ln = load_ln(I["ln_g_2"][l, j:j + 1, :], I["ln_b_2"][l, j:j + 1, :])
                if j == 0:
                    ty = ffn(I["ffn1_in_2"][l], I["ffn1_out_2"][l], t_h)
                elif j == 1:
                    ty = hybrid(l, t_h)
                else:
                    ty = ffn(I["ffn2_in_2"][l], I["ffn2_out_2"][l], t_h)
                last = l == DEPTH - 1 and j == 2
                tx = layer_norm(ty, 1.0 if j == 1 else 0.5, t_ln, last)
                if not last:
                    i = 8 * (3 * l + j)
                    tf = fold(colr("ln_g_2", i, 8), colr("ln_b_2", i, 8), None, None, None, *t_h)
                    t_h = to_feature(vv, tx, tf, ty)
        t_out = SP.dma(out[0].rearrange("(t p) d -> p t d", p=P), xa[:, :, :], s_o, xa_tok[0])
        SP.wait(t_out)

        blk = ctx.enter_context(nc.Block())

        @blk.sync
        def _(e):
            SP.emit(e)

        @blk.tensor
        def _(e):
            PE.emit(e)

        @blk.vector
        def _(e):
            V.emit(e)

        @blk.scalar
        def _(e):
            S.emit(e)

        @blk.gpsimd
        def _(e):
            G.emit(e)


_INS = ["x", "c", "ada_w", "ada_b", "a_w_in", "a_b_in", "a_w_dw", "a_b_dw", "a_ln_g", "a_ln_b", "a_w_out", "a_b_out",
        "b_w_in", "b_w_dw", "b_w_out", "mix_ln_g", "mix_ln_b", "ffn_ln_g", "ffn_ln_b", "r_w_group", "r_b_group",
        "r_w_expert", "r_b_expert", "e_w_gate", "e_w_up", "e_w_down", "positions_2", "w_in_2", "sink_b_2", "w_br_a_2",
        "w_br_b_2", "w_br_c_2", "w_out_2", "ffn1_in_2", "ffn1_out_2", "ffn2_in_2", "ffn2_out_2", "ln_g_2", "ln_b_2"]


def kernel(**inputs):
    import numpy as _np
    import concourse.bacc as _bacc
    from concourse import mybir as _mybir
    from concourse.bass_utils import run_bass_kernel_spmd as _run

    nc = _bacc.Bacc("TRN2", target_bir_lowering=False, num_devices=1)
    arrays, aps = {}, {}
    for name in _INS:
        a = _np.ascontiguousarray(inputs[name])
        arrays[f"in_{name}_dram"] = a
        aps[name] = nc.dram_tensor(f"in_{name}_dram", a.shape, _mybir.dt.from_np(a.dtype), kind="ExternalInput").ap()
    c = constants()
    arrays["in_consts_dram"] = c
    aps["consts"] = nc.dram_tensor("in_consts_dram", c.shape, _mybir.dt.float32, kind="ExternalInput").ap()
    o = nc.dram_tensor("out_0_dram", (1, T, D), _mybir.dt.float32, kind="ExternalOutput").ap()
    program(nc, aps, o)
    r = _run(nc, [arrays], core_ids=[0])
    return r.results[0]["out_0_dram"]
```

```python
from contextlib import ExitStack

import numpy as np
import concourse.bass as bass
from concourse import mybir

F32 = mybir.dt.float32
F32R = mybir.dt.float32r
U32 = mybir.dt.uint32
I32 = mybir.dt.int32
ALU = mybir.AluOpType
ACT = mybir.ActivationFunctionType
AX = mybir.AxisListType.X

P = 128
T = 256
D = 1024
KC = 8
E = 32
F = 512
DFF = 2816
DEPTH = 2
ALPHA = (2.0 * DEPTH) ** 0.25
EPS = 1e-5
NEG = -1e30
GONE = -3e38
CW = 31
SLOT = 2048
NSLOT = 6
AREA = 13312
UNITS = 3
AHEAD = 2

C_ID, C_PERM, C_MA, C_MB, C_MC, C_IO, C_IG, C_INV, C_TRI, C_I5 = 0, 128, 256, 640, 1024, 1408, 1440, 1472, 1473, 1601
NCONST = 2113
CAP = 64

TWO_PI = 2.0 * np.pi


def split_const(value, parts, bits):
    out, rest = [], float(value)
    for _ in range(parts - 1):
        e = np.floor(np.log2(abs(rest))) + 1
        q = 2.0 ** (e - bits)
        c = np.floor(rest / q) * q
        out.append(float(c))
        rest -= c
    return out + [float(np.float32(rest))]


def constants():
    c = np.zeros((P, NCONST), np.float32)
    c[:, C_ID:C_ID + P] = np.eye(P)
    for i in range(P):
        if i % 64 < 32:
            c[i + 32, C_PERM + i] = -1.0
        else:
            c[i - 32, C_PERM + i] = 1.0
    t = np.arange(T)[:, None]
    s = np.arange(T)[None, :]
    d = t - s
    causal = d >= 0
    many = (causal & (d <= 128)).astype(np.float64) + (causal & (d % 4 == 0)) + (causal & (d % 16 == 0))
    ma = np.where(many > 0, np.log(np.maximum(many, 1)), NEG)
    mb = np.where(causal & (d <= 127), 0.0, NEG)
    mc = np.where(causal, 0.0, NEG)
    for off, m in ((C_MA, ma), (C_MB, mb), (C_MC, mc)):
        c[:, off:off + 128] = m[:128, :128]
        c[:, off + 128:off + 384] = m[128:, :]
    c[:, C_IO:C_IO + 32] = np.arange(32)[None, :]
    c[:, C_IG:C_IG + 32] = (np.arange(32) // 8)[None, :]
    inv = np.float32(10000.0) ** (-np.arange(0, 64, 2).astype(np.float32) / np.float32(64))
    c[:, C_INV] = np.tile(inv.astype(np.float32), 4)
    c[:, C_TRI:C_TRI + P] = np.triu(np.ones((P, P)), 1)
    c[:, C_I5:C_I5 + 512] = np.arange(512)[None, :]
    return c


class Queue:

    def __init__(self, sem):
        self.sem, self.n, self.ops, self.seen = sem, 0, [], {}

    def wait(self, *tokens):
        for tok in tokens:
            if tok is None:
                continue
            if isinstance(tok, list):
                self.wait(*tok)
                continue
            sem, v = tok
            if self.seen.get(id(sem), 0) < v:
                self.seen[id(sem)] = v
                self.ops.append(lambda e, sem=sem, v=v: e.wait_ge(sem, v))

    def do(self, fn, *waits, mark=True):
        self.wait(*waits)
        if not mark:
            self.ops.append(fn)
            return None
        self.n += 1
        self.ops.append(lambda e, fn=fn: fn(e).then_inc(self.sem, 1))
        return (self.sem, self.n)

    def dma(self, out, in_, sem, *waits):
        self.wait(*waits)
        self.ops.append(lambda e: e.dma_start(out, in_).then_inc(sem[0], 16))
        sem[1] += 16
        return (sem[0], sem[1])

    def emit(self, e):
        for op in self.ops:
            op(e)


def program(nc, I, out):
    with ExitStack() as ctx:
        kept = {}

        def keep(name, make):
            if name not in kept:
                kept[name] = ctx.enter_context(make())
            return kept[name]

        order = []
        fences = []
        script(nc, I, out, keep, order, fences, True)
        queues = script(nc, I, out, keep, order, fences, False)
        blk = ctx.enter_context(nc.Block())
        for on, q in zip((blk.sync, blk.tensor, blk.vector, blk.scalar, blk.gpsimd), queues):
            on(lambda e, q=q: q.emit(e))


def script(nc, I, out, keep, order, keep_fences, learning):
    if True:
        sb = lambda name, shape, dt=F32: keep(name, lambda: nc.sbuf_tensor(name, shape, dt))
        sem = lambda name: keep("sem_" + name, lambda: nc.semaphore(name))
        dsem = lambda name: [sem(name), 0]

        PE, V, S, G, SP = (Queue(sem(n)) for n in ("pe", "ve", "ac", "po", "sy"))

        const = sb("const", [P, NCONST])
        ident = const[:, C_ID:C_ID + P]
        perm = const[:, C_PERM:C_PERM + P]
        ones = sb("ones", [P, P])
        ring = sb("ring", [P, NSLOT, SLOT])
        ring_sem = [dsem(f"r{i}") for i in range(NSLOT)]
        xa = sb("xa", [P, 2, D])
        vv = sb("vv", [P, 2, D])
        hh = sb("hh", [P, KC, T], F32R)
        hl = sb("hl", [P, KC, T], F32R)
        ht = sb("ht", [P, 4, 2, T])
        wsp = sb("wsp", [P, UNITS, 2, 1024], F32R)
        zsp = sb("zsp", [P, 4, 2, T], F32R)
        grow = sb("grow", [P, 2, 512])
        cols = sb("cols", [P, 5, P])
        mcol = sb("mcol", [P, 2, 48])
        ab = sb("ab", [P, 4, KC])
        gb = sb("gb", [P, D])
        lnp = sb("lnp", [P, 2, D])
        cos = sb("cos", [P, T])
        sin = sb("sin", [P, T])
        small = sb("small", [P, 512])
        arena = sb("arena", [P, AREA])

        YB = [keep(f"y{i}", lambda i=i: nc.psum_tensor(f"y{i}", [P, 512], F32)) for i in range(4)]
        WB = [keep(f"w{i}", lambda i=i: nc.psum_tensor(f"w{i}", [P, 512], F32)) for i in range(4)]
        y_read = [None] * 4
        w_read = [None] * 4
        w_next = [0]

        def bank():
            i = w_next[0] % 4
            w_next[0] += 1
            PE.wait(w_read[i])
            return i, WB[i]

        def area(off, *shape):
            n = int(np.prod(shape))
            assert off + n <= AREA, (off, shape)
            a = arena[:, off:off + n]
            if len(shape) == 1:
                return a
            names = "abcd"[:len(shape)]
            return a.rearrange(f"p ({' '.join(names)}) -> p {' '.join(names)}",
                               **{k: s for k, s in zip(names, shape)})

        released = []
        ln_plan = []

        def piece(*parts):
            n = len(released)
            if ln_plan and n >= ln_plan[0]:
                load = ln_plan[1]
                ln_plan.clear()
                load()
            s = n % NSLOT
            released.append(None)
            if n >= NSLOT:
                assert released[n - NSLOT] is not None, n
                SP.wait(released[n - NSLOT])
            for view, src in parts:
                tok = SP.dma(view(ring[:, s, :]), src, ring_sem[s])
            return n, ring[:, s, :], tok

        def block(src, k, n):
            view = lambda r: r[:, 0:k * n].rearrange("p (k n) -> p k n", k=k)
            i, r, tok = piece((view, src.rearrange("(k p) n -> p k n", p=P)))
            return i, view(r), tok

        unit_pe = [None] * UNITS
        unit_at = [0]
        low_by = [V]
        beside = ([], 5), ([], 12)
        unit_made = []
        unit_piece = {}
        fences = keep_fences

        def make_unit(i):
            key, src, k, n, cut, shape, last = order[i]
            if key not in unit_piece:
                unit_piece[key] = block(src, k, n) + ([],)
            ni, w, tok, readers = unit_piece[key]
            s = i % UNITS
            m = int(np.prod(shape))
            names = "abcd"[:len(shape)]
            vw = lambda j: wsp[:, s, j, 0:m].rearrange(f"p ({' '.join(names)}) -> p {' '.join(names)}",
                                                       **{c: z for c, z in zip(names, shape)})
            src_ = cut(w)
            th = S.do(lambda e: e.copy(vw(0), src_), tok, unit_pe[s])
            tl = low_by[0].do(lambda e: e.tensor_tensor(vw(1), src_, vw(0).bitcast(F32), ALU.subtract), th, unit_pe[s])
            readers += [th, tl]
            for todo, rate in beside:
                for _ in range(rate):
                    if todo:
                        todo.pop(0)()
            if last:
                released[ni] = readers
            flat = lambda j: wsp[:, s, j, 0:m]
            unit_made.append((flat(0), flat(1), tl, s))

        def unit(key, src, k, n, cut, shape, last, ahead=AHEAD, hold=False):
            if learning:
                order.append((key, src, k, n, cut, shape, last))
            i = unit_at[0]
            unit_at[0] += 1
            assert order[i][0] == key
            stop = min([f for f in fences if f > i] + [len(order)])
            while len(unit_made) < min(i + 1 + ahead, stop):
                make_unit(len(unit_made))
            wh, wl, tok, s = unit_made[i]
            if hold:
                return wh, wl, s, tok
            PE.wait(tok)
            return wh, wl, s

        def top_up():
            stop = min([f for f in fences if f > unit_at[0]] + [len(order)])
            while not learning and len(unit_made) < min(unit_at[0] + UNITS, stop):
                make_unit(len(unit_made))

        def prime():
            stop = min([f for f in fences if f > unit_at[0]] + [len(order)])
            for low in (V, G):
                if len(unit_made) < stop and not learning:
                    low_by[0] = low
                    make_unit(len(unit_made))
            low_by[0] = V

        def done(s, tok):
            unit_pe[s] = tok

        def mm(o, l, r, start, stop, mark=False, **kw):
            return PE.do(lambda e: e.matmul(o, l, r, start=start, stop=stop, **kw), mark=mark)

        def tr(o, i, idn, mark=False):
            return PE.do(lambda e: e.transpose(o, i, idn), mark=mark)

        t_ones = G.do(lambda e: e.memset(ones[:, :], 1.0))
        nhalf = small[:, 0:1]
        t_nh = G.do(lambda e: e.memset(nhalf, -0.5))

        vrows = area(5000, 5, P)
        s_c = dsem("s_c")
        t_const = SP.dma(const[:, :], I["consts"], s_c)
        s_v = [dsem(f"s_v{i}") for i in range(5)]
        rows = {}

        def put(tile, at, name, ap, n):
            rows[name] = tile * P + at
            return (G if tile else SP).dma(vrows[at:at + n, tile, :], ap, s_v[tile])

        vec = lambda a: a.rearrange("r (c k) -> (r c) k", k=P)
        t0 = put(0, 0, "c", vec(I["c"]), 8)
        t0 = put(0, 8, "a_b_in", vec(I["a_b_in"]), 16)
        t0 = put(0, 24, "a_b_dw", vec(I["a_b_dw"]), 8)
        t0 = put(0, 32, "a_ln_g", vec(I["a_ln_g"]), 8)
        t0 = put(0, 40, "a_ln_b", vec(I["a_ln_b"]), 8)
        t0 = put(0, 48, "b_w_dw", vec(I["b_w_dw"][0]), 24)
        nv = [72, 64, 96, 124, 124]
        for j, nm in enumerate(("mix_ln_g", "mix_ln_b", "ffn_ln_g", "ffn_ln_b")):
            t1 = put(1, 16 * j, nm, vec(I[nm]), 16)
        for j, nm in enumerate(("ln_g_2", "ln_b_2")):
            t2 = put(2, 48 * j, nm, vec(I[nm].rearrange("l j d -> (l j) d")), 48)
        wdw = I["a_w_dw"][0].rearrange("r (c k) -> (r c) k", k=P)
        t3 = G.dma(vrows[0:124, 3, :], wdw[0:124, :], s_v[3])
        t4 = G.dma(vrows[0:124, 4, :], wdw[124:248, :], s_v[4])
        s_x = dsem("s_x")
        bias = area(9472, 2, 3, 512)
        mrow = area(12544, 512)
        s_ab = dsem("s_ab")
        t_ab = [None]
        bout = area(8448, D)[0:1, :]
        rb = sb("rb", [1, 2, 36])
        wr = sb("wr", [P, 2, KC, 36])
        cnt = sb("cnt", [P, E])
        blk_n = sb("blk_n", [P, 97], I32)
        slot_all = sb("slot_all", [P, 4])
        most = small[:, 208:209]
        late_sems = [sem(f"late{i}") for i in range(4)]
        late_dma, late_in, late_step = sem("late_dma"), sem("late_in"), sem("late_step")
        late_go = [sem(f"late_go{i}") for i in range(4)]
        sink = sb("sink", [P, 2, 8, 2])
        sinkr = sb("sinkr", [P, 16])
        s_m = dsem("s_m")
        G.dma(bout, I["a_b_out"], s_m)
        for l in range(2):
            G.dma(rb[:, l, 0:4], I["r_b_group"][l:l + 1, :], s_m)
            G.dma(rb[:, l, 4:36], I["r_b_expert"][l:l + 1, :], s_m)
            G.dma(wr[:, l, :, 0:4], I["r_w_group"][l].rearrange("(k p) n -> p k n", p=P), s_m)
            G.dma(wr[:, l, :, 4:36], I["r_w_expert"][l].rearrange("(k p) n -> p k n", p=P), s_m)
        t_m = G.dma(sinkr[:, :], I["sink_b_2"].rearrange("l h -> (l h)").unsqueeze(0).to_broadcast([P, 16]), s_m)
        posi = area(8192, T).bitcast(I32)
        s_p = dsem("s_p")
        t_p = G.dma(posi, I["positions_2"].to_broadcast([P, T]), s_p)

        PE.wait(t_const, t_ones, t0)
        wi, b = bank()
        tk = tr(b[:, 0:nv[0]], vrows[0:nv[0], 0, :], const[0:nv[0], 0:nv[0]], mark=True)
        t_col0 = V.do(lambda e, b=b: e.tensor_copy(cols[:, 0, 0:nv[0]], b[:, 0:nv[0]]), tk)
        w_read[wi] = t_col0

        def other_cols():
            wi, b = bank()
            PE.wait(t1, t2, t3, t4)
            for j in range(1, 5):
                tk = tr(b[:, (j - 1) * P:(j - 1) * P + nv[j]], vrows[0:nv[j], j, :], const[0:nv[j], 0:nv[j]], mark=(j == 4))
            for j in range(1, 5):
                tv = V.do(lambda e, j=j: e.tensor_copy(cols[:, j, 0:nv[j]], b[:, (j - 1) * P:(j - 1) * P + nv[j]]), tk)
            w_read[wi] = tv

        flat = cols[:, :, :].rearrange("p a b -> p (a b)")
        col = lambda name, i: flat[:, rows[name] + i:rows[name] + i + 1]
        colr = lambda name, i, n: flat[:, rows[name] + i:rows[name] + i + n]

        def dw(j, f):
            r = j * 8 + f
            return cols[:, 3 + r // 124, r % 124:r % 124 + 1]

        cact = area(13056, KC, 32)
        ca = small[:, 8:16]
        ta = S.do(lambda e: e.activation(ca, colr("c", 0, 8), ACT.Silu), t_col0)
        t_ca = [V.do(lambda e: e.tensor_copy(cact, ca.unsqueeze(2).to_broadcast([P, KC, 32])), ta)]

        t_x = S.dma(xa[:, :, :], I["x"][0].rearrange("(t p) d -> p t d", p=P), s_x)
        for l in range(2):
            for g in range(4):
                src = I["ada_b"][l:l + 1, :].rearrange("o (c g n) -> o g c n", c=3, g=4)[:, g, :, :]
                t_ab[0] = S.dma(bias[32 * g:32 * g + 32, l, :, :], src.to_broadcast([32, 3, 512]), s_ab)
        mod_done = {}
        jobs = []

        def ada(l, cb):
            b = YB[0]
            for kc in range(KC):
                n, w, tok = piece((lambda r: r, I["ada_w"][l, kc * P:(kc + 1) * P, cb * 2048:(cb + 1) * 2048]))
                PE.wait(tok, t_ca[0])
                if kc == 0:
                    PE.wait(y_read[0])
                for g in range(4):
                    tk = mm(b[32 * g:32 * g + 32, :], cact[:, kc, :], w[:, g * 512:(g + 1) * 512],
                            kc == 0, kc == KC - 1, mark=(g == 3))
                released[n] = tk
                if kc < KC - 1:
                    yield
            tv = V.do(lambda e, b=b: e.tensor_tensor(mrow, b[:, :], bias[:, l, cb, :], ALU.add), tk, t_ab[0],
                      mod_done.get("turned"))
            y_read[0] = tv
            if cb == 1:
                mod_done[("row", l, 0)] = V.do(lambda e: e.tensor_copy(grow[0:64, l, :], mrow[0:64, :]), tv)
            if cb == 2:
                mod_done[("row", l, 1)] = V.do(lambda e: e.tensor_copy(grow[64:128, l, :], mrow[64:128, :]), tv)
            wi, b = bank()
            PE.wait(tv)
            for j in range(4):
                tk = tr(b[:, j * P:(j + 1) * P], mrow[:, j * P:(j + 1) * P], ident, mark=(j == 3))
            mod_done["turned"] = tk
            src = b[:, :].rearrange("p (j g r) -> p j g r", j=4, g=4)[:, :, :, 0]
            dst = mcol[:, l, cb * 16:(cb + 1) * 16].rearrange("p (g j) -> p j g", g=4)
            tv = V.do(lambda e, s=src, d=dst: e.tensor_copy(d, s), tk)
            w_read[wi] = tv
            mod_done[(l, cb)] = tv

        def ada_steps(n):
            while n and jobs:
                n -= 1
                try:
                    next(jobs[0])
                except StopIteration:
                    jobs.pop(0)

        def ada_inputs():
            for g in range(4):
                src = I["ada_b"][1:2, :].rearrange("o (c g n) -> o g c n", c=3, g=4)[:, g, :, :]
                t_ab[0] = S.dma(bias[32 * g:32 * g + 32, 1, :, :], src.to_broadcast([32, 3, 512]), s_ab,
                                *[(q.sem, q.n) for q in (PE, V, S, G)])
            t_ca[0] = V.do(lambda e: e.tensor_copy(cact, ca.unsqueeze(2).to_broadcast([P, KC, 32])),
                           *[(q.sem, q.n) for q in (PE, V, S, G)])

        def spread(l, which, *waits):
            PE.wait(mod_done[("row", l, which)])
            for h in range(2):
                wi, b = bank()
                p = 64 * which + 32 * h
                tk = mm(b[:, :], ones[p:p + 1, :], grow[p:p + 1, l, :], True, True, mark=True)
                tv = V.do(lambda e, b=b, h=h: e.tensor_scalar(gb[:, h * 512:(h + 1) * 512], b[:, :], 1.0, None, ALU.add), tk)
                w_read[wi] = tv
            return tv

        SHM, SCM, GM, SHF, SCF, GF = range(6)
        mvec = lambda l, w: mcol[:, l, 8 * w:8 * w + 8]

        def fold(gcol, bcol, l, sc, sh, *waits):
            if sc is None:
                V.do(lambda e: e.tensor_copy(ab[:, 0, :], gcol), *waits)
                return V.do(lambda e: e.tensor_copy(ab[:, 1, :], bcol))
            t = V.do(lambda e: e.tensor_scalar(ab[:, 2, :], mvec(l, sc), 1.0, None, ALU.add), *waits)
            if gcol is None:
                V.do(lambda e: e.tensor_copy(ab[:, 0, :], ab[:, 2, :]), t)
                return V.do(lambda e: e.tensor_copy(ab[:, 1, :], mvec(l, sh)))
            V.do(lambda e: e.tensor_tensor(ab[:, 0, :], ab[:, 2, :], gcol, ALU.mult), t)
            t = V.do(lambda e: e.tensor_tensor(ab[:, 3, :], ab[:, 2, :], bcol, ALU.mult))
            return V.do(lambda e: e.tensor_tensor(ab[:, 1, :], ab[:, 3, :], mvec(l, sh), ALU.add), t)

        ht_rd = [None] * 4

        def to_feature(src, t_src, t_ab, t_free):
            toks = []
            banks = [bank() for _ in range(4)]
            ends = []
            for t in range(2):
                PE.wait(t_src[t])
                for f in range(KC):
                    tk = tr(banks[f // 2][1][:, f % 2 * T + t * P:f % 2 * T + (t + 1) * P], src[:, t, f * P:(f + 1) * P],
                            ident, mark=(t == 1 and f % 2 == 1))
                    if t == 1 and f % 2:
                        ends.append(tk)
            half, th, tl = [None] * 4, [None] * 4, [None] * 4

            def affine(u):
                (wi, b), tk = banks[u], ends[u]
                for q in range(2):
                    o = ht[:, u, q, :]
                    i = b[:, q * T:(q + 1) * T]
                    f = 2 * u + q
                    if u % 2 == 0:
                        half[u] = V.do(lambda e, i=i, o=o, f=f: e.tensor_scalar(o, i, ab[:, 0, f:f + 1], ab[:, 1, f:f + 1],
                                                                                ALU.mult, ALU.add), tk, t_ab, ht_rd[u])
                    else:
                        half[u] = S.do(lambda e, i=i, o=o, f=f: e.activation(o, i, ACT.Identity, bias=ab[:, 1, f:f + 1],
                                                                             scale=ab[:, 0, f:f + 1]), tk, t_ab, ht_rd[u])
                w_read[wi] = half[u]

            def high(u):
                hi, fp = hh[:, 2 * u:2 * u + 2, :], ht[:, u, :, :]
                if u % 2 == 0:
                    th[u] = S.do(lambda e: e.copy(hi, fp), half[u], t_free)
                else:
                    th[u] = V.do(lambda e: e.tensor_copy(hi, fp), half[u], t_free)

            def low(u):
                hi, lo, fp = hh[:, 2 * u:2 * u + 2, :], hl[:, 2 * u:2 * u + 2, :], ht[:, u, :, :]
                Q = V if u % 2 else G
                tl[u] = Q.do(lambda e: e.tensor_tensor(lo, fp, hi.bitcast(F32), ALU.subtract), th[u], t_free)
                ht_rd[u] = tl[u]

            for step, u in ((affine, 0), (affine, 1), (affine, 2), (high, 0), (low, 0), (high, 1), (low, 1), (affine, 3),
                            (high, 2), (low, 2), (high, 3), (low, 3)):
                step(u)
            return [[th[f // 2], tl[f // 2]] for f in range(KC)]

        st = small[:, 32:56].rearrange("p (t h s) -> p t h s", t=2, h=2)
        mv = small[:, 64:68].rearrange("p (t s) -> p t s", t=2)
        ve = small[:, 72:74]
        rs = small[:, 76:78]
        s_ln = dsem("s_ln")
        s_o = dsem("s_o")
        lnp_free = [None]
        t_ln = [None]
        xa_tok = [t_x]

        def load_ln(gsrc, bsrc, last=False):
            def load():
                SP.dma(lnp[:, 0, :], gsrc.to_broadcast([P, D]), s_ln, lnp_free[0])
                t_ln[0] = SP.dma(lnp[:, 1, :], bsrc.to_broadcast([P, D]), s_ln)
                if not last:
                    t_ln[0] = S.do(lambda e: e.activation(lnp[:, :, :], lnp[:, :, :], ACT.Copy, scale=ALPHA), t_ln[0])
            ln_plan[:] = [len(released) + NSLOT + 3, load]

        def layer_norm(t_y, gate, ahead):
            tx = [None] * 2
            assert not ln_plan

            def half(t, h):
                y = YB[2 * t + h]
                v = vv[:, t, h * 512:(h + 1) * 512]
                xs = xa[:, t, h * 512:(h + 1) * 512]
                if isinstance(gate, float):
                    tk = V.do(lambda e: e.scalar_tensor_tensor(v, y[:, :], gate, xs, ALU.mult, ALU.add),
                              t_y[t], xa_tok[0])
                    y_read[2 * t + h] = tk
                else:
                    g = gb[:, h * 512:(h + 1) * 512]
                    tk = V.do(lambda e: e.tensor_tensor(v, y[:, :], g, ALU.mult), t_y[t], gate)
                    y_read[2 * t + h] = tk
                    tk = V.do(lambda e: e.tensor_tensor(v, v, xs, ALU.add), tk, xa_tok[0])
                return V.do(lambda e: e.bn_stats(st[:, t, h, :], v), tk)

            def stats(t, tk):
                tk = V.do(lambda e: e.bn_aggr(mv[:, t, :], st[:, t, :, :].rearrange("p a b -> p (a b)")), tk)
                tg = G.do(lambda e: e.tensor_scalar(ve[:, t:t + 1], mv[:, t, 1:2], EPS, None, ALU.add), tk)
                tg = G.do(lambda e: e.tensor_tensor(rs[:, t:t + 1], ve[:, t:t + 1], nhalf, ALU.pow), tg, t_nh)
                tx[t] = (tg, tk)

            def scale(t):
                tx[t] = V.do(lambda e: e.tensor_scalar(vv[:, t, :], vv[:, t, :], mv[:, t, 0:1], rs[:, t:t + 1],
                                                       ALU.subtract, ALU.mult), *tx[t])

            half(0, 0)
            stats(0, half(0, 1))
            scale(0)
            half(1, 0)
            stats(1, half(1, 1))
            if ahead:
                prime()
            scale(1)

            def rest(last=False):
                toks = []
                for t in range(2):
                    Q = V if last and t else G
                    tg = Q.do(lambda e, t=t: e.tensor_tensor(xa[:, t, :], vv[:, t, :], lnp[:, 0, :], ALU.mult), tx[t], t_ln[0])
                    toks.append(Q.do(lambda e, t=t: e.tensor_tensor(xa[:, t, :], xa[:, t, :], lnp[:, 1, :], ALU.add), tg))
                lnp_free[0] = xa_tok[0] = toks
            return tx, rest

        def proj(dst, u, t_h, m=P):
            wh, wl, s_ = u
            for kc in range(KC):
                PE.wait(t_h[kc][0])
                for i, a in enumerate((wh, wl)):
                    mm(dst, a[:, kc * m:(kc + 1) * m], hh[:, kc, :], kc == 0 and i == 0, False)
            for kc in range(KC):
                PE.wait(t_h[kc][1])
                tk = mm(dst, wh[:, kc * m:(kc + 1) * m], hl[:, kc, :], False, kc == KC - 1, mark=(kc == KC - 1))
            done(s_, tk)
            return tk

        def cunit(name, src, c0, q, n=256):
            return unit((name, c0), src[:, c0:c0 + n], KC, n, lambda w: w[:, :, q * P:(q + 1) * P], (KC, P),
                        q == n // P - 1)

        def y_rows(n, items, started=False):
            out_ = []
            for t in range(2):
                for k, (wh, wl, s_, *held), zh, zl, t_z in items:
                    PE.wait(t_z, *held)
                    for h in range(2):
                        if k == 0 and not started:
                            PE.wait(y_read[2 * t + h])
                        for i, (a, z) in enumerate(((wh, zh), (wl, zh), (wh, zl))):
                            tk = mm(YB[2 * t + h][:, :], z[:, t * P:(t + 1) * P], a[:, h * 512:(h + 1) * 512],
                                    k == 0 and i == 0 and not started, k == n - 1 and i == 2, mark=(h == 1 and i == 2))
                    if t:
                        done(s_, tk)
                out_.append(tk)
            return out_

        def row_unit(name, src, k, ahead=AHEAD):
            j, q = divmod(k, 2)
            return unit((name, j), src[256 * j:256 * j + 256, :], 2, D, lambda w: w[:, q, :], (D,), q == 1, ahead,
                        ahead != AHEAD)

        def last_rows(name, src, n, z, started=False):
            items = [(k, row_unit(name, src, k, n - 1 - k)) + tuple(z(k)) for k in range(n - 3, n)]
            return y_rows(n, items, started)

        def out_rows(name, src, t_z, started=False):
            z = lambda k: (hh[:, k, :], hl[:, k, :], t_z[k])
            for k in range(KC - 3):
                y_rows(KC, [(k, row_unit(name, src, k)) + z(k)], started)
            return last_rows(name, src, KC, z, started)

        def split(hi, lo, src, *waits):
            th = S.do(lambda e: e.copy(hi, src), *waits)
            return [th, G.do(lambda e: e.tensor_tensor(lo, src, hi.bitcast(F32), ALU.subtract), th)]

        t_rope, t_sink = [], []

        def rotary_tables():
            ang = area(7424, T)
            kq = area(7680, T)
            red = area(7936, T)
            V.do(lambda e: e.tensor_copy(ang, posi), t_p)
            tk = V.do(lambda e: e.tensor_scalar(red, ang, const[:, C_INV:C_INV + 1], None, ALU.mult), (V.sem, V.n), t_const)
            magic = 1.5 * 2.0 ** 23
            tk = V.do(lambda e: e.tensor_scalar(kq, red, float(np.float32(1 / TWO_PI)), magic, ALU.mult, ALU.add), tk)
            tk = V.do(lambda e: e.tensor_scalar(kq, kq, -magic, None, ALU.add), tk)
            for cst in split_const(TWO_PI, 4, 10):
                tk = V.do(lambda e, c=cst: e.scalar_tensor_tensor(red, kq, -c, red, ALU.mult, ALU.add), tk)
            tk = V.do(lambda e: e.tensor_scalar(red, red, float(np.float32(3.1415925)), float(np.float32(-3.1415925)), ALU.min, ALU.max), tk)
            ta = S.do(lambda e: e.activation(sin[:, :], red, ACT.Sin), tk)
            ta = S.do(lambda e: e.activation(cos[:, :], red, ACT.Sin, scale=0.5), tk)
            tk = V.do(lambda e: e.tensor_tensor(cos[:, :], cos[:, :], cos[:, :], ALU.mult), ta)
            t_rope.append(V.do(lambda e: e.tensor_scalar(cos[:, :], cos[:, :], -2.0, 1.0, ALU.mult, ALU.add), tk))
            tk = V.do(lambda e: e.tensor_copy(sink[:, :, :, 0], sinkr[:, :].rearrange("p (l h) -> p l h", l=2)), t_m)
            t_sink.append(V.do(lambda e: e.tensor_copy(sink[:, :, :, 1], sinkr[:, :].rearrange("p (l h) -> p l h", l=2)), t_m))

        def mixer_a(t_h):
            uT = area(0, KC, 30 + T)
            acc = area(2304, KC, T)
            sq = area(4352, KC, T)
            tmp = area(6400, 4, T)
            tz = G.do(lambda e: e.memset(uT[:, :, 0:30], 0.0))
            tu = []
            tmp_rd = [None] * 4
            low_by[0] = G
            jobs.extend([ada(0, 1), ada(0, 2)])
            t_acc = [None] * KC

            prod_rd = [None] * KC

            def tap(Q, j, f):
                if Q is G:
                    if j == 0:
                        t_acc[f] = S.do(lambda e: e.activation(acc[:, f, :], uT[:, f, 0:T], ACT.Identity,
                                                               bias=col("a_b_dw", f), scale=dw(0, f)), tu[f], tz)
                        return
                    r = j % KC
                    tp = S.do(lambda e: e.activation(sq[:, r, :], uT[:, f, j:j + T], ACT.Copy, scale=dw(j, f)),
                              tu[f], tz, prod_rd[r])
                    t_acc[f] = prod_rd[r] = G.do(lambda e: e.tensor_tensor(acc[:, f, :], acc[:, f, :], sq[:, r, :],
                                                                           ALU.add), tp, t_acc[f])
                elif j == 0:
                    t_acc[f] = Q.do(lambda e: e.tensor_scalar(acc[:, f, :], uT[:, f, 0:T], dw(0, f), col("a_b_dw", f),
                                                              ALU.mult, ALU.add), tu[f], tz)
                else:
                    t_acc[f] = Q.do(lambda e: e.scalar_tensor_tensor(acc[:, f, :], uT[:, f, j:j + T], dw(j, f),
                                                                     acc[:, f, :], ALU.mult, ALU.add), t_acc[f])

            def conv(Q, *fs):
                beside[Q is V][0].extend([lambda j=j, f=f: tap(Q, j, f) for j in range(CW) for f in fs])

            for f in range(KC):
                j, q = divmod(f, 2)
                wi, b = bank()
                proj(b[:, 0:T], cunit("a_in", I["a_w_in"][0], 256 * j, q), t_h)
                tk = proj(b[:, T:2 * T], cunit("a_in", I["a_w_in"][0], D + 256 * j, q), t_h)
                r = f % 4
                ts = S.do(lambda e, b=b, f=f, r=r: e.activation(tmp[:, r, :], b[:, T:2 * T], ACT.Sigmoid,
                                                                bias=col("a_b_in", 8 + f)), tk, tmp_rd[r])
                tv = V.do(lambda e, b=b, f=f, r=r: e.scalar_tensor_tensor(
                    uT[:, f, 30:30 + T], b[:, 0:T], col("a_b_in", f), tmp[:, r, :], ALU.add, ALU.mult), ts, tk)
                w_read[wi] = tv
                tmp_rd[r] = tv
                tu.append(tv)
                if f == 0:
                    rotary_tables()
                ada_steps(2)
                if f in (1, 4, 6):
                    conv(V, *{1: (0, 1), 4: (3, 4), 6: (5, 6)}[f])
                if f in (2, 7):
                    conv(G, f)
            for todo, _ in beside:
                while todo:
                    todo.pop(0)()
            t_free = tk
            ada_steps(16)
            low_by[0] = V
            wi, b = bank()
            PE.wait(*t_acc, t_ones)
            for f in range(KC):
                tk = mm(b[:, 0:T], ones[:, :], acc[:, f, :], f == 0, f == KC - 1, mark=(f == KC - 1))
            td, tq = [], []
            for f in range(KC):
                td.append(V.do(lambda e, f=f, b=b: e.scalar_tensor_tensor(acc[:, f, :], b[:, 0:T], -1.0 / D, acc[:, f, :],
                                                                     ALU.mult, ALU.add), tk))
                tq.append(S.do(lambda e, f=f: e.activation(sq[:, f, :], acc[:, f, :], ACT.Square), td[-1], prod_rd[f]))
            w_read[wi] = td[-1]
            wi, b = bank()
            for f in range(KC):
                PE.wait(tq[f])
            for t in range(2):
                for f in range(KC):
                    tk = mm(b[:, t:t + 1], sq[:, f, t * P:(t + 1) * P], ones[:, 0:1], f == 0, f == KC - 1,
                            mark=(f == KC - 1))
            var, rsd = small[:, 212:214], small[:, 214:216]
            tv = V.do(lambda e, b=b: e.tensor_scalar(var, b[:, 0:2], 1.0 / D, EPS, ALU.mult, ALU.add), tk)
            w_read[wi] = tv
            tg = G.do(lambda e: e.tensor_tensor(rsd, var, nhalf.to_broadcast([P, 2]), ALU.pow), tv, t_nh)
            wi, b = bank()
            PE.wait(tg)
            for t in range(2):
                ts = mm(b[:, t * P:(t + 1) * P], rsd[:, t:t + 1].to_broadcast([P, P]), ident, True, True, mark=(t == 1))
            tg = V.do(lambda e, b=b: e.tensor_copy(tmp[:, 1, :], b[:, 0:T]), ts)
            w_read[wi] = tg
            tzs = []
            for f in range(KC):
                tv = V.do(lambda e, f=f: e.tensor_tensor(acc[:, f, :], acc[:, f, :], tmp[:, 1, :], ALU.mult), tg)
                ts = S.do(lambda e, f=f: e.activation(sq[:, f, :], acc[:, f, :], ACT.Silu, bias=col("a_ln_b", f),
                                                      scale=col("a_ln_g", f)), tv, tk)
                tzs.append(split(hh[:, f, :], hl[:, f, :], sq[:, f, :], ts, t_free))
            for t in range(2):
                for h in range(2):
                    PE.wait(y_read[2 * t + h], t_m)
                    mm(YB[2 * t + h][:, :], ones[0:1, :], bout[:, h * 512:(h + 1) * 512], True, False)
            return out_rows("a_out", I["a_w_out"][0], tzs, started=True)

        def mixer_b(t_h):
            uT = area(0, KC, 2 + T)
            gbT = area(2304, KC, T)
            zT = area(4352, KC, T)
            tmp = area(6400, 4, T)
            tz = G.do(lambda e: e.memset(uT[:, :, 0:2], 0.0), *t_h)
            tzf = []
            tmp_rd = [None] * 4
            src = I["b_w_in"][0]
            for f in range(KC):
                j, q = divmod(f, 2)
                wi, b = bank()
                proj(b[:, 0:T], cunit("b_in", src, D + 256 * j, q), t_h)
                tk = proj(b[:, T:2 * T], cunit("b_in", src, 2 * D + 256 * j, q), t_h)
                r = f % 4
                ta = S.do(lambda e, b=b, r=r: e.copy(tmp[:, r, :], b[:, 0:T]), tk, tmp_rd[r])
                tv = V.do(lambda e, b=b, f=f, r=r: e.tensor_tensor(uT[:, f, 2:2 + T], b[:, T:2 * T], tmp[:, r, :], ALU.mult), ta)
                w_read[wi] = tv
                tmp_rd[r] = tv
                wi, b = bank()
                tk = proj(b[:, 0:T], cunit("b_in", src, 256 * j, q), t_h)
                ta = S.do(lambda e, b=b, f=f: e.copy(gbT[:, f, :], b[:, 0:T]), tk)
                w_read[wi] = ta
                w = lambda i, f=f: col("b_w_dw", i * 8 + f)
                tv = V.do(lambda e, f=f, w=w: e.tensor_scalar(zT[:, f, :], uT[:, f, 0:T], w(0), None, ALU.mult), tv, tz)
                for i in (1, 2):
                    tv = V.do(lambda e, f=f, w=w, i=i: e.scalar_tensor_tensor(
                        zT[:, f, :], uT[:, f, i:i + T], w(i), zT[:, f, :], ALU.mult, ALU.add), tv)
                tzf.append(V.do(lambda e, f=f: e.tensor_tensor(zT[:, f, :], zT[:, f, :], gbT[:, f, :], ALU.mult), tv, ta))
                ada_steps(1)
            ada_steps(8)
            tzs = [split(hh[:, f, :], hl[:, f, :], zT[:, f, :], tzf[f], tk) for f in range(KC)]
            return out_rows("b_out", I["b_w_out"][0], tzs)

        def moe(l, t_h, t_x_, after):
            vh, vl = [a[:, :, :].rearrange("p k t -> p (k t)").rearrange("p (t d) -> p t d", t=2) for a in (hh, hl)]

            def vv_split(tok):
                th = [S.do(lambda e, t=t: e.copy(vh[:, t, :], vv[:, t, :]), tok, t_x_[t]) for t in range(2)]
                return th, [G.do(lambda e, t=t: e.tensor_tensor(vl[:, t, :], vv[:, t, :], vh[:, t, :].bitcast(F32),
                                                                ALU.subtract), th[t]) for t in range(2)]

            lg = area(0, 2, 40)
            m8 = area(80, 2, 2, 8)
            ix = area(112, 2, 2, 8).bitcast(U32)
            sc = area(144, 2, 8)
            ef = area(160, 2, 32)
            oh = area(224, 2, 2, 32)
            pen = area(352, 2, 32)
            cum = area(416, 2, 32)
            rk = area(480, 4)
            slot = area(484, 4)
            sg = area(488, 4, 4)
            jk = area(504, 4, 32)
            oo = area(632, 2, 32)
            xg = area(768, 2, KC, 512)
            Sg = wsp[:, 0:2, 0, :].rearrange("p u (t n) -> p u t n", t=2)
            Cg = area(8960, 2, 2, 512)
            hd = ht[:, 2, :, :]
            he = ht[:, 3, :, :].rearrange("p a (b c s) -> p a b c s", b=2, c=2)
            ye = area(11008, 2, 2, 512)
            ct = ht[:, 1, :, :]
            tmpc = ht[:, 0, :, :].rearrange("p a b -> p (a b)")
            wrh, wrl = [wsp[:, 2, i, :].rearrange("p (k n) -> p k n", k=KC) for i in range(2)]
            lgt = area(13056, T)[0:36, :]
            th = V.do(lambda e: e.tensor_copy(wrh[:, :, 0:36], wr[:, l, :, :]), t_m, *unit_pe)
            twr = V.do(lambda e: e.tensor_tensor(wrl[:, :, 0:36], wr[:, l, :, :], wrh[:, :, 0:36].bitcast(F32),
                                                 ALU.subtract), th)
            wi, b = bank()
            PE.wait(t_m, t_ones, twr)
            for i, (a, z) in enumerate(((wrh, hh), (wrl, hh), (wrh, hl))):
                for kc in range(KC):
                    PE.wait(t_h[kc][i // 2])
                    tk = mm(b[:, 0:T], a[:, kc, :], z[:, kc, :], kc == 0 and i == 0, kc == KC - 1 and i == 2,
                            mark=(kc == KC - 1 and i == 2))
            t_vs = vv_split(tk)
            tv = V.do(lambda e, b=b: e.tensor_copy(lgt, b[0:36, 0:T]), tk, mod_done.get("turned"), t_ca[0])
            w_read[wi] = tv
            V.do(lambda e: e.memset(lg[:, :, 4:8], NEG))
            wi, b = bank()
            PE.wait(tv)
            for t in range(2):
                o = b[:, 64 * t:64 * t + 36]
                mm(o, lgt[:, t * P:(t + 1) * P], ident[0:36, 0:36], True, False)
                tk = mm(o, ones[0:1, :], rb[:, l, :], False, True, mark=True)
            v = lambda f, *w: V.do(f, (V.sem, V.n), *w)
            v(lambda e, b=b: e.tensor_copy(lg[:, :, 0:4], b[:, 0:128].rearrange("p (t n) -> p t n", t=2)[:, :, 0:4]), tk)
            tv = V.do(lambda e, b=b: e.tensor_copy(lg[:, :, 8:40], b[:, 0:128].rearrange("p (t n) -> p t n", t=2)[:, :, 4:36]), tk)
            w_read[wi] = tv
            last, ts = [tv] * 2, [None] * 2

            def both(fn, *w, Q=V):
                for t in range(2):
                    tok = Q.do(lambda e, t=t: fn(e, t), last[t], *[x[t] for x in w])
                    if Q is V:
                        last[t] = tok
                    else:
                        ts[t] = tok

            both(lambda e, t: e.max(m8[:, t, 0, :], lg[:, t, 0:8]))
            both(lambda e, t: e.max_index(ix[:, t, 0, :], m8[:, t, 0, :], lg[:, t, 0:8]))
            both(lambda e, t: e.tensor_scalar(sc[:, t, 7:8], m8[:, t, 0, 0:1], -1.0, None, ALU.mult))
            both(lambda e, t: e.activation(ef[:, t, 0:4], lg[:, t, 0:4], ACT.Exp, bias=sc[:, t, 7:8],
                                           accum_out=sc[:, t, 1:2]), Q=S)
            ts1 = list(ts)
            both(lambda e, t: e.tensor_copy(sc[:, t, 2:3], ix[:, t, 0, 0:1]))
            both(lambda e, t: e.tensor_scalar(pen[:, t, :], const[:, C_IG:C_IG + 32], sc[:, t, 2:3], NEG,
                                              ALU.not_equal, ALU.mult))
            both(lambda e, t: e.tensor_tensor(lg[:, t, 8:40], lg[:, t, 8:40], pen[:, t, :], ALU.add))
            both(lambda e, t: e.max(m8[:, t, 1, :], lg[:, t, 8:40]))
            both(lambda e, t: e.max_index(ix[:, t, 1, :], m8[:, t, 1, :], lg[:, t, 8:40]))
            both(lambda e, t: e.tensor_scalar(sc[:, t, 0:1], m8[:, t, 1, 0:1], -1.0, None, ALU.mult))
            both(lambda e, t: e.activation(sc[:, t, 3:4], m8[:, t, 1, 1:2], ACT.Exp, bias=sc[:, t, 0:1]), Q=S)
            both(lambda e, t: e.tensor_copy(jk[:, t, 0:2], ix[:, t, 1, 0:2]))
            for j in range(2):
                both(lambda e, t, j=j: e.tensor_scalar(oh[:, t, j, :], const[:, C_IO:C_IO + 32], jk[:, t, j:j + 1], None,
                                                       ALU.is_equal))
            both(lambda e, t: e.tensor_tensor(oo[:, t, :], oh[:, t, 0, :], oh[:, t, 1, :], ALU.add))
            to_ = list(last)
            both(lambda e, t: e.tensor_scalar(sc[:, t, 4:5], sc[:, t, 3:4], 1.0, None, ALU.add), ts)
            both(lambda e, t: e.tensor_tensor(sc[:, t, 4:5], sc[:, t, 4:5], sc[:, t, 1:2], ALU.mult), ts1)
            both(lambda e, t: e.reciprocal(sc[:, t, 5:6], sc[:, t, 4:5]))
            both(lambda e, t: e.tensor_tensor(sc[:, t, 6:7], sc[:, t, 5:6], sc[:, t, 3:4], ALU.mult))
            both(lambda e, t: e.tensor_copy(sc[:, t, 0:2], jk[:, t, 0:2]))
            wi, b = bank()
            PE.wait(to_)
            tri = const[:, C_TRI:C_TRI + P]
            mm(b[:, 0:32], tri, oo[:, 0, :], True, True)
            mm(b[:, 32:64], ones[:, :], oo[:, 0, :], True, False)
            mm(b[:, 32:64], tri, oo[:, 1, :], False, True)
            mm(b[:, 64:96], ones[:, :], oo[:, 0, :], True, False)
            tk = mm(b[:, 64:96], ones[:, :], oo[:, 1, :], False, True, mark=True)
            v(lambda e, b=b: e.tensor_copy(cum[:, :, :], b[:, 0:64].rearrange("p (t n) -> p t n", t=2)), tk)
            tv = v(lambda e, b=b: e.tensor_copy(cnt[:, :], b[:, 64:96]))
            w_read[wi] = tv
            for t in range(2):
                for j in range(2):
                    i = 2 * t + j
                    V.do(lambda e, t=t, j=j, i=i: e.tensor_tensor_reduce(
                        jk[:, i, :], oh[:, t, j, :], cum[:, t, :], 1.0, 0.0, ALU.mult, ALU.add, rk[:, i:i + 1]), tv)
            v(lambda e: e.scalar_tensor_tensor(slot.rearrange("p (t j) -> p t j", t=2), sc[:, :, 0:2], float(CAP),
                                               rk.rearrange("p (t j) -> p t j", t=2), ALU.mult, ALU.add))
            V.do(lambda e: e.tensor_scalar(jk[:, 0, 0:4], rk, float(CAP), -1e6, ALU.is_ge, ALU.mult))
            v(lambda e: e.tensor_tensor(sg[:, 0, :], slot, jk[:, 0, 0:4], ALU.add))

            def other_slots():
                for g in range(1, 4):
                    v(lambda e, g=g: e.tensor_scalar(sg[:, g, :], sg[:, 0, :], -512.0 * g, None, ALU.add))
                v(lambda e: e.tensor_copy(slot_all[:, :], slot))
                for r in range(1, 4):
                    v(lambda e, r=r: e.tensor_scalar(jk[:, 0, 0:4], rk, float(CAP * r), float(CAP * (E - 1)), ALU.is_ge,
                                                     ALU.mult))
                    v(lambda e: e.tensor_tensor(slot_all[:, :], slot_all[:, :], jk[:, 0, 0:4], ALU.add))
                v(lambda e: e.tensor_scalar(slot_all[:, :], slot_all[:, :], -float(CAP * (E - 1)), None, ALU.add))
                for r in range(3):
                    v(lambda e, r=r: e.tensor_scalar(blk_n[:, 1 + 32 * r:33 + 32 * r], cnt[:, :], float(CAP * (r + 1)), None,
                                                     ALU.is_gt))
                v(lambda e: e.tensor_reduce(most, cnt[:, :], AX, ALU.max))
                return v(lambda e: e.tensor_scalar(blk_n[:, 0:1], most, float(CAP), None, ALU.is_gt))

            xg_rd, c_rd = [None] * 2, [None] * 2
            t_S, t_C, t_xg = [None] * 4, [None] * 4, {}

            def choose(g):
                u = g % 2
                i5 = const[:, C_I5:C_I5 + 512]
                for t in range(2):
                    a = sg[:, g, 2 * t:2 * t + 1]
                    z = sg[:, g, 2 * t + 1:2 * t + 2]
                    tv = V.do(lambda e, t=t, a=a: e.tensor_scalar(Sg[:, u, t, :], i5, a, None, ALU.is_equal),
                              (V.sem, V.n), xg_rd[u])
                    t_S[g] = V.do(lambda e, t=t, z=z: e.scalar_tensor_tensor(Sg[:, u, t, :], i5, z, Sg[:, u, t, :].bitcast(F32),
                                                                             ALU.is_equal, ALU.add), tv)
                for t in range(2):
                    a = sg[:, g, 2 * t:2 * t + 1]
                    z = sg[:, g, 2 * t + 1:2 * t + 2]
                    V.do(lambda e, t=t, a=a: e.tensor_scalar(Cg[:, u, t, :], i5, a, sc[:, t, 5:6], ALU.is_equal, ALU.mult),
                         c_rd[u], t_S[g])
                    tv = V.do(lambda e, t=t, z=z: e.tensor_scalar(tmpc, i5, z, sc[:, t, 6:7], ALU.is_equal, ALU.mult),
                              (V.sem, V.n))
                    t_C[g] = V.do(lambda e, t=t: e.tensor_tensor(Cg[:, u, t, :], Cg[:, u, t, :], tmpc, ALU.add), tv)

            def gather(g, kc):
                u = g % 2
                wi, b = bank()
                PE.wait(t_S[g])
                for t in range(2):
                    for i, a in enumerate((vh, vl)):
                        PE.wait(t_vs[i][t])
                        tk = mm(b[:, :], a[:, t, kc * P:(kc + 1) * P], Sg[:, u, t, :], t == 0 and i == 0, t == 1 and i == 1,
                                mark=(t == 1 and i == 1))
                if kc == KC - 1:
                    xg_rd[u] = tk
                if kc % 2:
                    tv = V.do(lambda e, b=b: e.tensor_scalar(xg[:, u, kc, :], b[:, :], ab[:, 0, kc:kc + 1],
                                                             ab[:, 1, kc:kc + 1], ALU.mult, ALU.add), tk, x_done.get(g - 2))
                else:
                    tv = S.do(lambda e, b=b: e.activation(xg[:, u, kc, :], b[:, :], ACT.Identity, bias=ab[:, 1, kc:kc + 1],
                                                          scale=ab[:, 0, kc:kc + 1]), tk, x_done.get(g - 2))
                w_read[wi] = tv
                t_xg.setdefault(g, []).append(tv)

            x_done = {}
            hd_t, he_t, ye_t, ct_t = {}, {}, {}, {}
            hd_rd, he_rd, ye_rd, ct_rd = [None] * 2, [None] * 2, [None] * 2, [None] * 2

            def up(e_):
                g, u, x0 = e_ // 8, (e_ // 8) % 2, CAP * (e_ % 8)
                wi, b = bank()
                PE.wait(*t_xg[g])
                for h in range(4):
                    vw = lambda r, q: r.rearrange("p (k u n) -> p k u n", k=2, u=2)[:, :, q, :]
                    n, r, tok = piece(*[(lambda r, q=q: vw(r, q),
                                         I[nm][l, e_, 256 * h:256 * h + 256, :].rearrange("(k p) n -> p k n", p=P))
                                        for q, nm in enumerate(("e_w_gate", "e_w_up"))])
                    PE.wait(tok)
                    r4 = r.rearrange("p (k u n) -> p k u n", k=2, u=2)
                    for k in range(2):
                        kc = 2 * h + k
                        for c in range(2):
                            tk = mm(b[64 * c:64 * c + 64, :], xg[:, u, kc, x0:x0 + CAP], r4[:, k, :, 256 * c:256 * c + 256],
                                    kc == 0, kc == KC - 1, mark=(k == 1 and c == 1))
                    released[n] = tk
                if e_ % 8 == 7:
                    x_done[g] = tk
                i = e_ % 2
                ts = S.do(lambda e, b=b, i=i: e.activation(hd[:, i, :], b[:, 0:T], ACT.Silu), tk, hd_rd[i])
                hd_t[e_] = V.do(lambda e, b=b, i=i: e.tensor_tensor(hd[:, i, :], b[:, T:2 * T], hd[:, i, :], ALU.mult), ts)
                w_read[wi] = hd_t[e_]

            def turn(e_):
                i = e_ % 2
                wi, b = bank()
                PE.wait(hd_t[e_])
                for c in range(2):
                    tk = tr(b[:, c * P:(c + 1) * P], hd[:, i, c * P:(c + 1) * P], ident, mark=(c == 1))
                hd_rd[i] = tk
                he_t[e_] = V.do(lambda e, b=b, i=i: e.tensor_copy(he[:, i, :, :, :].rearrange("p c h s -> p (c h s)"), b[:, 0:T]), tk, he_rd[i])
                w_read[wi] = he_t[e_]
                if e_ % 2 == 0:
                    g, u, x0 = e_ // 8, (e_ // 8) % 2, CAP * (e_ % 8)
                    i = (e_ // 2) % 2
                    wi, b = bank()
                    PE.wait(t_C[g])
                    for t in range(2):
                        tk = tr(b[:, t * P:(t + 1) * P], Cg[:, u, t, x0:x0 + P], ident, mark=(t == 1))
                    if e_ % 8 == 6:
                        c_rd[u] = tk
                    ct_t[e_ // 2] = S.do(lambda e, b=b, i=i: e.copy(ct[:, i, :], b[:, 0:T]), tk, ct_rd[i])
                    w_read[wi] = ct_t[e_ // 2]

            def down(e_):
                i = e_ % 2
                wi, b = bank()
                PE.wait(he_t[e_])
                for h in range(2):
                    n, w, tok = block(I["e_w_down"][l, e_, 256 * h:256 * h + 256, :], 2, D)
                    PE.wait(tok)
                    for c in range(2):
                        for dh in range(2):
                            tk = mm(b[64 * dh:64 * dh + 64, :], he[:, i, c, h, :], w[:, c, 512 * dh:512 * dh + 512],
                                    h == 0 and c == 0, h == 1 and c == 1, mark=(c == 1 and dh == 1))
                    released[n] = tk
                he_rd[i] = tk
                pr = (e_ // 2) % 2
                p0 = 64 * i
                for dh in range(2):
                    o = ye[p0:p0 + 64, pr, dh, :]
                    src = b[64 * dh:64 * dh + 64, :]
                    if e_ % 2:
                        tv = S.do(lambda e, o=o, src=src: e.copy(o, src), tk, ye_rd[pr])
                    else:
                        tv = V.do(lambda e, o=o, src=src: e.tensor_copy(o, src), tk, ye_rd[pr])
                w_read[wi] = tv
                ye_t[e_] = tv

            def combine(p):
                i = p % 2
                PE.wait(ye_t[2 * p], ye_t[2 * p + 1], ct_t[p])
                for t in range(2):
                    for dh in range(2):
                        if p == 0:
                            PE.wait(y_read[2 * t + dh])
                        tk = mm(YB[2 * t + dh][:, :], ct[:, i, t * P:(t + 1) * P], ye[:, i, dh, :], p == 0, p == E // 2 - 1,
                                mark=(dh == 1))
                    if t == 0:
                        tk0 = tk
                ye_rd[i] = ct_rd[i] = tk
                return [tk0, tk]

            choose(0)
            for kc in range(KC):
                gather(0, kc)
            t_blk = other_slots()
            choose(1)
            t_gate = after()
            ht_rd[:] = [None] * 4
            for e_ in range(E + 3):
                if e_ < E:
                    up(e_)
                if 1 <= e_ <= E:
                    down(e_ - 1)
                if e_ % 2 == 1 and e_ >= 3:
                    tk = combine((e_ - 3) // 2)
                if e_ < E:
                    turn(e_)
                    g = e_ // 8 + 1
                    if g < 4:
                        gather(g, e_ % 8)
                    if e_ % 8 == 7 and g + 1 < 4:
                        choose(g + 1)
            late(l, t_blk, Sg, Cg, xg, hd, he, ye, ct, sc)
            for i in range(UNITS):
                unit_pe[i] = tk[1]
            if learning:
                fences.append(len(order))
            return tk, t_gate

        def late(l, t_blk, Sg, Cg, xg, hd, he, ye, ct, sc):
            before = [(q.sem, q.n) for q in (PE, V, S, G)]
            pe, ve, ac = (Queue(x) for x in late_sems[:3])
            at = {}
            S1 = Sg[:, 0, :, 0:CAP]
            C1 = Cg[:, 0, :, 0:CAP]
            tmp1 = Cg[:, 1, 0, 0:CAP]
            x1 = xg[:, 0, :, 0:CAP]
            io = const[:, C_I5:C_I5 + CAP]
            sl = lambda t, j: slot_all[:, 2 * t + j:2 * t + j + 1]

            def loads(e):
                x = at[id(e)]
                n = 0
                for h in range(4):
                    dst = ring[:, h, :].rearrange("p (k u n) -> p k u n", k=2, u=2)
                    for q, nm in enumerate(("e_w_gate", "e_w_up")):
                        src = I[nm][l].rearrange("e (h k p) n -> p h e k n", h=4, p=P)[:, h, bass.ds(x, 1), :, :]
                        e.dma_start(dst[:, :, q, :], src[:, 0, :, :]).then_inc(late_dma, 16)
                for h in range(2):
                    dst = ring[:, 4 + h, :].rearrange("p (k n) -> p k n", k=2)
                    src = I["e_w_down"][l].rearrange("e (h k p) n -> p h e k n", h=2, p=P)[:, h, bass.ds(x, 1), :, :]
                    e.dma_start(dst, src[:, 0, :, :]).then_inc(late_dma, 16)
            t_w = (late_dma, 160)

            for t in range(2):
                tv = ve.do(lambda e, t=t: e.tensor_scalar(S1[:, t, :], io, sl(t, 0), None, ALU.is_equal))
                t_s = ve.do(lambda e, t=t: e.scalar_tensor_tensor(S1[:, t, :], io, sl(t, 1), S1[:, t, :].bitcast(F32), ALU.is_equal,
                                                                  ALU.add), tv)
            for t in range(2):
                ve.do(lambda e, t=t: e.tensor_scalar(C1[:, t, :], io, sl(t, 0), sc[:, t, 5:6], ALU.is_equal, ALU.mult))
                tv = ve.do(lambda e, t=t: e.tensor_scalar(tmp1, io, sl(t, 1), sc[:, t, 6:7], ALU.is_equal, ALU.mult),
                           (ve.sem, ve.n))
                t_c = ve.do(lambda e, t=t: e.tensor_tensor(C1[:, t, :], C1[:, t, :], tmp1, ALU.add), tv)
            b = WB[0]
            pe.wait(t_s)
            for kc in range(KC):
                for t in range(2):
                    tk = pe.do(lambda e, kc=kc, t=t: e.matmul(b[:, kc * CAP:(kc + 1) * CAP], vv[:, t, kc * P:(kc + 1) * P],
                                                              S1[:, t, :].bitcast(F32), start=(t == 0), stop=(t == 1)))
            for kc in range(KC):
                tv = ve.do(lambda e, kc=kc: e.tensor_scalar(x1[:, kc, :], b[:, kc * CAP:(kc + 1) * CAP], ab[:, 0, kc:kc + 1],
                                                            ab[:, 1, kc:kc + 1], ALU.mult, ALU.add), tk)
            b1 = WB[1]
            pe.wait(tv, t_w)
            for kc in range(KC):
                for c in range(2):
                    w = ring[:, kc // 2, :].rearrange("p (k u n) -> p k u n", k=2, u=2)[:, kc % 2, :, 256 * c:256 * c + 256]
                    tk = pe.do(lambda e, kc=kc, c=c, w=w: e.matmul(b1[64 * c:64 * c + 64, :], x1[:, kc, :], w,
                                                                   start=(kc == 0), stop=(kc == KC - 1)))
            ts = ac.do(lambda e: e.activation(hd[:, 0, :], b1[:, 0:T], ACT.Silu), tk)
            tv = ve.do(lambda e: e.tensor_tensor(hd[:, 0, :], b1[:, T:2 * T], hd[:, 0, :], ALU.mult), ts)
            b2 = WB[2]
            pe.wait(tv, t_c)
            for c in range(2):
                tk = pe.do(lambda e, c=c: e.transpose(b2[:, c * P:(c + 1) * P], hd[:, 0, c * P:(c + 1) * P], ident))
            for t in range(2):
                tk = pe.do(lambda e, t=t: e.transpose(b2[0:CAP, T + t * P:T + (t + 1) * P], C1[:, t, :], ident))
            ve.do(lambda e: e.tensor_copy(he[:, 0, :, :, :].rearrange("p c h s -> p (c h s)"), b2[:, 0:T]), tk)
            tv = ve.do(lambda e: e.tensor_copy(ct[0:CAP, 0, :], b2[0:CAP, T:2 * T]))
            b3 = WB[3]
            pe.wait(tv)
            for h in range(2):
                for c in range(2):
                    for dh in range(2):
                        w = ring[:, 4 + h, c * D + 512 * dh:c * D + 512 * dh + 512]
                        tk = pe.do(lambda e, h=h, c=c, dh=dh, w=w: e.matmul(
                            b3[64 * dh:64 * dh + 64, :], he[:, 0, c, h, :], w, start=(h == 0 and c == 0),
                            stop=(h == 1 and c == 1)))
            for dh in range(2):
                tv = ve.do(lambda e, dh=dh: e.tensor_copy(ye[0:64, 0, dh, :], b3[64 * dh:64 * dh + 64, :]), tk)
            pe.wait(tv)
            for t in range(2):
                for dh in range(2):
                    pe.do(lambda e, t=t, dh=dh: e.matmul(YB[2 * t + dh][:, :], ct[0:64, 0, t * P:(t + 1) * P],
                                                         ye[0:64, 0, dh, :], start=False, stop=True,
                                                         skip_group_check=True))

            def walk(q, who, body):
                def run(e):
                    e.wait_ge(*t_blk)
                    any_ = e.value_load(blk_n[0:1, 0:1], min_val=0, max_val=1)
                    with e.If(any_ != 0):
                        for tok in before:
                            e.wait_ge(*tok)
                        with e.Fori(0, 3) as r:
                            with e.Fori(0, E) as x:
                                if who == 1:
                                    e.tensor_scalar(slot_all[:, :], slot_all[:, :], -float(CAP), None,
                                                    ALU.add).then_inc(late_step, 1)
                                    e.wait_ge(late_step, 1)
                                    e.sem_clear(late_step)
                                here = e.value_load(blk_n[0:1, bass.ds(r * E + x + 1, 1)], min_val=0, max_val=1)
                                with e.If(here != 0):
                                    at[id(e)] = x
                                    body(e)
                                    if who is None:
                                        e.wait_ge(late_in, 4)
                                        for s_ in late_sems[:3] + [late_dma, late_in]:
                                            e.sem_clear(s_)
                                        for s_ in late_go:
                                            e.sem_inc(s_, 1)
                                    else:
                                        e.drain().then_inc(late_in, 1)
                                        e.wait_ge(late_go[who], 1)
                                        e.sem_clear(late_go[who])
                q.ops.append(run)

            walk(SP, None, loads)
            walk(PE, 0, pe.emit)
            walk(V, 1, ve.emit)
            walk(S, 2, ac.emit)
            walk(G, 3, lambda e: None)

        def ffn(name, win, wout, t_h):
            hid = area(0, 4, T)
            oname = (name, "out")
            hrd, zrd = [None] * 4, [None] * 4
            th = {}

            def z(k):
                r = k % 4
                return zsp[:, r, 0, :], zsp[:, r, 1, :], th[k]

            for k in range(22):
                j, q = divmod(k, 2)
                wi, b = bank()
                proj(b[:, 0:T], cunit(name, win, 256 * j, q), t_h)
                tk = proj(b[:, T:2 * T], cunit(name, win, DFF + 256 * j, q), t_h)
                r = k % 4
                ts = S.do(lambda e, b=b, r=r: e.activation(hid[:, r, :], b[:, 0:T], ACT.Silu), tk, hrd[r])
                tv = V.do(lambda e, b=b, r=r: e.tensor_tensor(hid[:, r, :], b[:, T:2 * T], hid[:, r, :], ALU.mult), ts)
                w_read[wi] = tv
                th[k] = split(zsp[:, r, 0, :], zsp[:, r, 1, :], hid[:, r, :], tv, zrd[r])
                hrd[r] = th[k][1]
                if 0 < k < 20:
                    zrd[(k - 1) % 4] = y_rows(22, [(k - 1, row_unit(oname, wout, k - 1)) + z(k - 1)])[1]
            return last_rows(oname, wout, 22, z)

        def hybrid(l, t_h):
            W = I["w_in_2"][l]
            o = 0

            def take(*shape):
                nonlocal o
                a = area(o, *shape)
                o += int(np.prod(shape))
                return a

            qA, qB = take(4, T), take(4, T)
            kA, kB = take(4, T), take(2, T)
            va, vb, vc = take(2, 512), take(2, 128), take(2, 64)
            wi_ = take(2, 8)
            raw, rot = take(2, T), take(2, T)
            gates = [take(KC, T), take(KC, T)]
            sm = take(4, 384)
            isc = take(384)
            pt = take(2, 384)
            maskc = take(384)
            stt = take(2, 2, 4)
            mT = vv[:, :, :].rearrange("p a (b t) -> p (a b) t", t=T)
            oh = zsp[:, :, 0, :]
            ol = zsp[:, :, 1, :]
            raw_rd, rot_rd = [None] * 2, [None] * 2
            cnt_ = [0]

            def rope(src, dst, scale, tk, wi, *waits):
                r = cnt_[0] % 2
                cnt_[0] += 1
                ta = S.do(lambda e, r=r: e.activation(raw[:, r, :], src, ACT.Copy, scale=scale), tk, raw_rd[r])
                w_read[wi] = ta
                wj, b = bank()
                PE.wait(ta)
                tp = mm(b[:, 0:T], perm, raw[:, r, :], True, True, mark=True)
                tg = G.do(lambda e, r=r: e.tensor_tensor(rot[:, r, :], raw[:, r, :], cos[:, :], ALU.mult), ta, t_rope, rot_rd[r])
                raw_rd[r] = [tg, tp]
                tv = V.do(lambda e, b=b: e.tensor_tensor(dst, b[:, 0:T], sin[:, :], ALU.mult), tp, t_rope, *waits)
                w_read[wj] = tv
                tv = V.do(lambda e, r=r: e.tensor_tensor(dst, dst, rot[:, r, :], ALU.add), tv, tg)
                rot_rd[r] = tv
                return tv

            pend = []

            def flush():
                for _, f in pend:
                    f()
                pend.clear()

            tok_of = {}

            def later(key, b, dst, scale, tk, wi, *waits):
                flush()
                pend.append((key, lambda: tok_of.__setitem__(key, rope(b[:, 0:T], dst, scale, tk, wi, *waits))))

            def feat_chunk(c0, f, dst, key, scale, *waits):
                j, q = divmod(f, 2)
                wi, b = bank()
                tk = proj(b[:, 0:T], cunit(("w", l), W, c0 + 256 * j, q), t_h)
                later(key, b, dst[:, f, :], scale, tk, wi, *waits)

            def dup(piece_, c0, dst, key, last, *waits):
                u = unit(*piece_, lambda w: w[:, :, c0:c0 + 64].unsqueeze(2).to_broadcast([P, KC, 2, 64]), (KC, 2, 64), last)
                wi, b = bank()
                tk = proj(b[:, 0:T], u, t_h)
                later(key, b, dst, 1.0, tk, wi, *waits)

            def tokmajor(piece_, c0, n, dst, last, *waits):
                u = unit(*piece_, lambda w: w[:, :, c0:c0 + n], (KC, n), last)
                wi, b = bank()
                for t in range(2):
                    for kc in range(KC):
                        PE.wait(t_h[kc])
                        for i, (a, z) in enumerate(((hh, u[0]), (hl, u[0]), (hh, u[1]))):
                            tk = mm(b[:, t * T:t * T + n], a[:, kc, t * P:(t + 1) * P], z[:, kc * n:kc * n + n],
                                    kc == 0 and i == 0, kc == KC - 1 and i == 2, mark=(kc == KC - 1 and i == 2))
                done(u[2], tk)
                flush()
                tv = V.do(lambda e, b=b: e.tensor_copy(dst, b[:, :].rearrange("p (t n) -> p t n", t=2)[:, :, 0:n]), tk, *waits)
                w_read[wi] = tv
                return tv

            def few(piece_, m, c0, n, tmp, dst):
                u = unit(*piece_, lambda w: w[:, :, 0:m], (KC, m), True)
                wi, b = bank()
                tk = proj(b[0:m, 0:T], u, t_h, m)
                flush()
                tv = V.do(lambda e: e.tensor_copy(tmp[c0:c0 + n, :], b[c0:c0 + n, 0:T]), tk)
                w_read[wi] = tv
                wj, b2 = bank()
                PE.wait(tv)
                for t in range(2):
                    tk = tr(b2[:, 64 * t:64 * t + n], tmp[c0:c0 + n, t * P:(t + 1) * P], ident[c0:c0 + n, c0:c0 + n],
                            mark=(t == 1))
                w_read[wj] = V.do(lambda e: e.tensor_copy(dst, b2[:, 0:P].rearrange("p (t n) -> p t n", t=2)[:, :, 0:n]), tk)
                return w_read[wj]

            g_tok = {}
            g_rd = [None, None]

            def gate(bi, f):
                j, q = divmod(f, 2)
                wi, b = bank()
                tk = proj(b[:, 0:T], cunit(("w", l), W, 3528 + D * bi + 256 * j, q), t_h)
                flush()
                g = gates[bi % 2][:, f, :]
                g_tok[(bi, f)] = S.do(lambda e, b=b, g=g: e.activation(g, b[:, 0:T], ACT.Tanh, scale=0.5), tk, g_rd[bi % 2])
                w_read[wi] = g_tok[(bi, f)]
                return tk

            m_tok = [None] * KC
            SEG = ((0, 128), (128, 384))

            def ipiece():
                return ("wi", l), W[:, 3456:3528], KC, 72

            def cpiece():
                return ("wc", l), W[:, 2816:2944], KC, 128

            def bpiece():
                return ("wb", l), W[:, 2048:2304], KC, 256

            for f in range(4):
                feat_chunk(2944, f, qB, "qi", 1.0)
            dup(ipiece(), 0, kB[:, 0, :], "ki", False)
            t_wi = few(ipiece(), 72, 64, 8, pt[:, 0, 0:T], wi_[:, :, :])
            for f in range(4):
                feat_chunk(2304, f, qA, "qc", 0.125)
            srd = [None] * 4
            tacc = None

            def index_head(h):
                nonlocal tacc
                p = 64 * (h % 2)
                wi, b = bank()
                PE.wait(tok_of["qi"], tok_of["ki"])
                q = qB[p:p + 64, h // 2, :]
                k = kB[p:p + 64, 0, :]
                mm(b[:, 0:128], q[:, 0:128], k[:, 0:128], True, True)
                tk = mm(b[:, 128:384], q[:, 128:256], k[:, 0:256], True, True, mark=True)
                r = h % 2
                ts = S.do(lambda e, b=b, r=r: e.activation(sm[:, r, :], b[:, 0:384], ACT.Relu), tk, srd[r])
                w_read[wi] = ts
                for t, (a, z) in enumerate(SEG):
                    if h == 0:
                        tv = V.do(lambda e, t=t, a=a, z=z, r=r: e.tensor_scalar(
                            isc[:, a:z], sm[:, r, a:z], wi_[:, t, h:h + 1], None, ALU.mult), ts, t_wi)
                    else:
                        tv = V.do(lambda e, t=t, a=a, z=z, r=r: e.scalar_tensor_tensor(
                            isc[:, a:z], sm[:, r, a:z], wi_[:, t, h:h + 1], isc[:, a:z], ALU.mult, ALU.add), ts, tacc)
                tacc = tv
                srd[r] = tv
                return tk

            flush()
            for h in range(8):
                t_idx = index_head(h)
            dup(cpiece(), 0, kA[:, 0, :], "kc", False)
            t_vc = few(cpiece(), P, 64, 64, pt[:, 1, 0:T], vc[:, :, :])
            flush()

            tv = V.do(lambda e: e.tensor_tensor(isc, isc, const[:, C_MC:C_MC + 384], ALU.add), tacc)
            top = small[:, 128:144].rearrange("p (t k) -> p t k", t=2)
            last = [tv, tv]

            def top_round():
                for t, (a, z) in enumerate(SEG):
                    last[t] = V.do(lambda e, t=t, a=a, z=z: e.max(top[:, t, :], isc[:, a:z]), last[t])
                for t, (a, z) in enumerate(SEG):
                    last[t] = V.do(lambda e, t=t, a=a, z=z: e.match_replace(isc[:, a:z], top[:, t, :], isc[:, a:z], GONE),
                                   last[t])

            for f in range(8):
                gate(2, f)
                top_round()
            tv = V.do(lambda e: e.tensor_scalar(maskc, isc, -2e38, NEG, ALU.is_gt, ALU.mult), last[1])
            t_mc = V.do(lambda e: e.tensor_tensor(maskc, maskc, const[:, C_MC:C_MC + 384], ALU.add), tv)

            pt_rd = [None] * 2
            o_rd = [None] * 4

            def heads(qq, kk, mask, t_mask, vsl, t_v, t_qk, fill, sinks=None):
                t_o, state, points = [], {}, [12]

                def filler():
                    for _ in range(max(-(-len(fill) // points[0]), 2 if points[0] == 12 else 0)):
                        fill.pop(0)()
                    points[0] -= 1

                def scores(j):
                    if any(key in t_qk for key, _ in pend):
                        flush()
                    u = j % 2
                    tkk, banks = [], []
                    for q in range(2):
                        p = 64 * q
                        wi, b = bank()
                        PE.wait(*[tok_of[key] for key in t_qk])
                        a_, b_ = qq[p:p + 64, j, :], kk(j)[p:p + 64, :]
                        mm(b[:, 0:128], a_[:, 0:128], b_[:, 0:128], True, True)
                        tkk.append(mm(b[:, 128:384], a_[:, 128:256], b_[:, 0:256], True, True, mark=True))
                        banks.append((wi, b))
                    flush()
                    top_up()
                    state[j] = tkk, banks

                def softmax(j):
                    u = j % 2
                    tkk, banks = state[j]
                    mx, dn = stt[:, u, 0, :], stt[:, u, 1, :]
                    for q in range(2):
                        wi, b = banks[q]
                        for t, (a, z) in enumerate(SEG):
                            tv = V.do(lambda e, a=a, z=z, r=2 * u + q, i=2 * q + t, b=b: e.tensor_tensor_reduce(
                                sm[:, r, a:z], b[:, a:z], mask[:, a:z], 1.0, GONE, ALU.add, ALU.max,
                                mx[:, i:i + 1]), tkk[q], t_mask, srd[2 * u + q])
                        w_read[wi] = tv
                    nmx = small[:, 160 + 4 * u:164 + 4 * u]
                    if sinks is not None:
                        sk = sinks(j)
                        tv = V.do(lambda e: e.tensor_tensor(mx, mx, sk, ALU.max), tv, t_sink)
                    tv = V.do(lambda e: e.tensor_scalar(nmx, mx, -1.0, None, ALU.mult), tv)
                    for q in range(2):
                        for t, (a, z) in enumerate(SEG):
                            ts = S.do(lambda e, a=a, z=z, r=2 * u + q, i=2 * q + t: e.activation(
                                sm[:, r, a:z], sm[:, r, a:z], ACT.Exp, bias=nmx[:, i:i + 1], accum_out=dn[:, i:i + 1]), tv)
                    if sinks is not None:
                        t4 = small[:, 176 + 4 * u:180 + 4 * u]
                        tv = V.do(lambda e: e.tensor_tensor(t4, nmx, sk, ALU.add), tv)
                        te = S.do(lambda e: e.activation(t4, t4, ACT.Exp), tv)
                        ts = V.do(lambda e: e.tensor_tensor(dn, dn, t4, ALU.add), te, ts)
                    rd = small[:, 192 + 4 * u:196 + 4 * u]
                    tv = V.do(lambda e: e.reciprocal(rd, dn), ts)
                    tn = []
                    for q in range(2):
                        for t, (a, z) in enumerate(SEG):
                            tg = G.do(lambda e, a=a, z=z, r=2 * u + q, i=2 * q + t: e.tensor_scalar(
                                sm[:, r, a:z], sm[:, r, a:z], rd[:, i:i + 1], 0.5, ALU.mult, ALU.mult), tv)
                        tn.append(tg)
                    state[j] = tn

                def turned(j):
                    tn = state[j]
                    for q in range(2):
                        wi, b = bank()
                        PE.wait(tn[q])
                        r = 2 * (j % 2) + q
                        tr(b[:, 0:128], sm[:, r, 0:128], ident)
                        tr(b[:, 128:256], sm[:, r, 128:256], ident)
                        tk = tr(b[:, 256:384], sm[:, r, 256:384], ident, mark=True)
                        srd[r] = tk
                        tn[q] = S.do(lambda e, q=q, b=b: e.copy(pt[:, q, :], b[:, 0:384]), tk, pt_rd[q])
                        w_read[wi] = tn[q]
                    flush()

                def finish(j):
                    tn = state[j]
                    wo, bo = bank()
                    for q in range(2):
                        PE.wait(tn[q], t_v)
                        h = 2 * j + q
                        mm(bo[64 * q:64 * q + 64, 0:256], vsl(h, 0), pt[:, q, 0:256], True, False)
                        tk = mm(bo[64 * q:64 * q + 64, 128:256], vsl(h, 1), pt[:, q, 256:384], False, True, mark=True)
                        pt_rd[q] = tk
                    th = V.do(lambda e, j=j: e.tensor_copy(oh[:, j, :], bo[:, 0:256]), tk, o_rd[j])
                    tl = V.do(lambda e, j=j: e.tensor_tensor(ol[:, j, :], bo[:, 0:256], oh[:, j, :].bitcast(F32), ALU.subtract), th)
                    w_read[wo] = tl
                    t_o.append(tl)

                scores(0)
                softmax(0)
                for j in range(4):
                    filler()
                    if j < 3:
                        scores(j + 1)
                        if len(fill) > 1:
                            fill.pop(0)()
                        softmax(j + 1)
                    filler()
                    turned(j)
                    filler()
                    finish(j)
                flush()
                return t_o

            def branch(nm, bi, t_o):
                def two(nh, hf):
                    u = unit(("br", nm, l, nh), I[f"w_br_{nm}_2"][l, :, 512 * nh:512 * nh + 512], 4, 512,
                             lambda w: w[:, :, 256 * hf:256 * hf + 256], (4, 256), hf == 1)
                    wi, b = bank()
                    for c in range(2):
                        for k in range(4):
                            PE.wait(t_o[k])
                            for i, (a, z) in enumerate(((u[0], oh), (u[0], ol), (u[1], oh))):
                                tk = mm(b[:, T * c:T * c + T], a[:, k * 256 + c * P:k * 256 + c * P + P], z[:, k, :],
                                        k == 0 and i == 0, k == 3 and i == 2, mark=(k == 3 and i == 2))
                    done(u[2], tk)
                    flush()
                    for j in range(4):
                        o_rd[j] = tk
                    for c in range(2):
                        f = 4 * nh + 2 * hf + c
                        g = gates[bi % 2][:, f, :]
                        bb = b[:, T * c:T * c + T]
                        if m_tok[f] is None:
                            m_tok[f] = V.do(lambda e, g=g, f=f, bb=bb: e.scalar_tensor_tensor(mT[:, f, :], g, 1.0, bb, ALU.add, ALU.mult),
                                            tk, g_tok[(bi, f)], xa_tok[0])
                            g_rd[bi % 2] = m_tok[f]
                            w_read[wi] = m_tok[f]
                        else:
                            tv = V.do(lambda e, g=g, bb=bb: e.scalar_tensor_tensor(g, g, 1.0, bb, ALU.add, ALU.mult), tk, g_tok[(bi, f)])
                            w_read[wi] = tv
                            m_tok[f] = G.do(lambda e, g=g, f=f: e.tensor_tensor(mT[:, f, :], mT[:, f, :], g, ALU.add),
                                            tv, m_tok[f])
                            g_rd[bi % 2] = m_tok[f]
                return [lambda nh=nh, hf=hf: two(nh, hf) for nh in range(2) for hf in range(2)]

            def vbk():
                t_v["b"] = tokmajor(bpiece(), 128, 128, vb[:, :, :], True)
                flush()

            def vak(j):
                wi, b = bank()
                us = [unit(("wv", l, j), W[:, 1024 + 256 * j:1280 + 256 * j], KC, 256,
                           lambda w, hf=hf: w[:, 4 * hf:4 * hf + 4, :], (4, 256), hf == 1, AHEAD - hf, True)
                      for hf in range(2)]
                for t in range(2):
                    for kc in range(KC):
                        wh, wl, s_, tok = us[kc // 4]
                        k = kc % 4
                        PE.wait(t_h[kc], tok)
                        for i, (a, z) in enumerate(((hh, wh), (hl, wh), (hh, wl))):
                            tk = mm(b[:, t * T:t * T + T], a[:, kc, t * P:(t + 1) * P], z[:, k * T:k * T + T],
                                    kc == 0 and i == 0, kc == KC - 1 and i == 2, mark=(k == 3 and i == 2))
                        if t and k == 3:
                            done(s_, tk)
                flush()
                t_v["a"] = V.do(lambda e: e.tensor_copy(va[:, :, 256 * j:256 * j + 256],
                                                        b[:, :].rearrange("p (t n) -> p t n", t=2)), tk)
                w_read[wi] = t_v["a"]

            t_v = {}
            fill = [lambda f=f: feat_chunk(1536, f, qB, "qb", 0.125, t_idx) for f in range(4)]
            fill += [lambda: dup(bpiece(), 0, kB[:, 0, :], "kb0", False, t_idx),
                     lambda: dup(bpiece(), 64, kB[:, 1, :], "kb1", False), vbk]
            fill += [lambda f=f: gate(1, f) for f in range(8)]
            t_oc = heads(qA, lambda j: kA[:, 0, :], maskc, t_mc, lambda h, s_: vc[:, s_, :], t_vc,
                         ("qc", "kc"), fill)
            free_a = (PE.sem, PE.n)
            fill = branch("c", 2, t_oc)
            fill += [lambda f=f: feat_chunk(0, f, qA, "qa", 0.125, free_a) for f in range(4)]
            fill += [lambda f=f: feat_chunk(512, f, kA, "ka", 1.0, free_a) for f in range(4)]
            fill += [lambda: vak(0), lambda: (vak(1), flush())]
            fill += [lambda f=f: gate(0, f) for f in range(8)]
            sk = lambda j: sink[:, l, 2 * j:2 * j + 2, :].rearrange("p h t -> p (h t)")
            rest_b = fill[14:]
            t_ob = heads(qB, lambda j: kB[:, j // 2, :], const[:, C_MB:C_MB + 384], t_const,
                         lambda h, s_: vb[:, s_, 64 * (h // 4):64 * (h // 4) + 64], t_v["b"],
                         ("qb", "kb0", "kb1"), fill[:14], sk)
            t_oa = heads(qA, lambda j: kA[:, j, :], const[:, C_MA:C_MA + 384], t_const,
                         lambda h, s_: va[:, s_, 64 * h:64 * h + 64], t_v["a"],
                         ("qa", "ka"), branch("b", 1, t_ob) + rest_b)
            for f in branch("a", 0, t_oa):
                f()
            t_free = (PE.sem, PE.n)
            tz = [split(hh[:, f, :], hl[:, f, :], mT[:, f, :], m_tok[f], t_free) for f in range(KC)]
            return out_rows(("w_out", l), I["w_out_2"][l], tz)

        jobs.append(ada(0, 0))
        ada_steps(8)
        other_cols()
        tf = fold(None, None, 0, SCM, SHM, mod_done[(0, 0)])
        t_h = to_feature(xa, [t_x, t_x], tf, None)
        xa_tok[0] = S.do(lambda e: e.activation(xa[:, :, :], xa[:, :, :], ACT.Copy, scale=ALPHA), (PE.sem, PE.n))
        for l in range(DEPTH):
            load_ln(I["mix_ln_g"][l:l + 1, :], I["mix_ln_b"][l:l + 1, :])
            ty = mixer_a(t_h) if l == 0 else mixer_b(t_h)
            tg = spread(l, 0)
            tx, rest = layer_norm(ty, tg, False)
            if l == 0:
                jobs.append(ada(1, 0))
                ada_steps(5)
            tf = fold(colr("mix_ln_g", 8 * l, 8), colr("mix_ln_b", 8 * l, 8), l, SCF, SHF, *t_h)
            t_h = to_feature(vv, tx, tf, ty[1])
            ada_steps(8)
            load_ln(I["ffn_ln_g"][l:l + 1, :], I["ffn_ln_b"][l:l + 1, :])
            ty, tg = moe(l, t_h, tx, lambda: (rest(), spread(l, 1))[1])
            tx, rest = layer_norm(ty, tg, l == 1)
            g_, b_ = colr("ffn_ln_g", 8 * l, 8), colr("ffn_ln_b", 8 * l, 8)
            if l == 0:
                ada_inputs()
                jobs.extend([ada(1, 1), ada(1, 2)])
                ada_steps(5)
                tf = fold(g_, b_, 1, SCM, SHM, *t_h)
            else:
                tf = fold(g_, b_, None, None, None, *t_h)
            t_h = to_feature(vv, tx, tf, ty[1])
            ada_steps(3)
            rest()
        for l in range(DEPTH):
            for j in range(3):
                last = l == DEPTH - 1 and j == 2
                load_ln(I["ln_g_2"][l, j:j + 1, :], I["ln_b_2"][l, j:j + 1, :], last)
                if j == 0:
                    ty = ffn(("f1", l), I["ffn1_in_2"][l], I["ffn1_out_2"][l], t_h)
                elif j == 1:
                    ty = hybrid(l, t_h)
                else:
                    ty = ffn(("f2", l), I["ffn2_in_2"][l], I["ffn2_out_2"][l], t_h)
                tx, rest = layer_norm(ty, 1.0 if j == 1 else 0.5, not last)
                if not last:
                    i = 8 * (3 * l + j)
                    tf = fold(colr("ln_g_2", i, 8), colr("ln_b_2", i, 8), None, None, None, *t_h)
                    t_h = to_feature(vv, tx, tf, ty[1])
                rest(last)
        for t in range(2):
            t_out = SP.dma(out[0, t * P:(t + 1) * P, :], xa[:, t, :], s_o, xa_tok[0][t])
        SP.wait(t_out)
        return SP, PE, V, S, G


_INS = ["x", "c", "ada_w", "ada_b", "a_w_in", "a_b_in", "a_w_dw", "a_b_dw", "a_ln_g", "a_ln_b", "a_w_out", "a_b_out",
        "b_w_in", "b_w_dw", "b_w_out", "mix_ln_g", "mix_ln_b", "ffn_ln_g", "ffn_ln_b", "r_w_group", "r_b_group",
        "r_w_expert", "r_b_expert", "e_w_gate", "e_w_up", "e_w_down", "positions_2", "w_in_2", "sink_b_2", "w_br_a_2",
        "w_br_b_2", "w_br_c_2", "w_out_2", "ffn1_in_2", "ffn1_out_2", "ffn2_in_2", "ffn2_out_2", "ln_g_2", "ln_b_2"]


def kernel(**inputs):
    import numpy as _np
    import concourse.bacc as _bacc
    from concourse import mybir as _mybir
    from concourse.bass_utils import run_bass_kernel_spmd as _run

    nc = _bacc.Bacc("TRN2", target_bir_lowering=False, num_devices=1)
    arrays, aps = {}, {}
    for name in _INS:
        a = _np.ascontiguousarray(inputs[name])
        arrays[f"in_{name}_dram"] = a
        aps[name] = nc.dram_tensor(f"in_{name}_dram", a.shape, _mybir.dt.from_np(a.dtype), kind="ExternalInput").ap()
    c = constants()
    arrays["in_consts_dram"] = c
    aps["consts"] = nc.dram_tensor("in_consts_dram", c.shape, _mybir.dt.float32, kind="ExternalInput").ap()
    o = nc.dram_tensor("out_0_dram", (1, T, D), _mybir.dt.float32, kind="ExternalOutput").ap()
    program(nc, aps, o)
    r = _run(nc, [arrays], core_ids=[0])
    return r.results[0]["out_0_dram"]
```
